# Optimizing a Trainium2 kernel written in Bass

```python
import jax, jax.numpy as jnp
from jax import lax
import numpy as np
import math

D_MODEL = 1024
BATCH = 1
SEQ = 512
DEPTH = 1

HEAD_DIM = 64
N_HEADS = D_MODEL // HEAD_DIM
N_HEADS_A = N_HEADS // 2
N_HEADS_B = N_HEADS - N_HEADS_A
DILATED_CONFIGS = ((128, 1), (512, 4), (2048, 16))
BLOCK = 128
KV_RANK = D_MODEL // 8
IDX_HEADS = 8
IDX_DIM = 64
IDX_SCALE = (IDX_HEADS * IDX_DIM) ** -0.5
TOPK_MAX = 256
D_FF = -(-8 * D_MODEL // (3 * 256)) * 256
EPS = 1e-6
SPLITS = (N_HEADS_A * HEAD_DIM, N_HEADS_A * HEAD_DIM, N_HEADS_A * HEAD_DIM,
          N_HEADS_B * HEAD_DIM, KV_RANK,
          IDX_HEADS * IDX_DIM, IDX_DIM, IDX_HEADS)
D_IN = sum(SPLITS)


def rmsnorm(x, g):
    xf = x.astype(jnp.float32)
    y = xf * lax.rsqrt(jnp.mean(xf * xf, axis=-1, keepdims=True) + EPS)
    return (y * g.astype(jnp.float32)).astype(x.dtype)

def alibi_slopes():
    s = 2.0 ** (-8.0 * (np.arange(N_HEADS, dtype=np.float32) + 1.0) / N_HEADS)
    return jnp.asarray(s[0::2], jnp.float32), jnp.asarray(s[1::2], jnp.float32)

def dilated_branch(q, k, v, window, dilation, slopes):
    bsz, seq, nh, hd = q.shape
    n = seq // dilation
    nb = -(-n // BLOCK)
    n_pad = nb * BLOCK
    w_res = window // dilation
    assert w_res <= BLOCK
    g = bsz * dilation

    def to_res(a):
        a = a.reshape(bsz, n, dilation, nh, hd).transpose(0, 2, 3, 1, 4).reshape(g, nh, n, hd)
        return jnp.pad(a, ((0, 0), (0, 0), (0, n_pad - n), (0, 0)))

    qr, kr, vr = to_res(q), to_res(k), to_res(v)

    def band(a):
        cur = a.reshape(g, nh, nb, BLOCK, hd)
        prev = jnp.pad(a, ((0, 0), (0, 0), (BLOCK, 0), (0, 0)))[:, :, :n_pad].reshape(g, nh, nb, BLOCK, hd)
        return jnp.concatenate([prev, cur], axis=3)

    kb, vb = band(kr), band(vr)
    qb = qr.reshape(g, nh, nb, BLOCK, hd)
    s = jnp.einsum('ghnqd,ghnkd->ghnqk', qb, kb).astype(jnp.float32) * (hd ** -0.5)
    dist = np.arange(BLOCK)[:, None] - np.arange(2 * BLOCK)[None, :] + BLOCK
    key_pos = np.arange(nb)[:, None] * BLOCK - BLOCK + np.arange(2 * BLOCK)[None, :]
    mask = ((dist >= 0) & (dist <= w_res))[None] & (key_pos >= 0)[:, None, :]
    bias = -slopes[:, None, None] * jnp.asarray(dist * dilation, jnp.float32)[None]
    s = jnp.where(mask[None, None], s + bias[None, :, None], -jnp.inf)
    m = jnp.max(s, axis=-1, keepdims=True)
    p = jnp.exp(s - m)
    l = jnp.sum(p, axis=-1, keepdims=True)
    o = jnp.einsum('ghnqk,ghnkd->ghnqd', (p / l).astype(v.dtype), vb)
    lse = (m + jnp.log(l))[..., 0]
    o = o.reshape(g, nh, n_pad, hd)[:, :, :n].reshape(bsz, dilation, nh, n, hd)
    o = o.transpose(0, 3, 1, 2, 4).reshape(bsz, seq, nh, hd)
    lse = lse.reshape(g, nh, n_pad)[:, :, :n].reshape(bsz, dilation, nh, n)
    lse = lse.transpose(0, 3, 1, 2).reshape(bsz, seq, nh)
    return o, lse

def dilated_mixture(q, k, v, slopes):
    outs, lses = [], []
    for window, dilation in DILATED_CONFIGS:
        o, lse = dilated_branch(q, k, v, window, dilation, slopes)
        outs.append(o.astype(jnp.float32))
        lses.append(lse)
    alpha = jax.nn.softmax(jnp.stack(lses, 0), axis=0)
    out = jnp.sum(alpha[..., None] * jnp.stack(outs, 0), axis=0)
    return out.astype(q.dtype)

def sparse_attention(q_idx, k_idx, w_idx, q_lat, c_kv, slopes):
    bsz, seq = c_kv.shape[0], c_kv.shape[1]
    nb = seq // BLOCK
    topk = min(TOPK_MAX, seq // 4)
    s_pos = jnp.arange(seq)
    k_idx_f = k_idx.astype(jnp.float32)

    def block_fn(i):
        start = i * BLOCK
        qi = lax.dynamic_slice_in_dim(q_idx, start, BLOCK, axis=1).astype(jnp.float32)
        wi = lax.dynamic_slice_in_dim(w_idx, start, BLOCK, axis=1).astype(jnp.float32)
        ql = lax.dynamic_slice_in_dim(q_lat, start, BLOCK, axis=1)
        t_pos = start + jnp.arange(BLOCK)
        logits = jnp.einsum('bqhd,bkd->bqhk', qi, k_idx_f)
        score = jnp.einsum('bqh,bqhk->bqk', wi, jax.nn.relu(logits))
        score = jnp.where(s_pos[None, None, :] <= t_pos[None, :, None], score, -jnp.inf)
        _, idx = lax.top_k(score, topk)
        c_sel = jax.vmap(lambda cb, ib: cb[ib])(c_kv, idx)
        s = jnp.einsum('bqhr,bqkr->bhqk', ql, c_sel).astype(jnp.float32) * (HEAD_DIM ** -0.5)
        dist = (t_pos[None, :, None] - idx).astype(jnp.float32)
        s = s - slopes[None, :, None, None] * dist[:, None]
        s = jnp.where((idx <= t_pos[None, :, None])[:, None], s, -jnp.inf)
        p = jax.nn.softmax(s, axis=-1)
        return jnp.einsum('bhqk,bqkr->bqhr', p.astype(c_sel.dtype), c_sel)

    o = lax.map(block_fn, jnp.arange(nb))
    return o.transpose(1, 0, 2, 3, 4).reshape(bsz, seq, o.shape[3], o.shape[4])

def first_inputs(seed: int = 0) -> dict:
    key = jax.random.key(seed)
    ks = jax.random.split(key, 16)
    f32 = jnp.float32
    nrm = lambda k, shape, scale: jax.random.normal(k, shape, f32) * scale
    return {
        "x": nrm(ks[0], (BATCH, SEQ, D_MODEL), 1.0),
        "c": nrm(ks[1], (BATCH, D_MODEL), 1.0),
        "w_ada": nrm(ks[2], (DEPTH, D_MODEL, 6 * D_MODEL), 0.5 * D_MODEL ** -0.5),
        "b_ada": nrm(ks[3], (DEPTH, 6 * D_MODEL), 0.01),
        "g_attn": 1.0 + nrm(ks[4], (DEPTH, D_MODEL), 0.02),
        "w_in": nrm(ks[5], (DEPTH, D_MODEL, D_IN), D_MODEL ** -0.5),
        "kv_norm_g": 1.0 + nrm(ks[6], (DEPTH, KV_RANK), 0.02),
        "w_uk": nrm(ks[7], (DEPTH, N_HEADS_B, HEAD_DIM, KV_RANK), HEAD_DIM ** -0.5),
        "w_uv": nrm(ks[8], (DEPTH, N_HEADS_B, KV_RANK, HEAD_DIM), KV_RANK ** -0.5),
        "w_out": nrm(ks[9], (DEPTH, D_MODEL, D_MODEL), D_MODEL ** -0.5),
        "g_ffn": 1.0 + nrm(ks[10], (DEPTH, D_MODEL), 0.02),
        "w_gu": nrm(ks[11], (DEPTH, D_MODEL, 2 * D_FF), D_MODEL ** -0.5),
        "w_down": nrm(ks[12], (DEPTH, D_FF, D_MODEL), D_FF ** -0.5),
        "g_final": 1.0 + nrm(ks[13], (D_MODEL,), 0.02),
    }

def first_block(x, c, w_ada, b_ada, g_attn, w_in, kv_norm_g, w_uk, w_uv, w_out, g_ffn, w_gu, w_down, g_final):
    bsz, seq, _ = x.shape
    slopes_a, slopes_b = alibi_slopes()
    offsets = [int(o) for o in np.cumsum(SPLITS)[:-1]]
    c_act = jax.nn.silu(c)
    for l in range(DEPTH):
        mod = c_act @ w_ada[l] + b_ada[l]
        sh1, sc1, ga1, sh2, sc2, ga2 = [m[:, None, :] for m in jnp.split(mod, 6, axis=-1)]

        h = rmsnorm(x, g_attn[l]) * (1.0 + sc1) + sh1
        proj = h @ w_in[l]
        qa, ka, va, qb, ckv, qi, ki, wi = jnp.split(proj, offsets, axis=-1)
        shp_a = (bsz, seq, N_HEADS_A, HEAD_DIM)
        out_a = dilated_mixture(qa.reshape(shp_a), ka.reshape(shp_a), va.reshape(shp_a), slopes_a)
        ckv = rmsnorm(ckv, kv_norm_g[l])
        q_lat = jnp.einsum('bthd,hdr->bthr', qb.reshape(bsz, seq, N_HEADS_B, HEAD_DIM), w_uk[l])
        o_lat = sparse_attention(qi.reshape(bsz, seq, IDX_HEADS, IDX_DIM), ki, wi * IDX_SCALE,
                                 q_lat, ckv, slopes_b)
        out_b = jnp.einsum('bthr,hrd->bthd', o_lat, w_uv[l])
        mixed = jnp.concatenate([out_a.reshape(bsz, seq, -1), out_b.reshape(bsz, seq, -1)], axis=-1)
        x = x + ga1 * (mixed @ w_out[l])

        h2 = rmsnorm(x, g_ffn[l]) * (1.0 + sc2) + sh2
        gate, up = jnp.split(h2 @ w_gu[l], 2, axis=-1)
        x = x + ga2 * ((jax.nn.silu(gate) * up) @ w_down[l])
    return rmsnorm(x, g_final)


D_MIX = 2 * D_MODEL
D_CONV = D_MIX // 2
D_LRU = D_MIX - D_CONV
CONV_GROUPS = 8
LRU_HEADS = 8
LRU_HEAD_DIM = D_LRU // LRU_HEADS
CONV_KERNEL = 31
SHORT_CONV = 4
LRU_C = 8.0
D_IN_2 = 3 * D_CONV + 2 * D_LRU


def rmsnorm_2(x, g):
    xf = x.astype(jnp.float32)
    y = xf * lax.rsqrt(jnp.mean(xf * xf, axis=-1, keepdims=True) + EPS)
    return (y * g.astype(jnp.float32)).astype(x.dtype)

def layernorm(x, g, b):
    xf = x.astype(jnp.float32)
    mu = jnp.mean(xf, axis=-1, keepdims=True)
    var = jnp.mean(jnp.square(xf - mu), axis=-1, keepdims=True)
    y = (xf - mu) * lax.rsqrt(var + EPS)
    return (y * g.astype(jnp.float32) + b.astype(jnp.float32)).astype(x.dtype)

def causal_depthwise_conv(v, w, b):
    k, ch = w.shape
    y = lax.conv_general_dilated(
        v, w.astype(v.dtype)[:, None, :], window_strides=(1,),
        padding=[(k - 1, 0)], dimension_numbers=("NWC", "WIO", "NWC"),
        feature_group_count=ch)
    return y + b.astype(v.dtype)

def linear_scan(a, bx):
    def step(h, inp):
        a_t, b_t = inp
        h = a_t * h + b_t
        return h, h
    h0 = jnp.zeros((a.shape[0], a.shape[2]), jnp.float32)
    _, hs = lax.scan(step, h0, (jnp.swapaxes(a, 0, 1), jnp.swapaxes(bx, 0, 1)))
    return jnp.swapaxes(hs, 0, 1)

def second_inputs(seed: int = 0) -> dict:
    key = jax.random.key(seed)
    ks = jax.random.split(key, 24)
    f32 = jnp.float32
    nrm = lambda k, s, sc: (jax.random.normal(k, s, f32) * sc)
    x = jax.random.normal(ks[0], (BATCH, SEQ, D_MODEL), f32)
    c = jax.random.normal(ks[1], (BATCH, D_MODEL), f32)
    norm_g = 1.0 + nrm(ks[2], (DEPTH, D_MODEL), 0.05)
    mod_w = nrm(ks[3], (DEPTH, D_MODEL, 3 * D_MODEL), 0.5 * D_MODEL ** -0.5)
    mod_b = nrm(ks[4], (DEPTH, 3 * D_MODEL), 0.02)
    w_in = nrm(ks[5], (DEPTH, D_MODEL, D_IN_2), D_MODEL ** -0.5)
    dw_w = nrm(ks[6], (DEPTH, CONV_KERNEL, D_CONV), CONV_KERNEL ** -0.5)
    dw_b = nrm(ks[7], (DEPTH, D_CONV), 0.02)
    cln_g = 1.0 + nrm(ks[8], (DEPTH, D_CONV), 0.05)
    cln_b = nrm(ks[9], (DEPTH, D_CONV), 0.02)
    pw2_w = nrm(ks[10], (DEPTH, D_CONV, D_CONV), D_CONV ** -0.5)
    pw2_b = nrm(ks[11], (DEPTH, D_CONV), 0.02)
    sc_w = nrm(ks[12], (DEPTH, SHORT_CONV, D_LRU), SHORT_CONV ** -0.5)
    sc_b = nrm(ks[13], (DEPTH, D_LRU), 0.02)
    wr = nrm(ks[14], (DEPTH, LRU_HEADS, LRU_HEAD_DIM, LRU_HEAD_DIM), LRU_HEAD_DIM ** -0.5)
    br = nrm(ks[15], (DEPTH, D_LRU), 0.02)
    wi = nrm(ks[16], (DEPTH, LRU_HEADS, LRU_HEAD_DIM, LRU_HEAD_DIM), LRU_HEAD_DIM ** -0.5)
    bi = nrm(ks[17], (DEPTH, D_LRU), 0.02)
    a0 = jax.random.uniform(ks[18], (DEPTH, D_LRU), f32, 0.9, 0.999)
    s = a0 ** (1.0 / LRU_C)
    lam = jnp.log(s) - jnp.log1p(-s)
    w_out = nrm(ks[19], (DEPTH, D_MIX, D_MODEL), D_MIX ** -0.5)
    final_g = 1.0 + nrm(ks[20], (D_MODEL,), 0.05)
    return {"x": x, "c": c, "norm_g": norm_g, "mod_w": mod_w, "mod_b": mod_b,
            "w_in": w_in, "dw_w": dw_w, "dw_b": dw_b, "cln_g": cln_g, "cln_b": cln_b,
            "pw2_w": pw2_w, "pw2_b": pw2_b, "sc_w": sc_w, "sc_b": sc_b,
            "wr": wr, "br": br, "wi": wi, "bi": bi, "lam": lam,
            "w_out": w_out, "final_g": final_g}

def second_block(x, c, norm_g, mod_w, mod_b, w_in, dw_w, dw_b, cln_g, cln_b,
              pw2_w, pw2_b, sc_w, sc_b, wr, br, wi, bi, lam, w_out, final_g):
    bsz, seq, _ = x.shape
    c_act = jax.nn.silu(c)
    for l in range(DEPTH):
        mod = c_act @ mod_w[l] + mod_b[l]
        shift, scale, gate = jnp.split(mod, 3, axis=-1)
        h = rmsnorm_2(x, norm_g[l]) * (1.0 + scale[:, None, :]) + shift[:, None, :]

        u = h @ w_in[l]
        cv, cg, cs, lx, ls = jnp.split(
            u, [D_CONV, 2 * D_CONV, 3 * D_CONV, 3 * D_CONV + D_LRU], axis=-1)

        v = cv * jax.nn.sigmoid(cg)
        v = causal_depthwise_conv(v, dw_w[l], dw_b[l])
        v = jax.nn.silu(layernorm(v, cln_g[l], cln_b[l]))
        v = v @ pw2_w[l] + pw2_b[l]
        y_conv = v * jax.nn.silu(cs)

        xs = causal_depthwise_conv(lx, sc_w[l], sc_b[l])
        xh = xs.reshape(bsz, seq, LRU_HEADS, LRU_HEAD_DIM)
        r = jax.nn.sigmoid(jnp.einsum("bshd,hde->bshe", xh, wr[l]).reshape(bsz, seq, D_LRU) + br[l])
        i = jax.nn.sigmoid(jnp.einsum("bshd,hde->bshe", xh, wi[l]).reshape(bsz, seq, D_LRU) + bi[l])
        log_a = (-LRU_C * r.astype(jnp.float32)
                 * jax.nn.softplus(-lam[l].astype(jnp.float32)))
        a = jnp.exp(log_a)
        mult = jnp.sqrt(-jnp.expm1(2.0 * log_a))
        bx = mult * (i * xs).astype(jnp.float32)
        hs = linear_scan(a, bx).astype(x.dtype)
        y_lru = hs * jax.nn.silu(ls)

        y = jnp.concatenate([y_conv, y_lru], axis=-1) @ w_out[l]
        x = x + (1.0 + gate[:, None, :]) * y
    return rmsnorm_2(x, final_g)


def setup_inputs(seed=0):
    out = dict(first_inputs(seed))
    for name, value in second_inputs(seed + 1).items():
        if name != "x":
            out[name + "_2"] = value
    return out


def reference(
    x, c, w_ada, b_ada, g_attn, w_in, kv_norm_g, w_uk, w_uv, w_out, g_ffn, w_gu, w_down,
    g_final, c_2, norm_g_2, mod_w_2, mod_b_2, w_in_2, dw_w_2, dw_b_2, cln_g_2, cln_b_2, pw2_w_2,
    pw2_b_2, sc_w_2, sc_b_2, wr_2, br_2, wi_2, bi_2, lam_2, w_out_2, final_g_2,
):
    x = first_block(
        x, c, w_ada, b_ada, g_attn, w_in, kv_norm_g, w_uk, w_uv, w_out, g_ffn, w_gu, w_down,
        g_final,
    )
    return second_block(
        x, c_2, norm_g_2, mod_w_2, mod_b_2, w_in_2, dw_w_2, dw_b_2, cln_g_2, cln_b_2, pw2_w_2,
        pw2_b_2, sc_w_2, sc_b_2, wr_2, br_2, wi_2, bi_2, lam_2, w_out_2, final_g_2,
    )


_drawn_inputs = setup_inputs


def setup_inputs(seed=0):
    import zlib

    import numpy as np

    out = dict(_drawn_inputs(seed))
    spreads = {}
    factors = {'b_ada': 3.321,
     'g_attn': 3.475,
     'kv_norm_g': 8.0,
     'g_ffn': 8.0,
     'dw_b_2': 6.475,
     'cln_g_2': 3.789,
     'cln_b_2': 8.0,
     'pw2_b_2': 7.011,
     'br_2': 46.048,
     'bi_2': 8.0}
    for name, (base, spread) in spreads.items():
        noise = np.random.default_rng([zlib.crc32(name.encode()), seed]).standard_normal(out[name].shape)
        drawn = base * np.exp(spread * noise) if base else spread * noise
        out[name] = __import__('jax').numpy.asarray(drawn.astype(out[name].dtype))
    for name, factor in factors.items():
        out[name] = (out[name] * factor).astype(out[name].dtype)
    return out
```

```python
from contextlib import ExitStack

import concourse.bass as bass
from concourse import mybir

F32 = mybir.dt.float32
F32R = mybir.dt.float32r
ALU = mybir.AluOpType
ACT = mybir.ActivationFunctionType

P = 128
T = 512
TT = T // P
D = 1024
KD = D // P
D_FF = 2816
KF = D_FF // P
HD = 64
NH = 8
TOPK = 128
EPS = 1e-6
BIG = 1.0e30
NCOL = 256
CONV = 31
SHORT = 4
PADV, PADL = CONV - 1, SHORT - 1
QSCALE = -(HD ** -0.5)
IDX_SCALE = (8 * 64) ** -0.5

W_IN_COLS = [2048, 2304, 2560, 1536, 1792, 0, 256, 512, 768, 1024, 1280]
N_IN = len(W_IN_COLS)
C_OUT = N_IN
C_GU = C_OUT + 4
C_DOWN = C_GU + 2 * (D_FF // NCOL)
C_IN2 = C_DOWN + 12
C_LRU = C_IN2 + 20
C_PW2 = C_LRU + 4
C_OUT2 = C_PW2 + 4
C_END = C_OUT2 + 4

ADA1, ADA2 = 24, 12
ADA_FIRST = 8
ADA_WINDOW = {0: 3, 1: 3, 2: 3, 3: 3, 4: 3, 5: 2}
ADA_LOOP = ADA_FIRST + sum(ADA_WINDOW.values())

ITEMS = [(kind, h, i) for kind in "AB" for h in range(NH) for i in range(TT)]
PAIRS = [(i, h) for i in range(1, TT) for h in range(NH)]
PAIRS_PER_TILE = 4

ADA_PE = list(range(0, ADA_FIRST, 2))
ADA_ORD = {c: n for n, c in enumerate(c for c in range(ADA1 + ADA2) if c not in ADA_PE)}
ADA_DVE = ADA_ORD[ADA_LOOP]

VECS = [("b_ada", 48), ("mod_b_2", 24), ("g_attn", 8), ("g_ffn", 8), ("g_final", 8), ("norm_g_2", 8),
        ("final_g_2", 8), ("cln_g_2", 8), ("cln_b_2", 8), ("pw2_b_2", 8), ("sc_b_2", 8), ("dw_b_2", 8),
        ("br_2", 8), ("bi_2", 8), ("lam_2", 8), ("sc_w_2", 32), ("pad", 48), ("dw_w_2", 248)]
VROW = {}
_at = 0
for _name, _n in VECS:
    VROW[_name] = _at
    _at += _n
NVEC_DMAS = len(VECS) - 1 + 1


def build(nc, a, out):
    with ExitStack() as ctx:
        offset = [nc.sbuf_base + (-nc.sbuf_base) % 64]

        def fixed(name, shape, dt=F32, at=None):
            n = 4
            for s in shape[1:]:
                n *= s
            if at is None:
                at = offset[0]
                offset[0] += (n + 63) // 64 * 64
                assert offset[0] <= nc.sbuf_usable_end, (name, offset[0])
            return nc.alloc_sbuf_tensor_at(name, shape, dt, offset=at), at

        def sem(name):
            return ctx.enter_context(nc.semaphore(name))

        xT, _ = fixed("xT", [P, KD, T])
        act_hi, at_hi = fixed("act_hi", [P, KD, T], F32R)
        act_lo, at_lo = fixed("act_lo", [P, KD, T], F32R)
        w_stage = [fixed(f"w_stage{b}", [P, KD, NCOL])[0] for b in range(2)]
        w_hi = [fixed(f"w_hi{b}", [P, KD, NCOL], F32R)[0] for b in range(2)]
        w_lo = [fixed(f"w_lo{b}", [P, KD, NCOL], F32R)[0] for b in range(2)]
        tmp = [fixed(f"tmp{b}", [P, T])[0] for b in range(4)]
        rstd, _ = fixed("rstd", [P, T])
        ident, _ = fixed("ident_sb", [P, P])
        ones, _ = fixed("ones", [P, P])
        vcol, _ = fixed("vcol", [P, 512])
        mod, _ = fixed("mod", [P, 72])
        scale1, _ = fixed("scale1", [P, 4, KD])
        c_sb, _ = fixed("c_sb", [P, 2, KD])
        c_act, _ = fixed("c_act", [P, 2, KD])
        eps, _ = fixed("eps", [P, 1])
        lam_t, _ = fixed("lam_t", [P, 8, KD])
        wi_sb, _ = fixed("wi_sb", [P, TT, 8])
        negmax, _ = fixed("negmax", [P, 64])
        expsum, _ = fixed("expsum", [P, 64])
        expinv, _ = fixed("expinv", [P, 64])
        ckv_ss, _ = fixed("ckv_ss", [P, 3, TT])
        region = offset[0]

        dist, _ = fixed("dist_sb", [P, T])
        maskA, _ = fixed("maskA_sb", [P, T])
        causal, _ = fixed("causal_sb", [P, 2, P])
        ada_stage = [fixed(f"ada_stage{b}", [P, KD, NCOL])[0] for b in range(2)]
        ada_acc = [fixed(f"ada_acc{b}", [P, 2, NCOL])[0] for b in range(2)]
        qaT, at_qa = fixed("qaT", [P, 4, T])
        kaT, at_ka = fixed("kaT", [P, 4, T])
        va, _ = fixed("va", [P, TT, T])
        qbT, _ = fixed("qbT", [P, 4, T])
        x_nat, _ = fixed("x_nat", [P, TT, D], at=at_qa)
        at_score = offset[0]
        score = [None] + [fixed(f"score{i}", [P, P * (i + 1)])[0] for i in range(1, TT)]
        work = [None] + [fixed(f"work{i}", [P, P * (i + 1)])[0] for i in range(1, TT)]
        probs = tmp[2:4] + [fixed(f"probs{b}", [P, T], at=at_score + 2048 * b)[0] for b in range(2)]
        top8 = [None] + [fixed(f"top8_{i}", [P, 8])[0] for i in range(1, TT)]
        qiT, at_qi = fixed("qiT", [P, 4, T])
        qlatT = [fixed(f"qlatT{b}", [P, T], at=at_qi + 2048 * b)[0] for b in range(2)]
        olat = [fixed(f"olat{b}", [P, T], at=at_qi + 2048 * (2 + b))[0] for b in range(2)]
        kiT, at_ki = fixed("kiT", [P, T])
        ckv, at_ckv = fixed("ckv", [P, TT, P])
        ckvT, _ = fixed("ckvT", [P, T])
        wuk, _ = fixed("wuk", [P, 4, P])
        wuv, at_wuv = fixed("wuv", [P, NH, HD])
        probsT = [fixed(f"probsT{b}", [P, TT, P])[0] for b in range(2)]
        probsT.append(fixed("probsT2", [P, TT, P], at=at_ki)[0])
        comb, at_comb = zip(*[fixed(f"comb{b}", [P, T]) for b in range(2)])
        relu = [fixed(f"relu{b}", [P, T], at=at_comb[b])[0] for b in range(2)]
        table = [fixed(f"table{b}", [P, T])[0] for b in range(2)]
        kvg, _ = fixed("kvg", [P, P])
        wiT, _ = fixed("wiT", [P, T], at=at_comb[0])
        vrow, _ = fixed("vrow", [P, 4, P], at=at_wuv)
        first_end = offset[0]

        offset[0] = region
        ff_hi, _ = fixed("ff_hi", [P, KF, T], F32R)
        ff_lo, _ = fixed("ff_lo", [P, KF, T], F32R)
        ada2_stage, _ = fixed("ada2_stage", [P, KD, NCOL])
        ada2_acc, _ = fixed("ada2_acc", [P, NCOL])

        offset[0] = region
        v_pad, at_v = fixed("v_pad", [P, KD, PADV + T])
        l_pad, at_l = fixed("l_pad", [P, KD, PADL + T])
        conv, at_conv = fixed("conv", [P, KD, T])
        lgate, at_lgate = fixed("lgate", [P, KD, T])
        cgate, _ = fixed("cgate", [P, KD, T])
        wr, _ = fixed("wr_sb", [P, 8, P])
        wi, _ = fixed("wi2_sb", [P, 8, P])
        decay, _ = fixed("decay", [P, KD, T], at=at_hi)
        gated, _ = fixed("gated", [P, KD, T], at=at_lo)
        ln_hi, _ = fixed("ln_hi", [P, KD, T], F32R, at=at_v)
        ln_lo, _ = fixed("ln_lo", [P, KD, T], F32R, at=at_l)
        yc_hi, _ = fixed("yc_hi", [P, KD, T], F32R, at=at_conv)
        yc_lo, _ = fixed("yc_lo", [P, KD, T], F32R, at=at_lgate)
        o_nat, _ = fixed("o_nat", [P, TT, D], at=at_v)

        bank = [ctx.enter_context(nc.psum_tensor(f"bank{b}", [P, 512], F32)) for b in range(8)]

        def col(name, j):
            c = VROW[name] + j
            return vcol[:, c:c + 1]

        def modc(j):
            return mod[:, j:j + 1]

        SH1, SC1, GA1, SH2, SC2, GA2, SH3, SC3, GA3 = (KD * j for j in range(9))

        s_c = sem("c_loaded")
        s_ident = sem("ident_loaded")
        s_const = sem("constants_loaded")
        s_vec = sem("vector_rows_loaded")
        s_x = sem("x_loaded")
        s_late = sem("head_weights_loaded")
        s_lruw = sem("lru_weights_loaded")
        s_stage = [sem(f"w_stage_loaded{b}") for b in range(2)]
        s_hi = sem("w_hi_ready")
        s_lo = sem("w_lo_ready")
        s_wused = sem("w_used")
        s_ada = [sem(f"ada_loaded{b}") for b in range(2)]
        s_adadir = sem("ada_chunk_by_pe")
        s_adaloop = sem("ada_loop_loaded")
        s_adastep = sem("ada_step")
        s_adaacc = sem("ada_acc_ready")
        s_adamm = sem("ada_acc_used")
        s_mod = sem("mod_ready")
        s_set = sem("dve_set")
        s_cact = sem("c_act_ready")
        s_vt = sem("vectors_turned")
        s_vcol = sem("vcol_ready")
        s_xt = sem("x_turned")
        s_xTr = sem("xT_ready")
        s_sq = sem("squares_ready")
        s_sqused = sem("squares_used")
        s_ss = sem("sum_of_squares")
        s_sd = sem("deviation_ready")
        s_rstd = sem("rstd_ready")
        s_u = sem("scaled_ready")
        s_ahi = sem("act_hi_ready")
        s_alo = sem("act_lo_ready")
        s_acc = sem("in_acc_ready")
        s_free = sem("in_acc_free")
        s_ckv = sem("ckv_steps")
        s_ckvsd = sem("ckv_deviation")
        s_ckvt = sem("ckv_turned")
        s_ckvT = sem("ckvT_ready")
        s_wiT = sem("indexer_weights_turned")
        s_wi = sem("indexer_weights_ready")
        s_lg = sem("logits_ready")
        s_relu = sem("relu_ready")
        s_score = sem("score_added")
        s_top = sem("topk_step")
        s_tab = sem("table_ready")
        s_tabm = sem("table_made")
        s_comb = sem("comb_ready")
        s_s = sem("scores_ready")
        s_min = sem("min_ready")
        s_exp = sem("exp_ready")
        s_inv = sem("expinv_ready")
        s_norm = sem("probs_ready")
        s_t = sem("probs_turned")
        s_pt = sem("probsT_ready")
        s_pv = sem("pv_done")
        s_ql = sem("qlat_ready")
        s_qlT = sem("qlatT_copied")
        s_oh = sem("olat_copied")
        s_uv = sem("uv_done")
        s_mhi = sem("mixed_hi_ready")
        s_mlo = sem("mixed_lo_ready")
        s_racc = sem("residual_acc_ready")
        s_res = sem("residual_added")
        s_guacc = sem("gu_acc_ready")
        s_silu = sem("silu_ready")
        s_up = sem("up_ready")
        s_ffhi = sem("ff_hi_ready")
        s_fflo = sem("ff_lo_ready")
        s_xf = sem("x_normed")
        s_i2acc = sem("in2_acc_ready")
        s_sig = sem("sigmoid_ready")
        s_v = sem("v_ready")
        s_gate = sem("gates_copied")
        s_conv = sem("conv_step")
        s_xs = sem("short_conv_step")
        s_gmm = sem("lru_gate_products")
        s_r = sem("r_ready")
        s_i = sem("i_ready")
        s_gx = sem("gated_ready")
        s_a = sem("decay_ready")
        s_m = sem("mult_step")
        s_mt = sem("mult_ready")
        s_scan = sem("scan_step")
        s_lhi = sem("lru_hi_ready")
        s_llo = sem("lru_lo_ready")
        s_mean = sem("mean_sum")
        s_mu = sem("mean_ready")
        s_cen = sem("centred")
        s_lnu = sem("ln_scaled")
        s_lns = sem("ln_silu")
        s_lnhi = sem("ln_hi_ready")
        s_lnlo = sem("ln_lo_ready")
        s_pacc = sem("pw2_acc_ready")
        s_yc = sem("y_conv_ready")
        s_ychi = sem("yc_hi_ready")
        s_yclo = sem("yc_lo_ready")
        s_lam = sem("lam_step")
        s_lama = sem("lam_act")
        s_ot = sem("out_turned")
        s_on = sem("out_copied")
        s_out = sem("out_stored")

        block = ctx.enter_context(nc.Block())

        def w_cols(w, k0, kn, c0):
            return w.rearrange("(k p) c -> p k c", p=P)[:, k0:k0 + kn, bass.ds(c0, NCOL)]

        @block.sync
        def _(sp):
            def w_dma(n, src, half=None):
                b = n % 2 if half is None else half[0]
                if half is None:
                    if n >= 2:
                        sp.wait_ge(s_lo, n - 1)
                else:
                    sp.wait_ge(s_lo, n - 1)
                kn, cn = src.shape[1], src.shape[2]
                sp.dma_start(w_stage[b][:, 0:kn, 0:cn], src).then_inc(s_stage[b], 16)

            def ada_dma(c):
                if c >= 2:
                    if c - 2 in ADA_PE:
                        sp.wait_ge(s_adadir, ADA_PE.index(c - 2) + 1)
                    else:
                        sp.wait_ge(s_adaacc, ADA_ORD[c - 2] + 1)
                w, j = (a["w_ada"], c) if c < ADA1 else (a["mod_w_2"], c - ADA1)
                src = w.rearrange("(p t) c -> p t c", t=KD)[:, :, j * NCOL:(j + 1) * NCOL]
                sp.dma_start(ada_stage[c % 2][:], src).then_inc(s_ada[c % 2], 16)

            sp.dma_start(c_sb[:, 0, :], a["c"].rearrange("o (p t) -> (o p) t", t=KD)).then_inc(s_c, 16)
            sp.dma_start(c_sb[:, 1, :], a["c_2"].rearrange("o (p t) -> (o p) t", t=KD)).then_inc(s_c, 16)
            ada_dma(0)
            ada_dma(1)
            sp.dma_start(ident[:], a["ident"]).then_inc(s_ident, 16)
            for t in range(TT):
                sp.dma_start(x_nat[:, t, :], a["x"][t * P:(t + 1) * P, :]).then_inc(s_x, 16)
            nvec = 0
            for name, n in VECS:
                if name == "pad":
                    continue
                src = a[name].rearrange("(r c) -> r c", c=P)
                r0, done = VROW[name], 0
                while done < n:
                    tile, row = divmod(r0 + done, P)
                    m = min(n - done, P - row)
                    sp.dma_start(vrow[row:row + m, tile, :], src[done:done + m, :]).then_inc(s_vec, 16)
                    nvec += 1
                    done += m
            assert nvec == NVEC_DMAS, nvec
            sp.dma_start(dist[:], a["dist"]).then_inc(s_const, 16)
            sp.dma_start(maskA[:], a["maskA"]).then_inc(s_const, 16)
            sp.dma_start(causal[:], a["causal"]).then_inc(s_const, 16)
            sp.dma_start(kvg[:], a["kv_norm_g"].to_broadcast([P, P])).then_inc(s_const, 16)
            for c in range(2, ADA_FIRST):
                ada_dma(c)

            def w_in_dma(n):
                c0 = W_IN_COLS[n]
                cn = min(NCOL, a["w_in"].shape[1] - c0)
                w_dma(n, a["w_in"].rearrange("(k p) c -> p k c", p=P)[:, :, c0:c0 + cn])

            w_in_dma(0)
            w_in_dma(1)
            c = ADA_FIRST
            for n in range(N_IN):
                for _ in range(ADA_WINDOW.get(n, 0)):
                    ada_dma(c)
                    c += 1
                if n == 5:
                    sp.wait_ge(s_vt, 1)
                    sp.dma_start(wuk[:], a["w_uk"].rearrange("(g e) d r -> (e d) g r", e=2)).then_inc(s_late, 16)
                    sp.dma_start(wuv[:], a["w_uv"].rearrange("h r d -> r h d")).then_inc(s_late, 16)
                if n + 2 < N_IN:
                    w_in_dma(n + 2)
            w_dma(C_OUT, w_cols(a["w_out"], 0, KD, 0))
            w_dma(C_OUT + 1, w_cols(a["w_out"], 0, KD, NCOL))
            w_dma(C_OUT + 2, w_cols(a["w_out"], 0, KD, 2 * NCOL))
            w_dma(C_OUT + 3, w_cols(a["w_out"], 0, KD, 3 * NCOL))

            def stream(n0, steps, srcs, first=0):
                per = len(srcs)
                with sp.Fori(first, first + steps) as j:
                    for q, src in enumerate(srcs):
                        w_dma(j * per + (n0 + q - first * per), src(j), half=((n0 + q) % 2,))

            sp.wait_ge(s_res, 1)
            with sp.Fori(2, KF // 2 + 2) as j:
                w_dma(j * 2 + (C_GU - 4), w_cols(a["w_gu"], 0, KD, j * NCOL - 2 * NCOL), half=(C_GU % 2,))
                w_dma(j * 2 + (C_GU - 3), w_cols(a["w_gu"], 0, KD, j * NCOL + (D_FF - 2 * NCOL)), half=((C_GU + 1) % 2,))
                sp.wait_ge(s_adaacc, j + (ADA_DVE - 2))
                sp.dma_start(ada2_stage[:], a["mod_w_2"].rearrange("(p t) c -> p t c", t=KD)[
                    :, :, bass.ds(j * NCOL + (ADA_LOOP - ADA1 - 2) * NCOL, NCOL)]).then_inc(s_adaloop, 16)
            groups = [(0, 8), (8, 8), (16, 6)]
            stream(C_DOWN, 2, [lambda j, m=m, g=g: w_cols(a["w_down"], g[0], g[1], j * 2 * NCOL + m * NCOL)
                               for m in range(2) for g in groups])
            stream(C_IN2, 4, [lambda j: w_cols(a["w_in_2"], 0, KD, j * NCOL + (D - NCOL)),
                              lambda j: w_cols(a["w_in_2"], 0, KD, j * NCOL - NCOL)], first=1)
            for part in (3, 4, 2):
                n0 = C_IN2 + 8 + 4 * (3, 4, 2).index(part)
                stream(n0, 2, [lambda j, q=q, part=part: w_cols(a["w_in_2"], 0, KD, j * 2 * NCOL + part * D + q * NCOL)
                               for q in range(2)])
            for g in range(2):
                if g == 0:
                    sp.wait_ge(s_res, 2 * KD)
                sp.dma_start((wr, wi)[g][:], a[("wr_2", "wi_2")[g]].rearrange("h d e -> d h e")).then_inc(s_lruw, 16)
            stream(C_LRU, 2, [lambda j, q=q: w_cols(a["w_out_2"], KD, KD, j * 2 * NCOL + q * NCOL) for q in range(2)])
            stream(C_PW2, 2, [lambda j, q=q: w_cols(a["pw2_w_2"], 0, KD, j * 2 * NCOL + q * NCOL) for q in range(2)])
            stream(C_OUT2, 2, [lambda j, q=q: w_cols(a["w_out_2"], 0, KD, j * 2 * NCOL + q * NCOL) for q in range(2)])

            for t in range(TT):
                sp.wait_ge(s_on, 2 * (t + 1))
                sp.dma_start(out[t * P:(t + 1) * P, :], o_nat[:, t, :]).then_inc(s_out, 16)
            sp.wait_ge(s_out, 16 * TT)

        @block.gpsimd
        def _(pool):
            def lo(n, b):
                pool.wait_ge(s_hi, n + 1)
                nc.gpsimd.tensor_tensor(w_lo[b][:], w_stage[b][:], w_hi[b][:].bitcast(F32),
                                        ALU.subtract).then_inc(s_lo, 1)


            slopes = [2.0 ** (-8.0 * (g + 1.0) / 16) for g in range(16)]

            def make_table(g):
                kind, h = g // NH, g % NH
                if g >= 2:
                    if g - 2 < NH:
                        pool.wait_ge(s_min, TT * (g - 1))
                    else:
                        pool.wait_ge(s_comb, TT * (g - 2 - NH + 1))
                m = nc.gpsimd.tensor_scalar(table[g % 2][:], dist[:], float(slopes[2 * h + kind]), 0.0, ALU.mult, ALU.add)
                if kind == 0:
                    m.then_inc(s_tabm, 1)
                    pool.wait_ge(s_tabm, h + 1)
                    m = nc.gpsimd.tensor_tensor(table[g % 2][:], table[g % 2][:], maskA[:], ALU.add)
                m.then_inc(s_tab, 1)

            for n in range(C_OUT + 2):
                lo(n, n % 2)
                if n == 5:
                    pool.wait_ge(s_const, 16 * NCONST)
                    make_table(0)
                    make_table(1)
            for g in range(2, NH):
                make_table(g)
            for h in range(NH):
                make_table(NH + h)
                pool.wait_ge(s_tab, NH + h + 1)
                for i in range(TT):
                    s, n = TT * h + i, P * (i + 1)
                    if s == 0:
                        pool.wait_ge(s_top, TOP_STEPS)
                    if s >= 2:
                        pool.wait_ge(s_min, TT * NH + s - 1)
                    t = table[h % 2][:, T - n:T]
                    if i == 0:
                        nc.gpsimd.tensor_tensor(comb[s % 2][:, 0:n], t, causal[:, 0, :], ALU.add).then_inc(s_comb, 1)
                    else:
                        nc.gpsimd.tensor_tensor(comb[s % 2][:, 0:n], t, work[i][:], ALU.add).then_inc(s_comb, 1)
            lo(C_OUT + 2, (C_OUT + 2) % 2)
            lo(C_OUT + 3, (C_OUT + 3) % 2)
            for n0, n1 in ((C_GU, C_END),):
                odd = (n1 - n0) % 2
                with pool.Fori(0, (n1 - n0) // 2) as j:
                    for q in range(2):
                        lo(j * 2 + (n0 + q), (n0 + q) % 2)
                if odd:
                    lo(n1 - 1, (n1 - 1) % 2)

        @block.tensor
        def _(pe):
            def chunk_ready(n):
                pe.wait_ge(s_lo, n + 1)

            def normed_parts(j, k):
                pe.wait_ge(s_alo, KD * j + k + 1)

            def tile(dst, b, cols, n_k, rhs_hi, rhs_lo, first=True, last=True, wait=None):
                for k in range(n_k):
                    if wait:
                        wait(k)
                    wh, wl = w_hi[b][:, k, cols], w_lo[b][:, k, cols]
                    pe.matmul(dst, wh, rhs_hi(k), start=(first and k == 0), stop=False)
                    pe.matmul(dst, wh, rhs_lo(k), start=False, stop=False)
                    mm = pe.matmul(dst, wl, rhs_hi(k), start=False, stop=(last and k == n_k - 1))
                return mm

            def tile_tokens(dst, b, cols, t, wait=None):
                ts = slice(t * P, (t + 1) * P)
                for k in range(KD):
                    if wait:
                        wait(k)
                    ah, al = act_hi[:, k, ts], act_lo[:, k, ts]
                    pe.matmul(dst, ah, w_hi[b][:, k, cols], start=(k == 0), stop=False)
                    pe.matmul(dst, ah, w_lo[b][:, k, cols], start=False, stop=False)
                    mm = pe.matmul(dst, al, w_hi[b][:, k, cols], start=False, stop=(k == KD - 1))
                return mm

            pe.wait_ge(s_set, 2)
            pe.wait_ge(s_ident, 16)
            pe.wait_ge(s_vec, 16 * NVEC_DMAS)
            for q, rows in enumerate(VROWS):
                mm = pe.transpose(bank[4][:, q * P:q * P + rows], vrow[0:rows, q, :], ident[0:rows, 0:rows])
            mm.then_inc(s_vt, 1)
            pe.wait_ge(s_x, 16 * TT)
            for k in range(KD):
                if k >= 4:
                    pe.wait_ge(s_xTr, k - 3)
                for t in range(TT):
                    mm = pe.transpose(bank[k % 4][:, t * P:(t + 1) * P], x_nat[:, t, k * P:(k + 1) * P], ident[:])
                mm.then_inc(s_xt, 1)

            norms = [0]

            def sum_squares(total=s_ss):
                j = norms[0]
                norms[0] += 1
                for k in range(KD):
                    pe.wait_ge(s_sq, KD * j + k + 1)
                    mm = pe.matmul(bank[4][:], ones[:], tmp[k % 2][:], start=(k == 0), stop=(k == KD - 1))
                    mm.then_inc(s_sqused, 1)

            def ada_products(c):
                o = ADA_ORD[c]
                pe.wait_ge(s_adaacc, o + 1)
                for m in range(2):
                    mm = pe.matmul(bank[7][:, 2 * c + m:2 * c + m + 1],
                                   ada_acc[o % 2][:, 0, m * P:(m + 1) * P], ones[:, 0:1], start=True, stop=True)
                mm.then_inc(s_adamm, 1)

            def ada_direct(c):
                pe.wait_ge(s_ada[c % 2], 16 * (c // 2 + 1))
                pe.wait_ge(s_cact, 1)
                for m in range(2):
                    for t in range(KD):
                        mm = pe.matmul(bank[7][:, 2 * c + m:2 * c + m + 1], ada_stage[c % 2][:, t, m * P:(m + 1) * P],
                                       c_act[:, 0, t:t + 1], start=(t == 0), stop=(t == KD - 1))
                mm.then_inc(s_adadir, 1)

            pe.wait_ge(s_vcol, 2)
            for c in range(ADA_FIRST):
                if c in ADA_PE:
                    ada_direct(c)
                else:
                    ada_products(c)
                if c == 3:
                    sum_squares()

            hi = lambda k: act_hi[:, k, :]
            lo = lambda k: act_lo[:, k, :]
            t_acc = [0]

            def acc_bank():
                if t_acc[0] >= 4:
                    pe.wait_ge(s_free, t_acc[0] - 3 + (t_acc[0] - 4 >= 5))
                b = bank[t_acc[0] % 4]
                t_acc[0] += 1
                return b

            pairs = list(enumerate(PAIRS))

            def logits():
                for _ in range(PAIRS_PER_TILE):
                    if not pairs:
                        return
                    s, (i, h) = pairs.pop(0)
                    if s == 0:
                        pe.wait_ge(s_free, 7)
                        pe.wait_ge(s_wi, 1)
                    if s >= 2:
                        pe.wait_ge(s_relu, s - 1)
                    half = slice(HD * (h % 2), HD * (h % 2) + HD)
                    n = P * (i + 1)
                    pe.matmul(bank[4 + s % 2][:, 0:n], qiT[half, h // 2, i * P:(i + 1) * P], kiT[half, 0:n],
                              start=True, stop=True).then_inc(s_lg, 1)

            ada_at = [ADA_FIRST]

            def ada_next(count):
                for _ in range(count):
                    ada_products(ada_at[0])
                    ada_at[0] += 1

            for n in range(N_IN):
                chunk_ready(n)
                b = n % 2
                if n == 0:
                    dst = acc_bank()
                    for t in range(TT):
                        mm = tile_tokens(dst[:, t * P:(t + 1) * P], b, slice(0, P), t, (lambda k: normed_parts(0, k)) if t == 0 else None)
                    mm.then_inc(s_acc, 1)
                    ada_next(1)
                    tile(acc_bank()[:], b, slice(P, 2 * P), KD, hi, lo).then_inc(s_wused, 1)
                    ada_next(2)
                elif n == 2:
                    tile(acc_bank()[:], b, slice(0, P), KD, hi, lo).then_inc(s_acc, 1)
                    ada_next(1)
                    tile(acc_bank()[:], b, slice(P, 2 * P), KD, hi, lo).then_inc(s_wused, 1)
                    ada_next(2)
                    pe.wait_ge(s_free, 7)
                    for t in range(TT):
                        mm = pe.transpose(bank[5][:, t * 8:(t + 1) * 8], wiT[HD:HD + 8, t * P:(t + 1) * P],
                                          ident[HD:HD + 8, HD:HD + 8])
                    mm.then_inc(s_wiT, 1)
                elif n >= 9:
                    for tp in range(2):
                        dst = acc_bank()
                        for t in (2 * tp, 2 * tp + 1):
                            mm = tile_tokens(dst[:, (t % 2) * NCOL:(t % 2 + 1) * NCOL], b, slice(0, NCOL), t)
                        mm.then_inc((s_acc, s_wused)[tp], 1)
                else:
                    for m in range(2):
                        tile(acc_bank()[:], b, slice(m * P, (m + 1) * P), KD, hi, lo).then_inc((s_acc, s_wused)[m], 1)
                        ada_next(max(0, min(m + 1, ADA_WINDOW.get(n, 0) - 1)))
                        if n >= 3:
                            logits()
                if n == 2:
                    pe.wait_ge(s_ckv, CKV_STEPS)
                    for t in range(TT):
                        mm = pe.transpose(bank[6][:, t * P:(t + 1) * P], ckv[:, t, :], ident[:])
                    mm.then_inc(s_ckvt, 1)
            assert not pairs and t_acc[0] == N_IN_TILES

            pe.wait_ge(s_free, N_IN_TILES + 1)
            pe.wait_ge(s_ckvT, 1)
            pe.wait_ge(s_late, 32)
            n_items = len(ITEMS)
            O_BANK = (7, 1)

            def q_lat(h):
                half = slice(HD * (h % 2), HD * (h % 2) + HD)
                if h >= 1:
                    pe.wait_ge(s_qlT, h)
                pe.matmul(bank[2][:], wuk[half, h // 2, :], qbT[half, h // 2, :], start=True, stop=True).then_inc(s_ql, 1)

            def scores(s):
                kind, h, i = ITEMS[s]
                n = P * (i + 1)
                if s >= 2:
                    pe.wait_ge(s_min, s - 1)
                qs = slice(i * P, (i + 1) * P)
                if kind == "A":
                    half = slice(HD * (h % 2), HD * (h % 2) + HD)
                    lhs, rhs = qaT[half, h // 2, qs], kaT[half, h // 2, 0:n]
                else:
                    pe.wait_ge(s_qlT, h + 1)
                    lhs, rhs = qlatT[h % 2][:, qs], ckvT[:, 0:n]
                pe.matmul(bank[4 + s % 2][:, 0:n], lhs, rhs, start=True, stop=True).then_inc(s_s, 1)

            def turn(s):
                i = ITEMS[s][2]
                pe.wait_ge(s_norm, s + 1)
                if s >= 1:
                    pe.wait_ge(s_pt, s)
                for kb in range(i + 1):
                    mm = pe.transpose(bank[6][:, kb * P:(kb + 1) * P], probs[s % 4][:, kb * P:(kb + 1) * P], ident[:])
                mm.then_inc(s_t, 1)

            def weigh(s):
                kind, h, i = ITEMS[s]
                g = s // TT
                pe.wait_ge(s_pt, s + 1)
                if i == 0 and g >= 2:
                    if g - 2 < NH:
                        pe.wait_ge(s_mlo, g - 1)
                    else:
                        pe.wait_ge(s_oh, g - 1 - NH)
                qs = slice(i * P, (i + 1) * P)
                o = bank[O_BANK[g % 2]]
                for kb in range(i + 1):
                    if kind == "A":
                        half = slice(HD * (h % 2), HD * (h % 2) + HD)
                        lhs, dst = va[:, kb, h * HD:(h + 1) * HD], o[half, qs]
                    else:
                        lhs, dst = ckv[:, kb, :], o[:, qs]
                    mm = pe.matmul(dst, lhs, probsT[s % 3][:, kb, :], start=(kb == 0), stop=(kb == i))
                mm.then_inc(s_pv, 1)

            def up_v(h):
                half = slice(HD * (h % 2), HD * (h % 2) + HD)
                pe.wait_ge(s_oh, h + 1)
                if h >= 1:
                    pe.wait_ge(s_mlo, NH + h)
                pe.matmul(bank[3][half, :], wuv[:, h, :], olat[h % 2][:], start=True, stop=True).then_inc(s_uv, 1)

            assert ada_at[0] == ADA_LOOP
            pe.wait_ge(s_mod, 3)
            for s in range(n_items + 9):
                if s < n_items:
                    kind, h, i = ITEMS[s]
                    if s + 2 < n_items and ITEMS[s + 2][0] == "B" and ITEMS[s + 2][2] == 0:
                        q_lat(ITEMS[s + 2][1])
                    scores(s)
                if 3 <= s < n_items + 3:
                    turn(s - 3)
                if 5 <= s < n_items + 5:
                    weigh(s - 5)
                if s >= 7 and s - 7 < n_items and ITEMS[s - 7][0] == "B" and ITEMS[s - 7][2] == TT - 1:
                    up_v(ITEMS[s - 7][1])

            def project(n0, steps, ready, rhs_hi, rhs_lo, waits=None, groups=((0, KD),), pairs=1, t0=0):
                with pe.Fori(0, steps) as j:
                    n = 0
                    for m2 in range(pairs):
                        base = 2 * (m2 % 2) if pairs > 1 else 0
                        for g, (k0, kn) in enumerate(groups):
                            b = (n0 + n) % 2
                            pe.wait_ge(s_lo, j * (pairs * len(groups)) + (n0 + n + 1))
                            for m in range(2):
                                if g == 0 and waits:
                                    waits(j, 2 * m2 + m)
                                mm = tile(bank[base + m][:], b, slice(m * P, (m + 1) * P), kn,
                                          lambda k, k0=k0: rhs_hi(k0 + k), lambda k, k0=k0: rhs_lo(k0 + k),
                                          first=(g == 0), last=(g == len(groups) - 1))
                                if m == 1:
                                    mm.then_inc(s_wused, 1)
                                elif g == len(groups) - 1:
                                    mm.then_inc(ready, 1)
                            n += 1

            pe.wait_ge(s_mlo, 2 * NH)
            RES = [0]

            def residual(n0, rhs_hi, rhs_lo, groups=((0, KD),)):
                r0 = RES[0]
                RES[0] += KD

                def waits(j, t):
                    pe.wait_ge(s_res, j * 4 + (r0 + t - 3))

                if r0:
                    project(n0, 2, s_racc, rhs_hi, rhs_lo, waits, groups, pairs=2)
                else:
                    n = 0
                    for t in range(KD):
                        b = (n0 + n) % 2
                        if t % 2 == 0:
                            pe.wait_ge(s_lo, n0 + n + 1)
                        if t >= 4:
                            pe.wait_ge(s_res, t - 3)
                        tile(bank[t % 4][:], b, slice((t % 2) * P, (t % 2 + 1) * P), KD, rhs_hi, rhs_lo).then_inc((s_racc, s_wused)[t % 2], 1)
                        n += t % 2

            residual(C_OUT, hi, lo)
            sum_squares()
            pe.wait_ge(s_res, KD)
            with pe.Fori(0, KF // 2) as j:
                for q in range(2):
                    b = (C_GU + q) % 2
                    pe.wait_ge(s_lo, j * 2 + (C_GU + q + 1))
                    for m in range(2):
                        pe.wait_ge((s_silu, s_up)[q], j * 2 + (1 + m))
                        tile(bank[2 * q + m][:], b, slice(m * P, (m + 1) * P), KD, hi, lo,
                             wait=(lambda k: normed_parts(1, k)) if (q, m) == (0, 0) else None).then_inc((s_guacc, s_wused)[m], 1)
                pe.wait_ge(s_adaacc, j + (ADA_DVE + 1))
                for m in range(2):
                    mm = pe.matmul(bank[5][:, bass.ds(j * 2 + m, 1)], ada2_acc[:, m * P:(m + 1) * P], ones[:, 0:1],
                                   start=True, stop=True)
                mm.then_inc(s_adamm, 1)
            pe.wait_ge(s_silu, 2 + KF)
            pe.wait_ge(s_up, 2 + KF)
            pe.wait_ge(s_fflo, 2 + KF)
            residual(C_DOWN, lambda k: ff_hi[:, k, :], lambda k: ff_lo[:, k, :], ((0, 8), (8, 8), (16, 6)))
            sum_squares()
            sum_squares()
            pe.wait_ge(s_res, 2 * KD)
            with pe.Fori(0, KD // 2) as j:
                for q in range(2):
                    b = (C_IN2 + q) % 2
                    pe.wait_ge(s_lo, j * 2 + (C_IN2 + q + 1))
                    for m in range(2):
                        pe.wait_ge(s_v, j * 2 + (1 + m))
                        tile(bank[2 * q + m][:], b, slice(m * P, (m + 1) * P), KD, hi, lo,
                             wait=(lambda k: normed_parts(2, k)) if (q, m) == (0, 0) else None).then_inc((s_i2acc, s_wused)[m], 1)
            pe.wait_ge(s_v, 2 + KD)
            with pe.Fori(0, 6) as j:
                for q in range(2):
                    b = (C_IN2 + 8 + q) % 2
                    pe.wait_ge(s_lo, j * 2 + (C_IN2 + 8 + q + 1))
                    for m in range(2):
                        pe.wait_ge(s_gate, j * 4 + (2 * q + m + 1))
                        tile(bank[2 * q + m][:], b, slice(m * P, (m + 1) * P), KD, hi, lo).then_inc((s_i2acc, s_wused)[m], 1)
            pe.wait_ge(s_lruw, 32)
            for k in range(KD):
                pe.wait_ge(s_xs, SHORT * (k + 1))
                for g in range(2):
                    if k >= 1:
                        pe.wait_ge((s_r, s_i)[g], k)
                    pe.matmul(bank[5 + g][:], (wr, wi)[g][:, k, :], tmp[k % 2][:], start=True, stop=True).then_inc(s_gmm, 1)
            pe.wait_ge(s_gate, 4 + 24)
            pe.wait_ge(s_llo, KD)
            residual(C_LRU, hi, lo)
            pe.wait_ge(s_conv, CONV * KD)
            for k in range(KD):
                mm = pe.matmul(bank[5][:], ones[:], conv[:, k, :], start=(k == 0), stop=(k == KD - 1))
            mm.then_inc(s_mean, 1)
            sum_squares()
            pe.wait_ge(s_lnlo, KD)
            pe.wait_ge(s_res, 3 * KD)
            with pe.Fori(0, 2) as j:
                for q in range(2):
                    b = (C_PW2 + q) % 2
                    pe.wait_ge(s_lo, j * 2 + (C_PW2 + q + 1))
                    for m in range(2):
                        pe.wait_ge(s_yc, j * 4 + (2 * q + m + 1))
                        tile(bank[2 * q + m][:], b, slice(m * P, (m + 1) * P), KD,
                             lambda k: ln_hi[:, k, :], lambda k: ln_lo[:, k, :]).then_inc((s_pacc, s_wused)[m], 1)
            pe.wait_ge(s_yc, 4 + KD)
            pe.wait_ge(s_yclo, KD)
            residual(C_OUT2, lambda k: yc_hi[:, k, :], lambda k: yc_lo[:, k, :])
            sum_squares()
            pe.wait_ge(s_xf, 2 * KD)
            pe.wait_ge(s_res, 4 * KD)
            for s in range(2 * TT):
                t, half = divmod(s, 2)
                if s >= 4:
                    pe.wait_ge(s_on, s - 3)
                for q in range(4):
                    k = 4 * half + q
                    mm = pe.transpose(bank[s % 4][:, q * P:(q + 1) * P], xT[:, k, t * P:(t + 1) * P], ident[:])
                mm.then_inc(s_ot, 1)

        @block.scalar
        def _(act):
            def hi_part(n, b, half):
                act.wait_ge(s_stage[b], half * 16 + 16)
                if not isinstance(n, int) or n >= 2:
                    act.wait_ge(s_wused, n - 1)
                nc.scalar.activation(w_hi[b][:], w_stage[b][:], ACT.Copy).then_inc(s_hi, 1)

            act.wait_ge(s_c, 32)
            nc.scalar.activation(c_act[:], c_sb[:], ACT.Silu).then_inc(s_cact, 1)
            act.wait_ge(s_vt, 1)
            nc.scalar.activation(vcol[:, 0:208], bank[4][:, 0:208], ACT.Copy).then_inc(s_vcol, 1)
            nc.scalar.activation(vcol[:, 256:504], bank[4][:, 256:504], ACT.Copy).then_inc(s_vcol, 1)
            for k in range(KD):
                act.wait_ge(s_xt, k + 1)
                nc.scalar.activation(xT[:, k, :], bank[k % 4][:], ACT.Copy).then_inc(s_xTr, 1)

            norms = [0]

            def squares(ready, src=None, inv=1.0 / D):
                j = norms[0]
                norms[0] += 1
                for k in range(KD):
                    ready(k)
                    if KD * j + k >= 2:
                        act.wait_ge(s_sqused, KD * j + k - 1)
                    nc.scalar.activation(tmp[k % 2][:], (src or xT)[:, k, :], ACT.Square).then_inc(s_sq, 1)
                act.wait_ge(s_sqused, KD * (j + 1))
                if j >= 1:
                    act.wait_ge(s_rstd, j)
                act.wait_ge(s_set, 2)
                nc.scalar.activation(rstd[:], bank[4][:], ACT.Sqrt, bias=eps[:, 0:1], scale=inv).then_inc(s_sd, 1)

            splits = [0]

            def act_hi_parts(shift):
                j = splits[0]
                splits[0] += 1
                for k in range(KD):
                    act.wait_ge(s_u, KD * j + k + 1)
                    nc.scalar.activation(act_hi[:, k, :], tmp[k % 2][:], ACT.Identity, bias=modc(shift + k)).then_inc(s_ahi, 1)

            squares(lambda k: act.wait_ge(s_xTr, k + 1))
            hi_part(0, 0, 0)
            hi_part(1, 1, 0)
            act.wait_ge(s_mod, 2)
            act_hi_parts(SH1)

            tiles = [0]

            firsts = [0]

            def arrived(n, last):
                if last:
                    act.wait_ge(s_wused, n + 1)
                else:
                    firsts[0] += 1
                    act.wait_ge(s_acc, firsts[0])

            def take(n, last, dst, src, scale=1.0):
                t = tiles[0]
                arrived(n, last)
                i = nc.scalar.activation(dst, src(bank[t % 4]), ACT.Copy, scale=scale)
                tiles[0] += 1
                return i

            whole = lambda b: b[:]
            pairs = list(enumerate(PAIRS))

            def relus():
                for _ in range(PAIRS_PER_TILE):
                    if not pairs:
                        return
                    s, (i, h) = pairs.pop(0)
                    n = P * (i + 1)
                    act.wait_ge(s_lg, s + 1)
                    if s >= 2:
                        act.wait_ge(s_score, s - 1)
                    nc.scalar.activation(relu[s % 2][:, 0:n], bank[4 + s % 2][:, 0:n], ACT.Relu).then_inc(s_relu, 1)

            for n in range(N_IN):
                if n == 0:
                    take(n, False, ckv[:].rearrange("p t r -> p (t r)"), whole).then_inc(s_free, 1)
                    take(n, True, qiT[:, 0, :], whole).then_inc(s_free, 1)
                elif n == 1:
                    take(n, False, qiT[:, 1, :], whole).then_inc(s_free, 1)
                    take(n, True, qiT[:, 2, :], whole).then_inc(s_free, 1)
                elif n == 2:
                    take(n, False, qiT[:, 3, :], whole).then_inc(s_free, 1)
                    t = tiles[0]
                    arrived(n, True)
                    nc.scalar.activation(kiT[0:HD, :], bank[t % 4][0:HD, :], ACT.Copy)
                    nc.scalar.activation(kiT[HD:P, :], bank[t % 4][0:HD, :], ACT.Copy).then_inc(s_free, 1)
                    nc.scalar.activation(wiT[HD:HD + 8, :], bank[t % 4][HD:HD + 8, :], ACT.Copy, scale=IDX_SCALE).then_inc(s_free, 1)
                    tiles[0] += 1
                    act.wait_ge(s_wiT, 1)
                    nc.scalar.activation(wi_sb[:].rearrange("p t h -> p (t h)"), bank[5][:, 0:TT * 8], ACT.Copy).then_inc(s_wi, 1)
                    act.wait_ge(s_ckv, TT)
                    nc.scalar.activation(ckv_ss[:, 1, :], ckv_ss[:, 0, :], ACT.Sqrt, bias=eps[:, 0:1], scale=1.0 / P).then_inc(s_ckvsd, 1)
                    act.wait_ge(s_ckvt, 1)
                    nc.scalar.activation(ckvT[:], bank[6][:], ACT.Copy).then_inc(s_ckvT, 1)
                elif n >= 9:
                    for tp in range(2):
                        vs = slice((n - 9) * NCOL, (n - 8) * NCOL)
                        take(n, tp == 1, va[:, 2 * tp:2 * tp + 2, vs], lambda b: b[:].rearrange("p (t c) -> p t c", t=2)).then_inc(s_free, 1)
                else:
                    for m in range(2):
                        if n <= 4:
                            take(n, m == 1, qbT[:, 2 * (n - 3) + m, :], whole).then_inc(s_free, 1)
                        elif n <= 6:
                            take(n, m == 1, qaT[:, 2 * (n - 5) + m, :], whole, QSCALE).then_inc(s_free, 1)
                        else:
                            take(n, m == 1, kaT[:, 2 * (n - 7) + m, :], whole).then_inc(s_free, 1)
                        relus()
                hi_part(n + 2, n % 2, (n + 2) // 2)
            assert tiles[0] == N_IN_TILES

            O_BANK = (7, 1)
            n_items = len(ITEMS)

            def exponentials(s):
                n = P * (ITEMS[s][2] + 1)
                act.wait_ge(s_min, s + 1)
                if s >= 4:
                    act.wait_ge(s_t, s - 3)
                nc.scalar.activation(probs[s % 4][:, 0:n], tmp[s % 2][:, 0:n], ACT.Exp, bias=negmax[:, s:s + 1],
                                     scale=-1.0, accum_out=expsum[:, s:s + 1]).then_inc(s_exp, 1)

            def turned(s):
                i = ITEMS[s][2]
                n = P * (i + 1)
                act.wait_ge(s_t, s + 1)
                if s >= 3:
                    act.wait_ge(s_pv, s - 2)
                nc.scalar.activation(probsT[s % 3][:, 0:i + 1, :].rearrange("p k q -> p (k q)"),
                                     bank[6][:, 0:n], ACT.Copy).then_inc(s_pt, 1)

            for s in range(n_items + 9):
                if s < n_items:
                    if s + 2 < n_items and ITEMS[s + 2][0] == "B" and ITEMS[s + 2][2] == 0:
                        h = ITEMS[s + 2][1]
                        act.wait_ge(s_ql, h + 1)
                        if h >= 2:
                            act.wait_ge(s_s, TT * (NH + h - 1))
                        nc.scalar.activation(qlatT[h % 2][:], bank[2][:], ACT.Copy, scale=QSCALE).then_inc(s_qlT, 1)
                    exponentials(s)
                if 3 <= s < n_items + 3:
                    turned(s - 3)
                if 6 <= s < n_items + 6 and ITEMS[s - 6][2] == TT - 1:
                    kind, h, i = ITEMS[s - 6]
                    act.wait_ge(s_pv, s - 5)
                    if kind == "A":
                        half = slice(HD * (h % 2), HD * (h % 2) + HD)
                        nc.scalar.activation(act_hi[half, h // 2, :], bank[O_BANK[h % 2]][half, :], ACT.Copy).then_inc(s_mhi, 1)
                    else:
                        if h >= 2:
                            act.wait_ge(s_uv, h - 1)
                        nc.scalar.activation(olat[h % 2][:], bank[O_BANK[h % 2]][:], ACT.Copy).then_inc(s_oh, 1)
                if s >= 8 and s - 8 < n_items and ITEMS[s - 8][0] == "B" and ITEMS[s - 8][2] == TT - 1:
                    h = ITEMS[s - 8][1]
                    half = slice(HD * (h % 2), HD * (h % 2) + HD)
                    act.wait_ge(s_uv, h + 1)
                    nc.scalar.activation(act_hi[half, 4 + h // 2, :], bank[3][half, :], ACT.Copy).then_inc(s_mhi, 1)

            for n in range(C_OUT, C_GU):
                hi_part(n + 2, n % 2, (n + 2) // 2)
            squares(lambda k: act.wait_ge(s_res, k + 1))
            act.wait_ge(s_mod, 4)
            act_hi_parts(SH2)
            act.wait_ge(s_alo, 2 * KD)
            nc.scalar.activation(lam_t[:, 6, 0:1], eps[:, 0:1], ACT.Silu).then_inc(s_silu, 2)
            with act.Fori(0, KF // 2) as j:
                for q in range(2):
                    for m in range(2):
                        if q == 0:
                            act.wait_ge((s_guacc, s_wused)[m], j * 2 + (1, C_GU + 1)[m])
                            act.wait_ge(s_up, j * 2 + (1 + m))
                            nc.scalar.activation(tmp[m][:], bank[m][:], ACT.Silu).then_inc(s_silu, 1)
                    hi_part(j * 2 + (C_GU + q + 2), (C_GU + q) % 2, j + (C_GU + q + 2) // 2)
            with act.Fori(0, 6) as j:
                for q in range(2):
                    hi_part(j * 2 + (C_DOWN + q + 2), (C_DOWN + q) % 2, j + (C_DOWN + q + 2) // 2)
            squares(lambda k: act.wait_ge(s_res, KD + k + 1))
            squares(lambda k: act.wait_ge(s_xf, k + 1))
            act.wait_ge(s_mod, 7)
            act_hi_parts(SH3)
            nc.scalar.activation(lam_t[:, 6, 0:1], eps[:, 0:1], ACT.Sigmoid).then_inc(s_sig, 1)
            act.wait_ge(s_alo, 3 * KD)
            with act.Fori(0, KD // 2) as j:
                for q in range(2):
                    if q == 0:
                        for m in range(2):
                            act.wait_ge((s_i2acc, s_wused)[m], j * 2 + (1, C_IN2 + 1)[m])
                            act.wait_ge(s_v, j * 2 + (1 + m))
                            nc.scalar.activation(tmp[m][:], bank[m][:], ACT.Sigmoid).then_inc(s_sig, 1)
                    hi_part(j * 2 + (C_IN2 + q + 2), (C_IN2 + q) % 2, j + (C_IN2 + q + 2) // 2)
            nc.scalar.activation(lam_t[:, 7, 0:1], eps[:, 0:1], ACT.Silu).then_inc(s_gate, 4)
            for part, (dst, func, lead) in enumerate(((l_pad, ACT.Copy, PADL), (lgate, ACT.Silu, 0), (cgate, ACT.Silu, 0))):
                with act.Fori(0, 2) as j:
                    for q in range(2):
                        for m in range(2):
                            act.wait_ge((s_i2acc, s_wused)[m], j * 2 + (KD + 4 * part + q + 1 + m * C_IN2))
                            nc.scalar.activation(dst[:, bass.ds(j * 4 + (2 * q + m), 1), lead:lead + T],
                                                 bank[2 * q + m][:].rearrange("p (o t) -> p o t", o=1), func).then_inc(s_gate, 1)
                        n = C_IN2 + 8 + 4 * part + q + 2
                        hi_part(j * 2 + n, n % 2, j + n // 2)
            lam = vcol[:, VROW["lam_2"]:VROW["lam_2"] + KD]
            nc.scalar.activation(lam_t[:, 0, :], lam, ACT.Abs).then_inc(s_lama, 1)
            act.wait_ge(s_lama, 1)
            nc.scalar.activation(lam_t[:, 1, :], lam_t[:, 0, :], ACT.Exp, scale=-1.0).then_inc(s_lama, 1)
            act.wait_ge(s_lama, 2)
            act.wait_ge(s_lam, 2)
            nc.scalar.activation(lam_t[:, 3, :], lam_t[:, 2, :], ACT.Ln).then_inc(s_lama, 1)
            for k in range(KD):
                act.wait_ge(s_gmm, 2 * k + 1)
                nc.scalar.activation(decay[:, k, :], bank[5][:], ACT.Sigmoid, bias=col("br_2", k)).then_inc(s_r, 1)
                act.wait_ge(s_gmm, 2 * k + 2)
                if k >= 2:
                    act.wait_ge(s_gx, k - 1)
                nc.scalar.activation(tmp[2 + k % 2][:], bank[6][:], ACT.Sigmoid, bias=col("bi_2", k)).then_inc(s_i, 1)
            act.wait_ge(s_lam, LAM_STEPS)
            for k in range(KD):
                act.wait_ge(s_r, k + 1)
                act.wait_ge(s_gx, k + 1)
                nc.scalar.activation(l_pad[:, k, 0:T], decay[:, k, :], ACT.Tanh, scale=lam_t[:, 5, k:k + 1]).then_inc(s_a, 1)
                act.wait_ge(s_a, 2 * k + 1)
                nc.scalar.activation(decay[:, k, :], decay[:, k, :], ACT.Exp, scale=lam_t[:, 4, k:k + 1]).then_inc(s_a, 1)
            for k in range(KD):
                act.wait_ge(s_m, 3 * (k + 1))
                nc.scalar.activation(l_pad[:, k, 0:T], l_pad[:, k, 0:T], ACT.Sqrt, scale=2.0).then_inc(s_mt, 1)
            for n in range(C_LRU, C_PW2):
                hi_part(n + 2, n % 2, (n + 2) // 2)
            act.wait_ge(s_mean, 1)
            nc.scalar.activation(tmp[2][:], bank[5][:], ACT.Copy, scale=1.0 / D).then_inc(s_mu, 1)
            squares(lambda k: act.wait_ge(s_cen, k + 1), conv)
            for k in range(KD):
                act.wait_ge(s_lnu, k + 1)
                if k >= 2:
                    act.wait_ge(s_lnlo, k - 1)
                nc.scalar.activation(tmp[2 + k % 2][:], tmp[k % 2][:], ACT.Silu, bias=col("cln_b_2", k)).then_inc(s_lns, 1)
            for n in range(C_PW2, C_END - 2):
                hi_part(n + 2, n % 2, (n + 2) // 2)
            squares(lambda k: act.wait_ge(s_res, 3 * KD + k + 1))
            for s in range(2 * TT):
                t, half = divmod(s, 2)
                act.wait_ge(s_ot, s + 1)
                nc.scalar.activation(o_nat[:, t, half * 512:(half + 1) * 512], bank[s % 4][:], ACT.Copy).then_inc(s_on, 1)

        @block.vector
        def _(dve):
            V = nc.vector
            dve.memset(eps[:], EPS).then_inc(s_set, 1)
            dve.memset(ones[:], 1.0).then_inc(s_set, 1)
            dve.wait_ge(s_set, 2)
            steps = [0]

            def ada(c):
                b, o = c % 2, ADA_ORD[c]
                dve.wait_ge(s_ada[b], 16 * (c // 2 + 1))
                if o >= 2:
                    dve.wait_ge(s_adamm, o - 1)
                which = 0 if c < ADA1 else 1
                for t in range(KD):
                    src, w = ada_stage[b][:, t, :], c_act[:, which, t:t + 1]
                    dst = ada_acc[o % 2][:, t % 2, :]
                    if t < 2:
                        i = V.tensor_scalar(dst, src, w, None, ALU.mult)
                    else:
                        dve.wait_ge(s_adastep, steps[0] - 1)
                        i = V.scalar_tensor_tensor(dst, src, w, dst, ALU.mult, ALU.add)
                    i.then_inc(s_adastep, 1)
                    steps[0] += 1
                dve.wait_ge(s_adastep, steps[0])
                V.tensor_tensor(ada_acc[o % 2][:, 0, :], ada_acc[o % 2][:, 0, :], ada_acc[o % 2][:, 1, :], ALU.add).then_inc(s_adaacc, 1)

            dve.wait_ge(s_cact, 1)
            for c in range(ADA_FIRST):
                if c not in ADA_PE:
                    ada(c)
            dve.wait_ge(s_vcol, 2)
            dve.wait_ge(s_adadir, len(ADA_PE))
            dve.wait_ge(s_adamm, ADA_FIRST - len(ADA_PE))
            nm = [0]

            def fold(gain, sc, slot):
                nm[0] += 1
                V.scalar_tensor_tensor(scale1[:, slot, :], mod[:, sc:sc + KD], 1.0,
                                       vcol[:, VROW[gain]:VROW[gain] + KD], ALU.add, ALU.mult).then_inc(s_mod, 1)

            V.tensor_tensor(mod[:, 0:16], bank[7][:, 0:16], vcol[:, 0:16], ALU.add).then_inc(s_mod, 1)
            dve.wait_ge(s_mod, 1)
            fold("g_attn", SC1, 0)
            dve.wait_ge(s_mod, 2)

            norms = [0]

            def rstd_ready():
                norms[0] += 1
                dve.wait_ge(s_sd, norms[0])
                V.reciprocal(rstd[:], rstd[:]).then_inc(s_rstd, 1)
                dve.wait_ge(s_rstd, norms[0])

            splits = [0]

            def normed(slot, shift):
                j = splits[0]
                splits[0] += 1
                for k in range(KD + 1):
                    if k < KD:
                        if k >= 2:
                            dve.wait_ge(s_alo, KD * j + k - 1)
                        V.scalar_tensor_tensor(tmp[k % 2][:], xT[:, k, :], scale1[:, slot, k:k + 1], rstd[:],
                                               ALU.mult, ALU.mult).then_inc(s_u, 1)
                    if k >= 1:
                        dve.wait_ge(s_ahi, KD * j + k)
                        V.scalar_tensor_tensor(act_lo[:, k - 1, :], tmp[(k - 1) % 2][:], modc(shift + k - 1),
                                               act_hi[:, k - 1, :].bitcast(F32), ALU.add, ALU.subtract).then_inc(s_alo, 1)

            rstd_ready()
            normed(0, SH1)

            pairs = list(enumerate(PAIRS))

            def scores_sum(count):
                for _ in range(count):
                    if not pairs:
                        return
                    s, (i, h) = pairs.pop(0)
                    n = P * (i + 1)
                    dve.wait_ge(s_relu, s + 1)
                    w = wi_sb[:, i, h:h + 1]
                    if h == 0:
                        V.tensor_scalar(score[i][:], relu[s % 2][:, 0:n], w, None, ALU.mult).then_inc(s_score, 1)
                    else:
                        dve.wait_ge(s_score, s)
                        V.scalar_tensor_tensor(score[i][:], relu[s % 2][:, 0:n], w, score[i][:], ALU.mult, ALU.add).then_inc(s_score, 1)

            c = ADA_FIRST
            for n in range(6):
                for _ in range(ADA_WINDOW.get(n, 0)):
                    ada(c)
                    c += 1
                if n == 1:
                    dve.wait_ge(s_free, 1)
                    for t in range(TT):
                        V.tensor_tensor_reduce(tmp[2][:, t * P:(t + 1) * P], ckv[:, t, :], ckv[:, t, :], 1.0, 0.0,
                                               ALU.mult, ALU.add, ckv_ss[:, 0, t:t + 1]).then_inc(s_ckv, 1)
                if n == 2:
                    dve.wait_ge(s_ckvsd, 1)
                    V.reciprocal(ckv_ss[:, 2, :], ckv_ss[:, 1, :]).then_inc(s_ckv, 1)
                    dve.wait_ge(s_ckv, TT + 1)
                    dve.wait_ge(s_const, 16 * NCONST)
                    for t in range(TT):
                        V.scalar_tensor_tensor(ckv[:, t, :], ckv[:, t, :], ckv_ss[:, 2, t:t + 1], kvg[:],
                                               ALU.mult, ALU.mult).then_inc(s_ckv, 1)
                if n >= 3:
                    scores_sum(2 * PAIRS_PER_TILE)
            assert not pairs
            dve.wait_ge(s_score, len(PAIRS))
            top = 0
            for i in range(1, TT):
                d = score[i][:, i * P:(i + 1) * P]
                V.tensor_tensor(d, d, causal[:, 1, :], ALU.min).then_inc(s_top, 1)
                top += 1
            for r in range(TOPK // 8):
                for i in range(1, TT):
                    dve.wait_ge(s_top, top - 2)
                    V.max(top8[i][:], (score if r == 0 else work)[i][:]).then_inc(s_top, 1)
                    top += 1
                for i in range(1, TT):
                    dve.wait_ge(s_top, top - 2)
                    V.match_replace(work[i][:], top8[i][:], (score if r == 0 else work)[i][:], -3.0e38).then_inc(s_top, 1)
                    top += 1
            for i in range(1, TT):
                dve.wait_ge(s_top, top - 2)
                V.tensor_tensor(work[i][:], work[i][:], score[i][:], ALU.is_equal).then_inc(s_top, 1)
                top += 1
            for i in range(1, TT):
                dve.wait_ge(s_top, top - 2)
                V.tensor_scalar(work[i][:], work[i][:], BIG, None, ALU.mult).then_inc(s_top, 1)
                top += 1
            assert top == TOP_STEPS
            dve.wait_ge(s_adamm, ADA_DVE)
            V.tensor_tensor(mod[:, 16:2 * ADA_LOOP], bank[7][:, 16:2 * ADA_LOOP], vcol[:, 16:2 * ADA_LOOP], ALU.add).then_inc(s_mod, 1)
            dve.wait_ge(s_mod, 3)
            fold("g_ffn", SC2, 1)

            O_BANK = (7, 1)
            n_items = len(ITEMS)

            def least(s):
                kind, h, i = ITEMS[s]
                n = P * (i + 1)
                dve.wait_ge(s_s, s + 1)
                if kind == "A":
                    dve.wait_ge(s_tab, h + 1)
                    t = table[h % 2][:, T - n:T]
                else:
                    u = s - NH * TT
                    dve.wait_ge(s_comb, u + 1)
                    t = comb[u % 2][:, 0:n]
                if s >= 2:
                    dve.wait_ge(s_exp, s - 1)
                V.tensor_tensor_reduce(tmp[s % 2][:, 0:n], bank[4 + s % 2][:, 0:n], t, 1.0, 3.0e38,
                                       ALU.add, ALU.min, negmax[:, s:s + 1]).then_inc(s_min, 1)

            def normalise(s):
                n = P * (ITEMS[s][2] + 1)
                dve.wait_ge(s_exp, s + 1)
                V.reciprocal(expinv[:, s:s + 1], expsum[:, s:s + 1]).then_inc(s_inv, 1)
                dve.wait_ge(s_inv, s + 1)
                V.tensor_scalar(probs[s % 4][:, 0:n], probs[s % 4][:, 0:n], expinv[:, s:s + 1], None,
                                ALU.mult).then_inc(s_norm, 1)

            def low(g, src, k):
                half = slice(HD * (g % 2), HD * (g % 2) + HD)
                dve.wait_ge(s_mhi, g + 1)
                V.tensor_tensor(act_lo[half, k, :], src[half, :], act_hi[half, k, :].bitcast(F32), ALU.subtract).then_inc(s_mlo, 1)

            for s in range(n_items + 9):
                if s < n_items:
                    least(s)
                if 1 <= s < n_items + 1:
                    normalise(s - 1)
                if 6 <= s < n_items + 6 and ITEMS[s - 6][2] == TT - 1 and ITEMS[s - 6][0] == "A":
                    h = ITEMS[s - 6][1]
                    low(h, bank[O_BANK[h % 2]], h // 2)
                if s >= 8 and s - 8 < n_items and ITEMS[s - 8][0] == "B" and ITEMS[s - 8][2] == TT - 1:
                    h = ITEMS[s - 8][1]
                    low(NH + h, bank[3], 4 + h // 2)
            dve.wait_ge(s_mod, 4)
            added = [0]

            def residual(n0, gain, groups=1):
                r0 = added[0]
                added[0] += KD
                for k in range(KD):
                    dve.wait_ge(*((s_wused, n0 + groups * (k // 2 + 1)) if k % 2 else (s_racc, (r0 + k) // 2 + 1)))
                    V.scalar_tensor_tensor(xT[:, k, :], bank[k % 4][:], gain(k), xT[:, k, :], ALU.mult, ALU.add).then_inc(s_res, 1)

            residual(C_OUT, lambda k: modc(GA1 + k))
            rstd_ready()
            dve.wait_ge(s_res, KD)
            normed(1, SH2)
            ada_steps = steps[0]
            dve.memset(lam_t[:, 7, 1:2], 0.0).then_inc(s_up, 2)
            dve.memset(lam_t[:, 7, 3:4], 0.0).then_inc(s_fflo, 2)
            with dve.Fori(0, KF // 2) as j:
                dve.wait_ge(s_adaloop, j * 16 + 16)
                dve.wait_ge(s_adamm, j + ADA_DVE)
                for t in range(KD):
                    src, w = ada2_stage[:, t, :], c_act[:, 1, t:t + 1]
                    if t == 0:
                        V.tensor_scalar(ada2_acc[:], src, w, None, ALU.mult).then_inc(s_adastep, 1)
                    else:
                        dve.wait_ge(s_adastep, j * (KD - 1) + (ada_steps + t))
                        V.scalar_tensor_tensor(ada2_acc[:], src, w, ada2_acc[:], ALU.mult, ALU.add).then_inc(
                            s_adaacc if t == KD - 1 else s_adastep, 1)
                for m in range(2):
                    dve.wait_ge(s_silu, j * 2 + (3 + m))
                    dve.wait_ge((s_guacc, s_wused)[m], j * 2 + (2, C_GU + 2)[m])
                    dve.wait_ge(s_fflo, j * 2 + (1 + m))
                    V.tensor_tensor(tmp[2 + m][:], bank[2 + m][:], tmp[m][:], ALU.mult).then_inc(s_up, 1)
                for m in range(2):
                    dve.wait_ge(s_up, j * 2 + (3 + m))
                    V.tensor_copy(ff_hi[:, bass.ds(j * 2 + m, 1), :], tmp[2 + m][:].rearrange("p (o t) -> p o t", o=1)).then_inc(s_ffhi, 1)
                for m in range(2):
                    dve.wait_ge(s_ffhi, j * 2 + (1 + m))
                    V.tensor_tensor(ff_lo[:, bass.ds(j * 2 + m, 1), :], tmp[2 + m][:].rearrange("p (o t) -> p o t", o=1),
                                    ff_hi[:, bass.ds(j * 2 + m, 1), :].bitcast(F32), ALU.subtract).then_inc(s_fflo, 1)
            dve.wait_ge(s_adamm, ADA_DVE + KF // 2)
            V.tensor_tensor(mod[:, 2 * ADA_LOOP:72], bank[5][:, 0:72 - 2 * ADA_LOOP], vcol[:, 2 * ADA_LOOP:72], ALU.add).then_inc(s_mod, 1)
            dve.wait_ge(s_mod, 5)
            fold("norm_g_2", SC3, 2)
            V.tensor_scalar(scale1[:, 3, :], mod[:, GA3:GA3 + KD], 1.0, None, ALU.add).then_inc(s_mod, 1)
            dve.wait_ge(s_mod, 7)
            residual(C_DOWN, lambda k: modc(GA2 + k), 3)
            rstd_ready()
            dve.wait_ge(s_res, 2 * KD)
            for k in range(KD):
                V.scalar_tensor_tensor(xT[:, k, :], xT[:, k, :], col("g_final", k), rstd[:], ALU.mult, ALU.mult).then_inc(s_xf, 1)
            dve.wait_ge(s_xf, KD)
            rstd_ready()
            normed(2, SH3)
            V.memset(v_pad[:, :, 0:PADV], 0.0).then_inc(s_v, 1)
            V.memset(l_pad[:, :, 0:PADL], 0.0).then_inc(s_v, 1)
            with dve.Fori(0, KD // 2) as j:
                for m in range(2):
                    dve.wait_ge(s_sig, j * 2 + (2 + m))
                    dve.wait_ge((s_i2acc, s_wused)[m], j * 2 + (2, C_IN2 + 2)[m])
                    V.tensor_tensor(v_pad[:, bass.ds(j * 2 + m, 1), PADV:PADV + T], bank[2 + m][:].rearrange("p (o t) -> p o t", o=1),
                                    tmp[m][:].rearrange("p (o t) -> p o t", o=1), ALU.mult).then_inc(s_v, 1)
            dve.wait_ge(s_v, 2 + KD)
            cs = [0]

            def conv_pair(k0):
                for tap in range(CONV):
                    for k in (k0, k0 + 1):
                        src = v_pad[:, k, tap:tap + T]
                        if tap == 0:
                            V.tensor_scalar(conv[:, k, :], src, col("dw_w_2", 8 * tap + k), col("dw_b_2", k), ALU.mult, ALU.add).then_inc(s_conv, 1)
                        else:
                            dve.wait_ge(s_conv, cs[0] - 1)
                            V.scalar_tensor_tensor(conv[:, k, :], src, col("dw_w_2", 8 * tap + k), conv[:, k, :], ALU.mult, ALU.add).then_inc(s_conv, 1)
                        cs[0] += 1

            for k0 in (0, 2, 4):
                conv_pair(k0)
            lam = vcol[:, VROW["lam_2"]:VROW["lam_2"] + KD]
            L = lambda r: lam_t[:, r, :]
            ls = [0]

            def link(i):
                ls[0] += 1
                i.then_inc(s_lam, 1)
                dve.wait_ge(s_lam, ls[0])

            dve.wait_ge(s_lama, 2)
            link(V.tensor_scalar(L(2), L(1), 1.0, None, ALU.add))
            link(V.tensor_scalar(L(0), L(2), -1.0, 1e-37, ALU.add, ALU.max))
            dve.wait_ge(s_lama, 3)
            link(V.reciprocal(L(6), L(0)))
            link(V.tensor_tensor(L(6), L(6), L(1), ALU.mult))
            link(V.tensor_tensor(L(6), L(6), L(3), ALU.mult))
            link(V.tensor_scalar(L(5), L(0), 1e-30, None, ALU.is_lt))
            link(V.tensor_tensor(L(5), L(5), L(1), ALU.mult))
            link(V.tensor_tensor(L(6), L(6), L(5), ALU.add))
            link(V.tensor_scalar(L(7), lam, -1.0, 0.0, ALU.mult, ALU.max))
            link(V.tensor_tensor(L(6), L(6), L(7), ALU.add))
            link(V.tensor_scalar(L(5), L(6), 8.0, None, ALU.mult))
            link(V.tensor_scalar(L(4), L(6), -8.0, None, ALU.mult))
            assert ls[0] == LAM_STEPS

            dve.wait_ge(s_gate, 4 + KD)
            dve.wait_ge(s_gate, 4 + 3 * KD)
            x_steps = 0
            for k in range(KD + 1):
                if k < KD:
                    for tap in range(SHORT):
                        src = l_pad[:, k, tap:tap + T]
                        if tap == 0:
                            if k >= 2:
                                dve.wait_ge(s_gmm, 2 * (k - 1))
                                dve.wait_ge(s_gx, k - 1)
                            i = V.tensor_scalar(tmp[k % 2][:], src, col("sc_w_2", k), col("sc_b_2", k), ALU.mult, ALU.add)
                        else:
                            dve.wait_ge(s_xs, x_steps)
                            i = V.scalar_tensor_tensor(tmp[k % 2][:], src, col("sc_w_2", 8 * tap + k), tmp[k % 2][:], ALU.mult, ALU.add)
                        i.then_inc(s_xs, 1)
                        x_steps += 1
                if k >= 1:
                    dve.wait_ge(s_i, k)
                    dve.wait_ge(s_xs, SHORT * k)
                    V.tensor_tensor(gated[:, k - 1, :], tmp[2 + (k - 1) % 2][:], tmp[(k - 1) % 2][:], ALU.mult).then_inc(s_gx, 1)
            dve.wait_ge(s_gx, KD)
            for k in range(KD):
                t = l_pad[:, k, 0:T]
                u = tmp[2 + k % 2][:]
                dve.wait_ge(s_a, 2 * k + 2)
                V.tensor_scalar(u, t, 1.0, None, ALU.add).then_inc(s_m, 1)
                dve.wait_ge(s_m, 3 * k + 1)
                V.reciprocal(u, u).then_inc(s_m, 1)
                dve.wait_ge(s_m, 3 * k + 2)
                V.tensor_tensor(t, t, u, ALU.mult).then_inc(s_m, 1)
            for k in range(KD):
                t = l_pad[:, k, 0:T]
                u = tmp[2 + k % 2][:]
                dve.wait_ge(s_mt, k + 1)
                V.tensor_tensor(gated[:, k, :], gated[:, k, :], t, ALU.mult).then_inc(s_scan, 1)
                dve.wait_ge(s_scan, 3 * k + 1)
                V.tensor_tensor_scan(t, decay[:, k, :], gated[:, k, :], 0.0, ALU.mult, ALU.add).then_inc(s_scan, 1)
                dve.wait_ge(s_scan, 3 * k + 2)
                V.tensor_tensor(u, t, lgate[:, k, :], ALU.mult).then_inc(s_scan, 1)
                dve.wait_ge(s_scan, 3 * k + 3)
                V.tensor_copy(act_hi[:, k, :], u).then_inc(s_lhi, 1)
                dve.wait_ge(s_lhi, k + 1)
                V.tensor_tensor(act_lo[:, k, :], u, act_hi[:, k, :].bitcast(F32), ALU.subtract).then_inc(s_llo, 1)
            dve.wait_ge(s_llo, KD)
            conv_pair(6)
            residual(C_LRU, lambda k: scale1[:, 3, k:k + 1])
            dve.wait_ge(s_mu, 1)
            for k in range(KD):
                V.tensor_tensor(conv[:, k, :], conv[:, k, :], tmp[2][:], ALU.subtract).then_inc(s_cen, 1)
            dve.wait_ge(s_cen, KD)
            rstd_ready()
            for k in range(KD + 1):
                if k < KD:
                    if k >= 2:
                        dve.wait_ge(s_lns, k - 1)
                    V.scalar_tensor_tensor(tmp[k % 2][:], conv[:, k, :], col("cln_g_2", k), rstd[:], ALU.mult, ALU.mult).then_inc(s_lnu, 1)
                if k >= 1:
                    dve.wait_ge(s_lns, k)
                    V.tensor_copy(ln_hi[:, k - 1, :], tmp[2 + (k - 1) % 2][:]).then_inc(s_lnhi, 1)
                    dve.wait_ge(s_lnhi, k)
                    V.tensor_tensor(ln_lo[:, k - 1, :], tmp[2 + (k - 1) % 2][:], ln_hi[:, k - 1, :].bitcast(F32), ALU.subtract).then_inc(s_lnlo, 1)
            V.memset(lam_t[:, 7, 2:3], 0.0).then_inc(s_yc, 4)
            for k in range(KD):
                dve.wait_ge(*((s_wused, C_PW2 + k // 2 + 1) if k % 2 else (s_pacc, k // 2 + 1)))
                if k >= 2:
                    dve.wait_ge(s_yclo, k - 1)
                V.scalar_tensor_tensor(tmp[k % 2][:], bank[k % 4][:], col("pw2_b_2", k), cgate[:, k, :], ALU.add, ALU.mult).then_inc(s_yc, 1)
                dve.wait_ge(s_yc, 4 + k + 1)
                V.tensor_copy(yc_hi[:, k, :], tmp[k % 2][:]).then_inc(s_ychi, 1)
                dve.wait_ge(s_ychi, k + 1)
                V.tensor_tensor(yc_lo[:, k, :], tmp[k % 2][:], yc_hi[:, k, :].bitcast(F32), ALU.subtract).then_inc(s_yclo, 1)
            residual(C_OUT2, lambda k: scale1[:, 3, k:k + 1])
            rstd_ready()
            dve.wait_ge(s_res, 4 * KD)
            for k in range(KD):
                V.scalar_tensor_tensor(xT[:, k, :], xT[:, k, :], col("final_g_2", k), rstd[:], ALU.mult, ALU.mult).then_inc(s_xf, 1)


VROWS = (128, 80, 128, 120)
NCONST = 4
CKV_STEPS = 2 * TT + 1
TOP_STEPS = 3 + (TOPK // 8) * 6 + 6
LAM_STEPS = 12
N_IN_TILES = 22


_INS = ["x", "c", "w_ada", "b_ada", "g_attn", "w_in", "kv_norm_g", "w_uk", "w_uv", "w_out", "g_ffn", "w_gu",
        "w_down", "g_final", "c_2", "norm_g_2", "mod_w_2", "mod_b_2", "w_in_2", "dw_w_2", "dw_b_2", "cln_g_2",
        "cln_b_2", "pw2_w_2", "pw2_b_2", "sc_w_2", "sc_b_2", "wr_2", "br_2", "wi_2", "bi_2", "lam_2", "w_out_2",
        "final_g_2"]
_OUT = (1, T, D)


def kernel(**inputs):
    import numpy as np
    import concourse.bacc as bacc
    from concourse.bass_utils import run_bass_kernel_spmd

    nc = bacc.Bacc("TRN2", target_bir_lowering=False, num_devices=1)
    p, x = np.arange(P)[:, None], np.arange(T)[None, :]
    d = p + (T - P) - x
    held = ((d >= 0) & (d <= 128)).astype(int) + ((d >= 0) & (d % 4 == 0)) + ((d >= 0) & (d % 16 == 0))
    key = np.arange(P)[None, :]
    tables = {
        "dist": d.astype(np.float32),
        "maskA": np.where(held > 0, -np.log(np.maximum(held, 1)), BIG).astype(np.float32),
        "causal": np.stack([np.where(key > p, BIG, 0.0), np.where(key > p, -3.0e38, 3.0e38)], 1).astype(np.float32),
        "ident": np.eye(P, dtype=np.float32),
    }
    arrays, aps = {}, {}
    for name in _INS:
        v = np.ascontiguousarray(inputs[name])
        if v.ndim >= 3:
            v = v.reshape(v.shape[1:])
        elif name not in ("c", "c_2", "kv_norm_g"):
            v = v.reshape(-1)
        if name == "dw_w_2" or name == "sc_w_2":
            v = v.reshape(-1)
        tables[name] = v
    for name, v in tables.items():
        arrays[f"in_{name}"] = v
        aps[name] = nc.dram_tensor(f"in_{name}", v.shape, F32, kind="ExternalInput").ap()
    out = nc.dram_tensor("out_0", (T, D), F32, kind="ExternalOutput").ap()
    build(nc, aps, out)
    r = run_bass_kernel_spmd(nc, [arrays], core_ids=[0])
    return r.results[0]["out_0"].reshape(_OUT)
```

```python
from contextlib import ExitStack

import concourse.bass as bass
from concourse import mybir

F32 = mybir.dt.float32
F32R = mybir.dt.float32r
ALU = mybir.AluOpType
ACT = mybir.ActivationFunctionType

P = 128
T = 512
TT = T // P
D = 1024
KD = D // P
D_FF = 2816
KF = D_FF // P
HD = 64
NH = 8
TOPK = 128
EPS = 1e-6
BIG = 1.0e30
NCOL = 256
CONV = 31
SHORT = 4
PADV, PADL = CONV - 1, SHORT - 1
QSCALE = -(HD ** -0.5)
IDX_SCALE = (8 * 64) ** -0.5

W_IN_COLS = [2048, 2304, 2560, 1536, 1792, 0, 256, 512, 768, 1024, 1280]
N_IN = len(W_IN_COLS)
C_OUT = N_IN
C_GU = C_OUT + 4
C_DOWN = C_GU + 2 * (D_FF // NCOL)
C_IN2 = C_DOWN + 12
C_LRU = C_IN2 + 20
C_PW2 = C_LRU + 4
C_OUT2 = C_PW2 + 4
C_END = C_OUT2 + 4

ADA1, ADA2 = 24, 12
ADA_FIRST = 8
ADA_WINDOW = {0: 3, 1: 3, 2: 3, 3: 3, 4: 3, 5: 2}
ADA_LOOP = ADA_FIRST + sum(ADA_WINDOW.values())

ITEMS = [(kind, h, i) for kind in "AB" for h in range(NH) for i in range(TT)]
PAIRS = [(i, h) for i in range(1, TT) for h in range(NH)]
PAIRS_PER_TILE = 4

ADA_PE = list(range(0, ADA_FIRST, 2))
ADA_ORD = {c: n for n, c in enumerate(c for c in range(ADA1 + ADA2) if c not in ADA_PE)}
ADA_DVE = ADA_ORD[ADA_LOOP]

LRU_SLOT = 10
MEAN_AFTER, VAR_AFTER = 1, 3
LN_CHUNKS = (3,)
RES_AT = (3, 5, 7)
TAPS_V, TAPS_LX, TAPS_BEFORE = 31, 16, 26
TAPS_A, TAPS_B = (10, 10, 10, 10), (10, 10, 10, 18)

VECS = [("b_ada", 48), ("mod_b_2", 24), ("g_attn", 8), ("g_ffn", 8), ("g_final", 8), ("norm_g_2", 8),
        ("final_g_2", 8), ("cln_g_2", 8), ("cln_b_2", 8), ("pw2_b_2", 8), ("sc_b_2", 8), ("dw_b_2", 8),
        ("br_2", 8), ("bi_2", 8), ("lam_2", 8), ("sc_w_2", 32), ("pad", 48), ("dw_w_2", 248)]
VROW = {}
_at = 0
for _name, _n in VECS:
    VROW[_name] = _at
    _at += _n
NVEC_DMAS = len(VECS) - 1 + 1


def build(nc, a, out):
    with ExitStack() as ctx:
        offset = [nc.sbuf_base + (-nc.sbuf_base) % 64]

        def fixed(name, shape, dt=F32, at=None):
            n = 4
            for s in shape[1:]:
                n *= s
            if at is None:
                at = offset[0]
                offset[0] += (n + 63) // 64 * 64
                assert offset[0] <= nc.sbuf_usable_end, (name, offset[0])
            return nc.alloc_sbuf_tensor_at(name, shape, dt, offset=at), at

        def sem(name):
            return ctx.enter_context(nc.semaphore(name))

        xT, _ = fixed("xT", [P, KD, T])
        act_hi, at_hi = fixed("act_hi", [P, KD, T], F32R)
        act_lo, at_lo = fixed("act_lo", [P, KD, T], F32R)
        w_stage = [fixed(f"w_stage{b}", [P, KD, NCOL])[0] for b in range(2)]
        w_hi = [fixed(f"w_hi{b}", [P, KD, NCOL], F32R)[0] for b in range(2)]
        w_lo = [fixed(f"w_lo{b}", [P, KD, NCOL], F32R)[0] for b in range(2)]
        tmp = [fixed(f"tmp{b}", [P, T])[0] for b in range(4)]
        rstd, _ = fixed("rstd", [P, T])
        ident, _ = fixed("ident_sb", [P, P])
        ones, _ = fixed("ones", [P, P])
        vcol, _ = fixed("vcol", [P, 512])
        mod, _ = fixed("mod", [P, 72])
        scale1, _ = fixed("scale1", [P, 4, KD])
        c_sb, _ = fixed("c_sb", [P, 2, KD])
        c_act, _ = fixed("c_act", [P, 2, KD])
        eps, _ = fixed("eps", [P, 1])
        lam_t, _ = fixed("lam_t", [P, 8, KD])
        wi_sb, _ = fixed("wi_sb", [P, TT, 8])
        negmax, _ = fixed("negmax", [P, 64])
        expsum, _ = fixed("expsum", [P, 64])
        expinv, at_expinv = fixed("expinv", [P, 64])
        nothing, _ = fixed("nothing", [P, 8], at=at_expinv)
        ckv_ss, _ = fixed("ckv_ss", [P, 3, TT])
        region = offset[0]

        dist, _ = fixed("dist_sb", [P, T])
        maskA, _ = fixed("maskA_sb", [P, T])
        causal, _ = fixed("causal_sb", [P, 2, P])
        ada_stage = [fixed(f"ada_stage{b}", [P, KD, NCOL])[0] for b in range(2)]
        ada_acc = [fixed(f"ada_acc{b}", [P, 2, NCOL])[0] for b in range(2)]
        qaT, at_qa = fixed("qaT", [P, 4, T])
        kaT, at_ka = fixed("kaT", [P, 4, T])
        va, _ = fixed("va", [P, TT, T])
        qbT, _ = fixed("qbT", [P, 4, T])
        x_nat, _ = fixed("x_nat", [P, TT, D], at=at_qa)
        at_score = offset[0]
        score = [None] + [fixed(f"score{i}", [P, P * (i + 1)])[0] for i in range(1, TT)]
        work = [None] + [fixed(f"work{i}", [P, P * (i + 1)])[0] for i in range(1, TT)]
        probs = tmp[2:4] + [fixed(f"probs{b}", [P, T], at=at_score + 2048 * b)[0] for b in range(2)]
        top8 = [None] + [fixed(f"top8_{i}", [P, 8])[0] for i in range(1, TT)]
        qiT, at_qi = fixed("qiT", [P, 4, T])
        qlatT = [fixed(f"qlatT{b}", [P, T], at=at_qi + 2048 * b)[0] for b in range(2)]
        olat = [fixed(f"olat{b}", [P, T], at=at_qi + 2048 * (2 + b))[0] for b in range(2)]
        kiT, at_ki = fixed("kiT", [P, T])
        ckv, at_ckv = fixed("ckv", [P, TT, P])
        ckvT, _ = fixed("ckvT", [P, T])
        wuk, _ = fixed("wuk", [P, 4, P])
        wuv, at_wuv = fixed("wuv", [P, NH, HD])
        probsT = [fixed(f"probsT{b}", [P, TT, P])[0] for b in range(2)]
        probsT.append(fixed("probsT2", [P, TT, P], at=at_ki)[0])
        comb, at_comb = zip(*[fixed(f"comb{b}", [P, T]) for b in range(2)])
        relu = [fixed(f"relu{b}", [P, T], at=at_comb[b])[0] for b in range(2)]
        table = [fixed(f"table{b}", [P, T])[0] for b in range(2)]
        kvg, _ = fixed("kvg", [P, P])
        wiT, _ = fixed("wiT", [P, T], at=at_comb[0])
        vrow, _ = fixed("vrow", [P, 4, P], at=at_wuv)
        first_end = offset[0]

        offset[0] = region
        ff_hi, _ = fixed("ff_hi", [P, KF, T], F32R)
        ff_lo, _ = fixed("ff_lo", [P, KF, T], F32R)
        ada2_stage, _ = fixed("ada2_stage", [P, KD, NCOL])
        ada2_acc, _ = fixed("ada2_acc", [P, NCOL])

        offset[0] = region
        v_pad, at_v = fixed("v_pad", [P, KD, PADV + T])
        l_pad, at_l = fixed("l_pad", [P, KD, PADL + 1 + T])
        conv, at_conv = fixed("conv", [P, KD, T])
        lgate, at_lgate = fixed("lgate", [P, KD, T])
        cgate, _ = fixed("cgate", [P, KD, T])
        wr, _ = fixed("wr_sb", [P, 8, P])
        wi, _ = fixed("wi2_sb", [P, 8, P])
        decay = [fixed(f"decay{m}", [P, T])[0] for m in range(2)]
        hidden = [fixed("hidden0", [P, T])[0], rstd]
        lru_hi, _ = fixed("lru_hi", [P, KD, T], F32R, at=at_lgate)
        lru_lo, _ = fixed("lru_lo", [P, KD, PADL + 1 + T], F32R, at=at_l)
        ln_hi, _ = fixed("ln_hi", [P, KD, T], F32R, at=at_v)
        ln_lo, _ = fixed("ln_lo", [P, KD, T], F32R, at=at_conv)
        o_nat, _ = fixed("o_nat", [P, TT, D], at=at_v)

        bank = [ctx.enter_context(nc.psum_tensor(f"bank{b}", [P, 512], F32)) for b in range(8)]

        def col(name, j):
            c = VROW[name] + j
            return vcol[:, c:c + 1]

        def modc(j):
            return mod[:, j:j + 1]

        SH1, SC1, GA1, SH2, SC2, GA2, SH3, SC3, GA3 = (KD * j for j in range(9))

        s_c = sem("c_loaded")
        s_ident = sem("ident_loaded")
        s_const = sem("constants_loaded")
        s_vec = sem("vector_rows_loaded")
        s_x = sem("x_loaded")
        s_late = sem("head_weights_loaded")
        s_lruw = sem("lru_weights_loaded")
        s_stage = [sem(f"w_stage_loaded{b}") for b in range(2)]
        s_hi = sem("w_hi_ready")
        s_lo = sem("w_lo_ready")
        s_wused = sem("w_used")
        s_ada = [sem(f"ada_loaded{b}") for b in range(2)]
        s_adadir = sem("ada_chunk_by_pe")
        s_adaloop = sem("ada_loop_loaded")
        s_adastep = sem("ada_step")
        s_adaacc = sem("ada_acc_ready")
        s_adamm = sem("ada_acc_used")
        s_mod = sem("mod_ready")
        s_set = sem("dve_set")
        s_cact = sem("c_act_ready")
        s_vt = sem("vectors_turned")
        s_vcol = sem("vcol_ready")
        s_xt = sem("x_turned")
        s_xTr = sem("xT_ready")
        s_sq = sem("squares_ready")
        s_sqused = sem("squares_used")
        s_ss = sem("sum_of_squares")
        s_sd = sem("deviation_ready")
        s_rstd = sem("rstd_ready")
        s_u = sem("scaled_ready")
        s_ahi = sem("act_hi_ready")
        s_alo = sem("act_lo_ready")
        s_acc = sem("in_acc_ready")
        s_free = sem("in_acc_free")
        s_ckv = sem("ckv_steps")
        s_ckvsd = sem("ckv_deviation")
        s_ckvt = sem("ckv_turned")
        s_ckvT = sem("ckvT_ready")
        s_wiT = sem("indexer_weights_turned")
        s_wi = sem("indexer_weights_ready")
        s_lg = sem("logits_ready")
        s_relu = sem("relu_ready")
        s_score = sem("score_added")
        s_top = sem("topk_step")
        s_tab = sem("table_ready")
        s_tabm = sem("table_made")
        s_comb = sem("comb_ready")
        s_s = sem("scores_ready")
        s_min = sem("min_ready")
        s_exp = sem("exp_ready")
        s_inv = sem("expinv_ready")
        s_norm = sem("probs_ready")
        s_t = sem("probs_turned")
        s_pt = sem("probsT_ready")
        s_pv = sem("pv_done")
        s_ql = sem("qlat_ready")
        s_qlT = sem("qlatT_copied")
        s_oh = sem("olat_copied")
        s_uv = sem("uv_done")
        s_mhi = sem("mixed_hi_ready")
        s_mlo = sem("mixed_lo_ready")
        s_racc = sem("residual_acc_ready")
        s_res = sem("residual_added")
        s_guacc = sem("gu_acc_ready")
        s_silu = sem("silu_ready")
        s_up = sem("up_ready")
        s_ffhi = sem("ff_hi_ready")
        s_fflo = sem("ff_lo_ready")
        s_xf = sem("x_normed")
        s_i2acc = sem("in2_acc_ready")
        s_sig = sem("sigmoid_ready")
        s_v = sem("v_ready")
        s_gate = sem("gates_copied")
        s_conv = sem("conv_step")
        s_xs = sem("short_conv_step")
        s_gmm = sem("lru_gate_products")
        s_r = sem("r_ready")
        s_i = sem("i_ready")
        s_gx = sem("gated_ready")
        s_a = sem("decay_ready")
        s_th = sem("tanh_ready")
        s_aa = sem("decay_squared")
        s_m = sem("mult_squared")
        s_bx = sem("scan_input_ready")
        s_y = sem("y_lru_ready")
        s_mt = sem("mult_ready")
        s_scan = sem("scan_done")
        s_lhi = sem("lru_hi_ready")
        s_llo = sem("lru_lo_ready")
        s_mean = sem("mean_sum")
        s_mu = sem("mean_ready")
        s_cen = sem("centred")
        s_lnu = sem("ln_scaled")
        s_lns = sem("ln_silu")
        s_lnhi = sem("ln_hi_ready")
        s_lnlo = sem("ln_lo_ready")
        s_pacc = sem("pw2_acc_ready")
        s_yc = sem("y_conv_ready")
        s_ychi = sem("yc_hi_ready")
        s_yclo = sem("yc_lo_ready")
        s_lam = sem("lam_step")
        s_lama = sem("lam_act")
        s_ot = sem("out_turned")
        s_on = sem("out_copied")
        s_out = sem("out_stored")

        block = ctx.enter_context(nc.Block())

        def w_cols(w, k0, kn, c0):
            return w.rearrange("(k p) c -> p k c", p=P)[:, k0:k0 + kn, bass.ds(c0, NCOL)]

        @block.sync
        def _(sp):
            def w_dma(n, src, half=None):
                b = n % 2 if half is None else half[0]
                if half is None:
                    if n >= 2:
                        sp.wait_ge(s_lo, n - 1)
                else:
                    sp.wait_ge(s_lo, n - 1)
                kn, cn = src.shape[1], src.shape[2]
                sp.dma_start(w_stage[b][:, 0:kn, 0:cn], src).then_inc(s_stage[b], 16)

            def ada_dma(c):
                if c >= 2:
                    if c - 2 in ADA_PE:
                        sp.wait_ge(s_adadir, ADA_PE.index(c - 2) + 1)
                    else:
                        sp.wait_ge(s_adaacc, ADA_ORD[c - 2] + 1)
                w, j = (a["w_ada"], c) if c < ADA1 else (a["mod_w_2"], c - ADA1)
                src = w.rearrange("(p t) c -> p t c", t=KD)[:, :, j * NCOL:(j + 1) * NCOL]
                sp.dma_start(ada_stage[c % 2][:], src).then_inc(s_ada[c % 2], 16)

            sp.dma_start(c_sb[:, 0, :], a["c"].rearrange("o (p t) -> (o p) t", t=KD)).then_inc(s_c, 16)
            sp.dma_start(c_sb[:, 1, :], a["c_2"].rearrange("o (p t) -> (o p) t", t=KD)).then_inc(s_c, 16)
            ada_dma(0)
            ada_dma(1)
            sp.dma_start(ident[:], a["ident"]).then_inc(s_ident, 16)
            for t in range(TT):
                sp.dma_start(x_nat[:, t, :], a["x"][t * P:(t + 1) * P, :]).then_inc(s_x, 16)
            nvec = 0
            for name, n in VECS:
                if name == "pad":
                    continue
                src = a[name].rearrange("(r c) -> r c", c=P)
                r0, done = VROW[name], 0
                while done < n:
                    tile, row = divmod(r0 + done, P)
                    m = min(n - done, P - row)
                    sp.dma_start(vrow[row:row + m, tile, :], src[done:done + m, :]).then_inc(s_vec, 16)
                    nvec += 1
                    done += m
            assert nvec == NVEC_DMAS, nvec
            sp.dma_start(dist[:], a["dist"]).then_inc(s_const, 16)
            sp.dma_start(maskA[:], a["maskA"]).then_inc(s_const, 16)
            sp.dma_start(causal[:], a["causal"]).then_inc(s_const, 16)
            sp.dma_start(kvg[:], a["kv_norm_g"].to_broadcast([P, P])).then_inc(s_const, 16)
            for c in range(2, ADA_FIRST):
                ada_dma(c)

            def w_in_dma(n):
                c0 = W_IN_COLS[n]
                cn = min(NCOL, a["w_in"].shape[1] - c0)
                w_dma(n, a["w_in"].rearrange("(k p) c -> p k c", p=P)[:, :, c0:c0 + cn])

            w_in_dma(0)
            w_in_dma(1)
            c = ADA_FIRST
            for n in range(N_IN):
                for _ in range(ADA_WINDOW.get(n, 0)):
                    ada_dma(c)
                    c += 1
                if n == 5:
                    sp.wait_ge(s_vt, 1)
                    sp.dma_start(wuk[:], a["w_uk"].rearrange("(g e) d r -> (e d) g r", e=2)).then_inc(s_late, 16)
                    sp.dma_start(wuv[:], a["w_uv"].rearrange("h r d -> r h d")).then_inc(s_late, 16)
                if n + 2 < N_IN:
                    w_in_dma(n + 2)
            w_dma(C_OUT, w_cols(a["w_out"], 0, KD, 0))
            w_dma(C_OUT + 1, w_cols(a["w_out"], 0, KD, NCOL))
            w_dma(C_OUT + 2, w_cols(a["w_out"], 0, KD, 2 * NCOL))
            w_dma(C_OUT + 3, w_cols(a["w_out"], 0, KD, 3 * NCOL))

            def stream(n0, steps, srcs, first=0):
                per = len(srcs)
                with sp.Fori(first, first + steps) as j:
                    for q, src in enumerate(srcs):
                        w_dma(j * per + (n0 + q - first * per), src(j), half=((n0 + q) % 2,))

            sp.wait_ge(s_res, 1)
            with sp.Fori(2, KF // 2 + 2) as j:
                w_dma(j * 2 + (C_GU - 4), w_cols(a["w_gu"], 0, KD, j * NCOL - 2 * NCOL), half=(C_GU % 2,))
                w_dma(j * 2 + (C_GU - 3), w_cols(a["w_gu"], 0, KD, j * NCOL + (D_FF - 2 * NCOL)), half=((C_GU + 1) % 2,))
                sp.wait_ge(s_adaacc, j + (ADA_DVE - 2))
                sp.dma_start(ada2_stage[:], a["mod_w_2"].rearrange("(p t) c -> p t c", t=KD)[
                    :, :, bass.ds(j * NCOL + (ADA_LOOP - ADA1 - 2) * NCOL, NCOL)]).then_inc(s_adaloop, 16)
            groups = [(0, 8), (8, 8), (16, 6)]
            stream(C_DOWN, 2, [lambda j, m=m, g=g: w_cols(a["w_down"], g[0], g[1], j * 2 * NCOL + m * NCOL)
                               for m in range(2) for g in groups])
            stream(C_IN2, 4, [lambda j: w_cols(a["w_in_2"], 0, KD, j * NCOL + (D - NCOL)),
                              lambda j: w_cols(a["w_in_2"], 0, KD, j * NCOL - NCOL)], first=1)
            for g in range(2):
                if g == 0:
                    sp.wait_ge(s_res, 2 * KD)
                sp.dma_start((wr, wi)[g][:], a[("wr_2", "wi_2")[g]].rearrange("h d e -> d h e")).then_inc(s_lruw, 16)
            for part in (3, 4, 2):
                n0 = C_IN2 + 8 + 4 * (3, 4, 2).index(part)
                stream(n0, 2, [lambda j, q=q, part=part: w_cols(a["w_in_2"], 0, KD, j * 2 * NCOL + part * D + q * NCOL)
                               for q in range(2)])
            stream(C_LRU, 2, [lambda j, q=q: w_cols(a["w_out_2"], KD, KD, j * 2 * NCOL + q * NCOL) for q in range(2)])
            stream(C_PW2, 2, [lambda j, q=q: w_cols(a["pw2_w_2"], 0, KD, j * 2 * NCOL + q * NCOL) for q in range(2)])
            stream(C_OUT2, 2, [lambda j, q=q: w_cols(a["w_out_2"], 0, KD, j * 2 * NCOL + q * NCOL) for q in range(2)])

            for t in range(TT):
                sp.wait_ge(s_on, 2 * (t + 1))
                sp.dma_start(out[t * P:(t + 1) * P, :], o_nat[:, t, :]).then_inc(s_out, 16)
            sp.wait_ge(s_out, 16 * TT)

        @block.gpsimd
        def _(pool):
            def lo(n, b):
                pool.wait_ge(s_hi, n + 1)
                nc.gpsimd.tensor_tensor(w_lo[b][:], w_stage[b][:], w_hi[b][:].bitcast(F32),
                                        ALU.subtract).then_inc(s_lo, 1)


            slopes = [2.0 ** (-8.0 * (g + 1.0) / 16) for g in range(16)]

            def make_table(g):
                kind, h = g // NH, g % NH
                if g >= 2:
                    if g - 2 < NH:
                        pool.wait_ge(s_min, TT * (g - 1))
                    else:
                        pool.wait_ge(s_comb, TT * (g - 2 - NH + 1))
                m = nc.gpsimd.tensor_scalar(table[g % 2][:], dist[:], float(slopes[2 * h + kind]), 0.0, ALU.mult, ALU.add)
                if kind == 0:
                    m.then_inc(s_tabm, 1)
                    pool.wait_ge(s_tabm, h + 1)
                    m = nc.gpsimd.tensor_tensor(table[g % 2][:], table[g % 2][:], maskA[:], ALU.add)
                m.then_inc(s_tab, 1)

            for n in range(C_OUT + 2):
                lo(n, n % 2)
                if n == 5:
                    pool.wait_ge(s_const, 16 * NCONST)
                    make_table(0)
                    make_table(1)
            for g in range(2, NH):
                make_table(g)
            for h in range(NH):
                make_table(NH + h)
                pool.wait_ge(s_tab, NH + h + 1)
                for i in range(TT):
                    s, n = TT * h + i, P * (i + 1)
                    if s == 0:
                        pool.wait_ge(s_top, TOP_STEPS)
                    if s >= 2:
                        pool.wait_ge(s_min, TT * NH + s - 1)
                    t = table[h % 2][:, T - n:T]
                    if i == 0:
                        nc.gpsimd.tensor_tensor(comb[s % 2][:, 0:n], t, causal[:, 0, :], ALU.add).then_inc(s_comb, 1)
                    else:
                        nc.gpsimd.tensor_tensor(comb[s % 2][:, 0:n], t, work[i][:], ALU.add).then_inc(s_comb, 1)
            lo(C_OUT + 2, (C_OUT + 2) % 2)
            lo(C_OUT + 3, (C_OUT + 3) % 2)

            def lo_loop(n0, n1):
                with pool.Fori(0, (n1 - n0) // 2) as j:
                    for q in range(2):
                        lo(j * 2 + (n0 + q), (n0 + q) % 2)
                if (n1 - n0) % 2:
                    lo(n1 - 1, (n1 - 1) % 2)

            first_y = C_IN2 + LRU_SLOT + 4
            lo_loop(C_GU, first_y)
            for p in range(KD // 2):
                n = first_y + 2 * p
                for k in (2 * p, 2 * p + 1):
                    pool.wait_ge(s_scan, k + 1)
                    pool.wait_ge(s_gate, KD + k + 1)
                    nc.gpsimd.tensor_tensor(hidden[k % 2][:], hidden[k % 2][:], lgate[:, k, :], ALU.mult).then_inc(s_y, 1)
                lo(n, n % 2)
                for k in (2 * p, 2 * p + 1):
                    pool.wait_ge(s_lhi, k + 1)
                    nc.gpsimd.tensor_tensor(lru_lo[:, k, 0:T], hidden[k % 2][:], lru_hi[:, k, :].bitcast(F32),
                                            ALU.subtract).then_inc(s_llo, 1)
                if p < KD // 2 - 1:
                    lo(n + 1, (n + 1) % 2)
            lo_loop(first_y + KD - 1, C_END)

        @block.tensor
        def _(pe):
            def chunk_ready(n):
                pe.wait_ge(s_lo, n + 1)

            def normed_parts(j, k):
                pe.wait_ge(s_alo, KD * j + k + 1)

            def tile(dst, b, cols, n_k, rhs_hi, rhs_lo, first=True, last=True, wait=None):
                for k in range(n_k):
                    if wait:
                        wait(k)
                    wh, wl = w_hi[b][:, k, cols], w_lo[b][:, k, cols]
                    pe.matmul(dst, wh, rhs_hi(k), start=(first and k == 0), stop=False)
                    pe.matmul(dst, wh, rhs_lo(k), start=False, stop=False)
                    mm = pe.matmul(dst, wl, rhs_hi(k), start=False, stop=(last and k == n_k - 1))
                return mm

            def tile_tokens(dst, b, cols, t, wait=None):
                ts = slice(t * P, (t + 1) * P)
                for k in range(KD):
                    if wait:
                        wait(k)
                    ah, al = act_hi[:, k, ts], act_lo[:, k, ts]
                    pe.matmul(dst, ah, w_hi[b][:, k, cols], start=(k == 0), stop=False)
                    pe.matmul(dst, ah, w_lo[b][:, k, cols], start=False, stop=False)
                    mm = pe.matmul(dst, al, w_hi[b][:, k, cols], start=False, stop=(k == KD - 1))
                return mm

            pe.wait_ge(s_set, 2)
            pe.wait_ge(s_ident, 16)
            pe.wait_ge(s_vec, 16 * NVEC_DMAS)
            for q, rows in enumerate(VROWS):
                mm = pe.transpose(bank[4][:, q * P:q * P + rows], vrow[0:rows, q, :], ident[0:rows, 0:rows])
            mm.then_inc(s_vt, 1)
            pe.wait_ge(s_x, 16 * TT)
            for k in range(KD):
                if k >= 4:
                    pe.wait_ge(s_xTr, k - 3)
                for t in range(TT):
                    mm = pe.transpose(bank[k % 4][:, t * P:(t + 1) * P], x_nat[:, t, k * P:(k + 1) * P], ident[:])
                mm.then_inc(s_xt, 1)

            norms = [0]

            def sum_squares(total=s_ss):
                j = norms[0]
                norms[0] += 1
                for k in range(KD):
                    pe.wait_ge(s_sq, KD * j + k + 1)
                    mm = pe.matmul(bank[4][:], ones[:], tmp[k % 2][:], start=(k == 0), stop=(k == KD - 1))
                    mm.then_inc(s_sqused, 1)

            def ada_products(c):
                o = ADA_ORD[c]
                pe.wait_ge(s_adaacc, o + 1)
                for m in range(2):
                    mm = pe.matmul(bank[7][:, 2 * c + m:2 * c + m + 1],
                                   ada_acc[o % 2][:, 0, m * P:(m + 1) * P], ones[:, 0:1], start=True, stop=True)
                mm.then_inc(s_adamm, 1)

            def ada_direct(c):
                pe.wait_ge(s_ada[c % 2], 16 * (c // 2 + 1))
                pe.wait_ge(s_cact, 1)
                for m in range(2):
                    for t in range(KD):
                        mm = pe.matmul(bank[7][:, 2 * c + m:2 * c + m + 1], ada_stage[c % 2][:, t, m * P:(m + 1) * P],
                                       c_act[:, 0, t:t + 1], start=(t == 0), stop=(t == KD - 1))
                mm.then_inc(s_adadir, 1)

            pe.wait_ge(s_vcol, 2)
            for c in range(ADA_FIRST):
                if c in ADA_PE:
                    ada_direct(c)
                else:
                    ada_products(c)
                if c == 3:
                    sum_squares()

            hi = lambda k: act_hi[:, k, :]
            lo = lambda k: act_lo[:, k, :]
            t_acc = [0]

            def acc_bank():
                if t_acc[0] >= 4:
                    pe.wait_ge(s_free, t_acc[0] - 3 + (t_acc[0] - 4 >= 5))
                b = bank[t_acc[0] % 4]
                t_acc[0] += 1
                return b

            pairs = list(enumerate(PAIRS))

            def logits():
                for _ in range(PAIRS_PER_TILE):
                    if not pairs:
                        return
                    s, (i, h) = pairs.pop(0)
                    if s == 0:
                        pe.wait_ge(s_free, 7)
                        pe.wait_ge(s_wi, 1)
                    if s >= 2:
                        pe.wait_ge(s_relu, s - 1)
                    half = slice(HD * (h % 2), HD * (h % 2) + HD)
                    n = P * (i + 1)
                    pe.matmul(bank[4 + s % 2][:, 0:n], qiT[half, h // 2, i * P:(i + 1) * P], kiT[half, 0:n],
                              start=True, stop=True).then_inc(s_lg, 1)

            ada_at = [ADA_FIRST]

            def ada_next(count):
                for _ in range(count):
                    ada_products(ada_at[0])
                    ada_at[0] += 1

            for n in range(N_IN):
                chunk_ready(n)
                b = n % 2
                if n == 0:
                    dst = acc_bank()
                    for t in range(TT):
                        mm = tile_tokens(dst[:, t * P:(t + 1) * P], b, slice(0, P), t, (lambda k: normed_parts(0, k)) if t == 0 else None)
                    mm.then_inc(s_acc, 1)
                    ada_next(1)
                    tile(acc_bank()[:], b, slice(P, 2 * P), KD, hi, lo).then_inc(s_wused, 1)
                    ada_next(2)
                elif n == 2:
                    tile(acc_bank()[:], b, slice(0, P), KD, hi, lo).then_inc(s_acc, 1)
                    ada_next(1)
                    tile(acc_bank()[:], b, slice(P, 2 * P), KD, hi, lo).then_inc(s_wused, 1)
                    ada_next(2)
                    pe.wait_ge(s_free, 7)
                    for t in range(TT):
                        mm = pe.transpose(bank[5][:, t * 8:(t + 1) * 8], wiT[HD:HD + 8, t * P:(t + 1) * P],
                                          ident[HD:HD + 8, HD:HD + 8])
                    mm.then_inc(s_wiT, 1)
                elif n >= 9:
                    for tp in range(2):
                        dst = acc_bank()
                        for t in (2 * tp, 2 * tp + 1):
                            mm = tile_tokens(dst[:, (t % 2) * NCOL:(t % 2 + 1) * NCOL], b, slice(0, NCOL), t)
                        mm.then_inc((s_acc, s_wused)[tp], 1)
                else:
                    for m in range(2):
                        tile(acc_bank()[:], b, slice(m * P, (m + 1) * P), KD, hi, lo).then_inc((s_acc, s_wused)[m], 1)
                        ada_next(max(0, min(m + 1, ADA_WINDOW.get(n, 0) - 1)))
                        if n >= 3:
                            logits()
                if n == 2:
                    pe.wait_ge(s_ckv, CKV_STEPS)
                    for t in range(TT):
                        mm = pe.transpose(bank[6][:, t * P:(t + 1) * P], ckv[:, t, :], ident[:])
                    mm.then_inc(s_ckvt, 1)
            assert not pairs and t_acc[0] == N_IN_TILES

            pe.wait_ge(s_free, N_IN_TILES + 1)
            pe.wait_ge(s_ckvT, 1)
            pe.wait_ge(s_late, 32)
            n_items = len(ITEMS)
            O_BANK = (7, 1)

            def q_lat(h):
                half = slice(HD * (h % 2), HD * (h % 2) + HD)
                if h >= 1:
                    pe.wait_ge(s_qlT, h)
                pe.matmul(bank[2][:], wuk[half, h // 2, :], qbT[half, h // 2, :], start=True, stop=True).then_inc(s_ql, 1)

            def scores(s):
                kind, h, i = ITEMS[s]
                n = P * (i + 1)
                if s >= 2:
                    pe.wait_ge(s_min, s - 1)
                qs = slice(i * P, (i + 1) * P)
                if kind == "A":
                    half = slice(HD * (h % 2), HD * (h % 2) + HD)
                    lhs, rhs = qaT[half, h // 2, qs], kaT[half, h // 2, 0:n]
                else:
                    pe.wait_ge(s_qlT, h + 1)
                    lhs, rhs = qlatT[h % 2][:, qs], ckvT[:, 0:n]
                pe.matmul(bank[4 + s % 2][:, 0:n], lhs, rhs, start=True, stop=True).then_inc(s_s, 1)

            def turn(s):
                i = ITEMS[s][2]
                pe.wait_ge(s_norm, s + 1)
                if s >= 1:
                    pe.wait_ge(s_pt, s)
                for kb in range(i + 1):
                    mm = pe.transpose(bank[6][:, kb * P:(kb + 1) * P], probs[s % 4][:, kb * P:(kb + 1) * P], ident[:])
                mm.then_inc(s_t, 1)

            def weigh(s):
                kind, h, i = ITEMS[s]
                g = s // TT
                pe.wait_ge(s_pt, s + 1)
                if i == 0 and g >= 2:
                    if g - 2 < NH:
                        pe.wait_ge(s_mlo, g - 1)
                    else:
                        pe.wait_ge(s_oh, g - 1 - NH)
                qs = slice(i * P, (i + 1) * P)
                o = bank[O_BANK[g % 2]]
                for kb in range(i + 1):
                    if kind == "A":
                        half = slice(HD * (h % 2), HD * (h % 2) + HD)
                        lhs, dst = va[:, kb, h * HD:(h + 1) * HD], o[half, qs]
                    else:
                        lhs, dst = ckv[:, kb, :], o[:, qs]
                    mm = pe.matmul(dst, lhs, probsT[s % 3][:, kb, :], start=(kb == 0), stop=(kb == i))
                mm.then_inc(s_pv, 1)

            def up_v(h):
                half = slice(HD * (h % 2), HD * (h % 2) + HD)
                pe.wait_ge(s_oh, h + 1)
                if h >= 1:
                    pe.wait_ge(s_mlo, NH + h)
                pe.matmul(bank[3][half, :], wuv[:, h, :], olat[h % 2][:], start=True, stop=True).then_inc(s_uv, 1)

            assert ada_at[0] == ADA_LOOP
            pe.wait_ge(s_mod, 3)
            for s in range(n_items + 9):
                if s < n_items:
                    kind, h, i = ITEMS[s]
                    if s + 2 < n_items and ITEMS[s + 2][0] == "B" and ITEMS[s + 2][2] == 0:
                        q_lat(ITEMS[s + 2][1])
                    scores(s)
                if 3 <= s < n_items + 3:
                    turn(s - 3)
                if 5 <= s < n_items + 5:
                    weigh(s - 5)
                if s >= 7 and s - 7 < n_items and ITEMS[s - 7][0] == "B" and ITEMS[s - 7][2] == TT - 1:
                    up_v(ITEMS[s - 7][1])

            def project(n0, steps, ready, rhs_hi, rhs_lo, waits=None, groups=((0, KD),), pairs=1, t0=0):
                with pe.Fori(0, steps) as j:
                    n = 0
                    for m2 in range(pairs):
                        base = 2 * (m2 % 2) if pairs > 1 else 0
                        for g, (k0, kn) in enumerate(groups):
                            b = (n0 + n) % 2
                            pe.wait_ge(s_lo, j * (pairs * len(groups)) + (n0 + n + 1))
                            for m in range(2):
                                if g == 0 and waits:
                                    waits(j, 2 * m2 + m)
                                mm = tile(bank[base + m][:], b, slice(m * P, (m + 1) * P), kn,
                                          lambda k, k0=k0: rhs_hi(k0 + k), lambda k, k0=k0: rhs_lo(k0 + k),
                                          first=(g == 0), last=(g == len(groups) - 1))
                                if m == 1:
                                    mm.then_inc(s_wused, 1)
                                elif g == len(groups) - 1:
                                    mm.then_inc(ready, 1)
                            n += 1

            pe.wait_ge(s_mlo, 2 * NH)
            RES = [0]

            def residual(n0, rhs_hi, rhs_lo, groups=((0, KD),)):
                r0 = RES[0]
                RES[0] += KD

                def waits(j, t):
                    pe.wait_ge(s_res, j * 4 + (r0 + t - 3))

                if r0:
                    project(n0, 2, s_racc, rhs_hi, rhs_lo, waits, groups, pairs=2)
                else:
                    n = 0
                    for t in range(KD):
                        b = (n0 + n) % 2
                        if t % 2 == 0:
                            pe.wait_ge(s_lo, n0 + n + 1)
                        if t >= 4:
                            pe.wait_ge(s_res, t - 3)
                        tile(bank[t % 4][:], b, slice((t % 2) * P, (t % 2 + 1) * P), KD, rhs_hi, rhs_lo).then_inc((s_racc, s_wused)[t % 2], 1)
                        n += t % 2

            residual(C_OUT, hi, lo)
            sum_squares()
            pe.wait_ge(s_res, KD)
            with pe.Fori(0, KF // 2) as j:
                for q in range(2):
                    b = (C_GU + q) % 2
                    pe.wait_ge(s_lo, j * 2 + (C_GU + q + 1))
                    for m in range(2):
                        pe.wait_ge((s_silu, s_up)[q], j * 2 + (1 + m))
                        tile(bank[2 * q + m][:], b, slice(m * P, (m + 1) * P), KD, hi, lo,
                             wait=(lambda k: normed_parts(1, k)) if (q, m) == (0, 0) else None).then_inc((s_guacc, s_wused)[m], 1)
                pe.wait_ge(s_adaacc, j + (ADA_DVE + 1))
                for m in range(2):
                    mm = pe.matmul(bank[5][:, bass.ds(j * 2 + m, 1)], ada2_acc[:, m * P:(m + 1) * P], ones[:, 0:1],
                                   start=True, stop=True)
                mm.then_inc(s_adamm, 1)
            pe.wait_ge(s_silu, 2 + KF)
            pe.wait_ge(s_up, 2 + KF)
            pe.wait_ge(s_fflo, 2 + KF)
            residual(C_DOWN, lambda k: ff_hi[:, k, :], lambda k: ff_lo[:, k, :], ((0, 8), (8, 8), (16, 6)))
            sum_squares()
            sum_squares()
            pe.wait_ge(s_res, 2 * KD)
            with pe.Fori(0, KD // 2) as j:
                for q in range(2):
                    b = (C_IN2 + q) % 2
                    pe.wait_ge(s_lo, j * 2 + (C_IN2 + q + 1))
                    for m in range(2):
                        pe.wait_ge((s_sig, s_v)[q], j * 2 + (1 + m))
                        tile(bank[2 * q + m][:], b, slice(m * P, (m + 1) * P), KD, hi, lo,
                             wait=(lambda k: normed_parts(2, k)) if (q, m) == (0, 0) else None).then_inc((s_i2acc, s_wused)[m], 1)
            pe.wait_ge(s_lruw, 32)
            for slot in range(KD, C_LRU - C_IN2):
                n = C_IN2 + slot
                pe.wait_ge(s_lo, n + 1)
                for m in range(2):
                    t = 2 * (slot - KD) + m
                    if t >= 4:
                        pe.wait_ge(s_gate, t - 3)
                    else:
                        pe.wait_ge((s_sig, s_v)[t // 2], 2 + KD)
                    tile(bank[t % 4][:], n % 2, slice(m * P, (m + 1) * P), KD, hi, lo).then_inc((s_i2acc, s_wused)[m], 1)
                p, odd = divmod(slot - LRU_SLOT, 2)
                if 0 <= p < KD // 2 and not odd:
                    pe.wait_ge(s_xs, 2 * SHORT * (p + 1))
                    for k in (2 * p, 2 * p + 1):
                        for g in range(2):
                            if p:
                                pe.wait_ge((s_r, s_i)[g], k - 1)
                            pe.matmul(bank[4 + 2 * (k % 2) + g][:], (wr, wi)[g][:, k, :], tmp[k % 2][:],
                                      start=True, stop=True).then_inc(s_gmm, 1)

            def residual_tile(n0, t, rhs_hi, rhs_lo, free, ready):
                n = n0 + t // 2
                if t % 2 == 0:
                    pe.wait_ge(s_lo, n + 1)
                free(t)
                tile(bank[t % 4][:], n % 2, slice((t % 2) * P, (t % 2 + 1) * P), KD, rhs_hi, rhs_lo,
                     wait=ready if t == 0 else None).then_inc((s_racc, s_wused)[t % 2], 1)

            def lru_ready(k):
                pe.wait_ge(s_lhi, k + 1)
                pe.wait_ge(s_llo, k + 1)

            for t in range(KD):
                residual_tile(C_LRU, t, lambda k: lru_hi[:, k, :], lambda k: lru_lo[:, k, 0:T],
                              lambda t: pe.wait_ge(*((s_gate, 3 * KD - 3 + t) if t < 4 else (s_res, 2 * KD + t - 3))),
                              lru_ready)
                if t == MEAN_AFTER:
                    pe.wait_ge(s_conv, CONV * KD)
                    pe.wait_ge(s_r, KD)
                    pe.wait_ge(s_i, KD)
                    for k in range(KD):
                        mm = pe.matmul(bank[5][:], ones[:], conv[:, k, :], start=(k == 0), stop=(k == KD - 1))
                    mm.then_inc(s_mean, 1)
                if t == VAR_AFTER:
                    sum_squares()
            pe.wait_ge(s_res, 3 * KD - 4)
            with pe.Fori(0, 2) as j:
                for q in range(2):
                    b = (C_PW2 + q) % 2
                    pe.wait_ge(s_lo, j * 2 + (C_PW2 + q + 1))
                    for m in range(2):
                        pe.wait_ge(s_res, 3 * KD - 3 + 2 * q + m)
                        pe.wait_ge(s_yc, j * 4 + (2 * q + m + 1))
                        tile(bank[2 * q + m][:], b, slice(m * P, (m + 1) * P), KD,
                             lambda k: ln_hi[:, k, :], lambda k: ln_lo[:, k, :],
                             wait=(lambda k: pe.wait_ge(s_lnlo, k + 1)) if (q, m) == (0, 0) else None).then_inc((s_pacc, s_wused)[m], 1)
            for t in range(KD):
                residual_tile(C_OUT2, t, hi, lo,
                              lambda t: pe.wait_ge(*((s_yc, 4 + 4 + t + 1) if t < 4 else (s_res, 3 * KD + t - 3))),
                              lambda k: pe.wait_ge(s_yclo, k + 1))
            sum_squares()
            pe.wait_ge(s_xf, 2 * KD)
            pe.wait_ge(s_res, 4 * KD)
            for s in range(2 * TT):
                t, half = divmod(s, 2)
                if s >= 4:
                    pe.wait_ge(s_on, s - 3)
                for q in range(4):
                    k = 4 * half + q
                    mm = pe.transpose(bank[s % 4][:, q * P:(q + 1) * P], xT[:, k, t * P:(t + 1) * P], ident[:])
                mm.then_inc(s_ot, 1)

        @block.scalar
        def _(act):
            def hi_part(n, b, half):
                act.wait_ge(s_stage[b], half * 16 + 16)
                if not isinstance(n, int) or n >= 2:
                    act.wait_ge(s_wused, n - 1)
                nc.scalar.activation(w_hi[b][:], w_stage[b][:], ACT.Copy).then_inc(s_hi, 1)

            act.wait_ge(s_c, 32)
            nc.scalar.activation(c_act[:], c_sb[:], ACT.Silu).then_inc(s_cact, 1)
            act.wait_ge(s_vt, 1)
            nc.scalar.activation(vcol[:, 0:208], bank[4][:, 0:208], ACT.Copy).then_inc(s_vcol, 1)
            nc.scalar.activation(vcol[:, 256:504], bank[4][:, 256:504], ACT.Copy).then_inc(s_vcol, 1)
            for k in range(KD):
                act.wait_ge(s_xt, k + 1)
                nc.scalar.activation(xT[:, k, :], bank[k % 4][:], ACT.Copy).then_inc(s_xTr, 1)

            norms = [0]

            def squares(ready, src=None, chunks=0, next_chunk=None):
                j = norms[0]
                norms[0] += 1
                for k in range(KD):
                    ready(k)
                    if KD * j + k >= 2:
                        act.wait_ge(s_sqused, KD * j + k - 1)
                    nc.scalar.activation(tmp[k % 2][:], (src or xT)[:, k, :], ACT.Square).then_inc(s_sq, 1)
                for _ in range(chunks):
                    next_chunk()
                act.wait_ge(s_sqused, KD * (j + 1))
                if j >= 1:
                    act.wait_ge(s_rstd, j)
                act.wait_ge(s_set, 2)
                nc.scalar.activation(rstd[:], bank[4][:], ACT.Sqrt, bias=eps[:, 0:1], scale=1.0 / D).then_inc(s_sd, 1)

            splits = [0]

            def act_hi_parts(shift):
                j = splits[0]
                splits[0] += 1
                for k in range(KD):
                    act.wait_ge(s_u, KD * j + k + 1)
                    nc.scalar.activation(act_hi[:, k, :], tmp[k % 2][:], ACT.Identity, bias=modc(shift + k)).then_inc(s_ahi, 1)

            squares(lambda k: act.wait_ge(s_xTr, k + 1))
            hi_part(0, 0, 0)
            hi_part(1, 1, 0)
            act.wait_ge(s_mod, 2)
            act_hi_parts(SH1)

            tiles = [0]

            firsts = [0]

            def arrived(n, last):
                if last:
                    act.wait_ge(s_wused, n + 1)
                else:
                    firsts[0] += 1
                    act.wait_ge(s_acc, firsts[0])

            def take(n, last, dst, src, scale=1.0):
                t = tiles[0]
                arrived(n, last)
                i = nc.scalar.activation(dst, src(bank[t % 4]), ACT.Copy, scale=scale)
                tiles[0] += 1
                return i

            whole = lambda b: b[:]
            pairs = list(enumerate(PAIRS))

            def relus():
                for _ in range(PAIRS_PER_TILE):
                    if not pairs:
                        return
                    s, (i, h) = pairs.pop(0)
                    n = P * (i + 1)
                    act.wait_ge(s_lg, s + 1)
                    if s >= 2:
                        act.wait_ge(s_score, s - 1)
                    nc.scalar.activation(relu[s % 2][:, 0:n], bank[4 + s % 2][:, 0:n], ACT.Relu).then_inc(s_relu, 1)

            for n in range(N_IN):
                if n == 0:
                    take(n, False, ckv[:].rearrange("p t r -> p (t r)"), whole).then_inc(s_free, 1)
                    take(n, True, qiT[:, 0, :], whole).then_inc(s_free, 1)
                elif n == 1:
                    take(n, False, qiT[:, 1, :], whole).then_inc(s_free, 1)
                    take(n, True, qiT[:, 2, :], whole).then_inc(s_free, 1)
                elif n == 2:
                    take(n, False, qiT[:, 3, :], whole).then_inc(s_free, 1)
                    t = tiles[0]
                    arrived(n, True)
                    nc.scalar.activation(kiT[0:HD, :], bank[t % 4][0:HD, :], ACT.Copy)
                    nc.scalar.activation(kiT[HD:P, :], bank[t % 4][0:HD, :], ACT.Copy).then_inc(s_free, 1)
                    nc.scalar.activation(wiT[HD:HD + 8, :], bank[t % 4][HD:HD + 8, :], ACT.Copy, scale=IDX_SCALE).then_inc(s_free, 1)
                    tiles[0] += 1
                    act.wait_ge(s_wiT, 1)
                    nc.scalar.activation(wi_sb[:].rearrange("p t h -> p (t h)"), bank[5][:, 0:TT * 8], ACT.Copy).then_inc(s_wi, 1)
                    act.wait_ge(s_ckv, TT)
                    nc.scalar.activation(ckv_ss[:, 1, :], ckv_ss[:, 0, :], ACT.Sqrt, bias=eps[:, 0:1], scale=1.0 / P).then_inc(s_ckvsd, 1)
                    act.wait_ge(s_ckvt, 1)
                    nc.scalar.activation(ckvT[:], bank[6][:], ACT.Copy).then_inc(s_ckvT, 1)
                elif n >= 9:
                    for tp in range(2):
                        vs = slice((n - 9) * NCOL, (n - 8) * NCOL)
                        take(n, tp == 1, va[:, 2 * tp:2 * tp + 2, vs], lambda b: b[:].rearrange("p (t c) -> p t c", t=2)).then_inc(s_free, 1)
                else:
                    for m in range(2):
                        if n <= 4:
                            take(n, m == 1, qbT[:, 2 * (n - 3) + m, :], whole).then_inc(s_free, 1)
                        elif n <= 6:
                            take(n, m == 1, qaT[:, 2 * (n - 5) + m, :], whole, QSCALE).then_inc(s_free, 1)
                        else:
                            take(n, m == 1, kaT[:, 2 * (n - 7) + m, :], whole).then_inc(s_free, 1)
                        relus()
                hi_part(n + 2, n % 2, (n + 2) // 2)
            assert tiles[0] == N_IN_TILES

            O_BANK = (7, 1)
            n_items = len(ITEMS)

            def exponentials(s):
                n = P * (ITEMS[s][2] + 1)
                act.wait_ge(s_min, s + 1)
                if s >= 4:
                    act.wait_ge(s_t, s - 3)
                nc.scalar.activation(probs[s % 4][:, 0:n], tmp[s % 2][:, 0:n], ACT.Exp, bias=negmax[:, s:s + 1],
                                     scale=-1.0, accum_out=expsum[:, s:s + 1]).then_inc(s_exp, 1)

            def turned(s):
                i = ITEMS[s][2]
                n = P * (i + 1)
                act.wait_ge(s_t, s + 1)
                if s >= 3:
                    act.wait_ge(s_pv, s - 2)
                nc.scalar.activation(probsT[s % 3][:, 0:i + 1, :].rearrange("p k q -> p (k q)"),
                                     bank[6][:, 0:n], ACT.Copy).then_inc(s_pt, 1)

            for s in range(n_items + 9):
                if s < n_items:
                    if s + 2 < n_items and ITEMS[s + 2][0] == "B" and ITEMS[s + 2][2] == 0:
                        h = ITEMS[s + 2][1]
                        act.wait_ge(s_ql, h + 1)
                        if h >= 2:
                            act.wait_ge(s_s, TT * (NH + h - 1))
                        nc.scalar.activation(qlatT[h % 2][:], bank[2][:], ACT.Copy, scale=QSCALE).then_inc(s_qlT, 1)
                    exponentials(s)
                if 3 <= s < n_items + 3:
                    turned(s - 3)
                if 6 <= s < n_items + 6 and ITEMS[s - 6][2] == TT - 1:
                    kind, h, i = ITEMS[s - 6]
                    act.wait_ge(s_pv, s - 5)
                    if kind == "A":
                        half = slice(HD * (h % 2), HD * (h % 2) + HD)
                        nc.scalar.activation(act_hi[half, h // 2, :], bank[O_BANK[h % 2]][half, :], ACT.Copy).then_inc(s_mhi, 1)
                    else:
                        if h >= 2:
                            act.wait_ge(s_uv, h - 1)
                        nc.scalar.activation(olat[h % 2][:], bank[O_BANK[h % 2]][:], ACT.Copy).then_inc(s_oh, 1)
                if s >= 8 and s - 8 < n_items and ITEMS[s - 8][0] == "B" and ITEMS[s - 8][2] == TT - 1:
                    h = ITEMS[s - 8][1]
                    half = slice(HD * (h % 2), HD * (h % 2) + HD)
                    act.wait_ge(s_uv, h + 1)
                    nc.scalar.activation(act_hi[half, 4 + h // 2, :], bank[3][half, :], ACT.Copy).then_inc(s_mhi, 1)

            for n in range(C_OUT, C_GU):
                hi_part(n + 2, n % 2, (n + 2) // 2)
            squares(lambda k: act.wait_ge(s_res, k + 1))
            act.wait_ge(s_mod, 4)
            act_hi_parts(SH2)
            act.wait_ge(s_alo, 2 * KD)
            nc.scalar.activation(nothing[:, 4:5], eps[:, 0:1], ACT.Silu).then_inc(s_silu, 2)
            with act.Fori(0, KF // 2) as j:
                for q in range(2):
                    for m in range(2):
                        if q == 0:
                            act.wait_ge((s_guacc, s_wused)[m], j * 2 + (1, C_GU + 1)[m])
                            act.wait_ge(s_up, j * 2 + (1 + m))
                            nc.scalar.activation(tmp[m][:], bank[m][:], ACT.Silu).then_inc(s_silu, 1)
                    hi_part(j * 2 + (C_GU + q + 2), (C_GU + q) % 2, j + (C_GU + q + 2) // 2)
            lam = vcol[:, VROW["lam_2"]:VROW["lam_2"] + KD]
            nc.scalar.activation(lam_t[:, 0, :], lam, ACT.Abs).then_inc(s_lama, 1)
            act.wait_ge(s_lama, 1)
            nc.scalar.activation(lam_t[:, 1, :], lam_t[:, 0, :], ACT.Exp, scale=-1.0).then_inc(s_lama, 1)
            act.wait_ge(s_lama, 2)
            act.wait_ge(s_lam, 2)
            nc.scalar.activation(lam_t[:, 3, :], lam_t[:, 2, :], ACT.Ln).then_inc(s_lama, 1)
            with act.Fori(0, 6) as j:
                for q in range(2):
                    hi_part(j * 2 + (C_DOWN + q + 2), (C_DOWN + q) % 2, j + (C_DOWN + q + 2) // 2)
            squares(lambda k: act.wait_ge(s_res, KD + k + 1))
            squares(lambda k: act.wait_ge(s_xf, k + 1))
            act.wait_ge(s_mod, 7)
            act_hi_parts(SH3)
            nc.scalar.activation(nothing[:, 4:5], eps[:, 0:1], ACT.Sigmoid).then_inc(s_sig, 2)
            act.wait_ge(s_alo, 3 * KD)
            with act.Fori(0, KD // 2) as j:
                for q in range(2):
                    if q == 0:
                        for m in range(2):
                            act.wait_ge((s_i2acc, s_wused)[m], j * 2 + (1, C_IN2 + 1)[m])
                            act.wait_ge(s_v, j * 2 + (1 + m))
                            nc.scalar.activation(tmp[m][:], bank[m][:], ACT.Sigmoid).then_inc(s_sig, 1)
                    hi_part(j * 2 + (C_IN2 + q + 2), (C_IN2 + q) % 2, j + (C_IN2 + q + 2) // 2)

            def lru_gates(p):
                for k in (2 * p, 2 * p + 1):
                    m = k % 2
                    act.wait_ge(s_gmm, 2 * k + 1)
                    if p:
                        act.wait_ge(s_scan, k - 1)
                    nc.scalar.activation(decay[m][:], bank[4 + 2 * m][:], ACT.Sigmoid, bias=col("br_2", k)).then_inc(s_r, 1)
                    act.wait_ge(s_gmm, 2 * k + 2)
                    nc.scalar.activation(tmp[2 + m][:], bank[5 + 2 * m][:], ACT.Sigmoid, bias=col("bi_2", k)).then_inc(s_i, 1)
                for k in (2 * p, 2 * p + 1):
                    act.wait_ge(s_r, k + 1)
                    nc.scalar.activation(l_pad[:, k, 0:T], decay[k % 2][:], ACT.Tanh, scale=lam_t[:, 5, k:k + 1]).then_inc(s_th, 1)
                for k in (2 * p, 2 * p + 1):
                    act.wait_ge(s_th, k + 1)
                    nc.scalar.activation(decay[k % 2][:], decay[k % 2][:], ACT.Exp, scale=lam_t[:, 4, k:k + 1]).then_inc(s_a, 1)
                for k in (2 * p, 2 * p + 1):
                    act.wait_ge(s_a, k + 1)
                    if p:
                        act.wait_ge(s_llo, k - 1)
                    nc.scalar.activation(hidden[k % 2][:], decay[k % 2][:], ACT.Square).then_inc(s_aa, 1)

            def lru_mult(p):
                for k in (2 * p, 2 * p + 1):
                    act.wait_ge(s_m, k + 1)
                    nc.scalar.activation(l_pad[:, k, 0:T], l_pad[:, k, 0:T], ACT.Sqrt).then_inc(s_mt, 1)

            def lru_high(p):
                for k in (2 * p, 2 * p + 1):
                    act.wait_ge(s_y, k + 1)
                    nc.scalar.activation(lru_hi[:, k, :], hidden[k % 2][:], ACT.Copy).then_inc(s_lhi, 1)

            act.wait_ge(s_lam, LAM_STEPS)
            for slot in range(KD, C_LRU - C_IN2):
                n = C_IN2 + slot
                dst, func, lead = ((l_pad, ACT.Copy, PADL), (lgate, ACT.Silu, 0), (cgate, ACT.Silu, 0))[(slot - KD) // 4]
                for m in range(2):
                    act.wait_ge(*((s_wused, n + 1) if m else (s_i2acc, slot + 1)))
                    nc.scalar.activation(dst[:, (2 * (slot - KD) + m) % KD, lead:lead + T],
                                         bank[(2 * (slot - KD) + m) % 4][:], func).then_inc(s_gate, 1)
                hi_part(n + 2, n % 2, (n + 2) // 2)
                p, odd = divmod(slot - LRU_SLOT, 2)
                if 1 <= p <= KD // 2 and not odd:
                    lru_high(p - 1)
                if 0 <= p < KD // 2:
                    (lru_gates, lru_mult)[odd](p)

            chunk = [C_LRU]

            def next_chunk():
                n = chunk[0]
                chunk[0] += 1
                hi_part(n + 2, n % 2, (n + 2) // 2)

            for _ in range((MEAN_AFTER + 1) // 2):
                next_chunk()
            act.wait_ge(s_mean, 1)
            nc.scalar.activation(tmp[2][:], bank[5][:], ACT.Copy, scale=1.0 / D).then_inc(s_mu, 1)
            act.wait_ge(s_gx, KD)
            act.wait_ge(s_llo, KD)
            squares(lambda k: act.wait_ge(s_cen, k + 1), conv, (VAR_AFTER + 1) // 2 - (MEAN_AFTER + 1) // 2, next_chunk)
            for k in range(KD):
                if k in LN_CHUNKS:
                    next_chunk()
                act.wait_ge(s_lnu, k + 1)
                if k >= 2:
                    act.wait_ge(s_lnlo, k - 1)
                nc.scalar.activation(tmp[2 + k % 2][:], tmp[k % 2][:], ACT.Silu, bias=col("cln_b_2", k)).then_inc(s_lns, 1)
            while chunk[0] < C_END - 2:
                next_chunk()
            squares(lambda k: act.wait_ge(s_res, 3 * KD + k + 1))
            for s in range(2 * TT):
                t, half = divmod(s, 2)
                act.wait_ge(s_ot, s + 1)
                nc.scalar.activation(o_nat[:, t, half * 512:(half + 1) * 512], bank[s % 4][:], ACT.Copy).then_inc(s_on, 1)

        @block.vector
        def _(dve):
            V = nc.vector
            dve.memset(eps[:], EPS).then_inc(s_set, 1)
            dve.memset(ones[:], 1.0).then_inc(s_set, 1)
            dve.wait_ge(s_set, 2)
            steps = [0]

            def ada(c):
                b, o = c % 2, ADA_ORD[c]
                dve.wait_ge(s_ada[b], 16 * (c // 2 + 1))
                if o >= 2:
                    dve.wait_ge(s_adamm, o - 1)
                which = 0 if c < ADA1 else 1
                for t in range(KD):
                    src, w = ada_stage[b][:, t, :], c_act[:, which, t:t + 1]
                    dst = ada_acc[o % 2][:, t % 2, :]
                    if t < 2:
                        i = V.tensor_scalar(dst, src, w, None, ALU.mult)
                    else:
                        dve.wait_ge(s_adastep, steps[0] - 1)
                        i = V.scalar_tensor_tensor(dst, src, w, dst, ALU.mult, ALU.add)
                    i.then_inc(s_adastep, 1)
                    steps[0] += 1
                dve.wait_ge(s_adastep, steps[0])
                V.tensor_tensor(ada_acc[o % 2][:, 0, :], ada_acc[o % 2][:, 0, :], ada_acc[o % 2][:, 1, :], ALU.add).then_inc(s_adaacc, 1)

            dve.wait_ge(s_cact, 1)
            for c in range(ADA_FIRST):
                if c not in ADA_PE:
                    ada(c)
            dve.wait_ge(s_vcol, 2)
            dve.wait_ge(s_adadir, len(ADA_PE))
            dve.wait_ge(s_adamm, ADA_FIRST - len(ADA_PE))
            nm = [0]

            def fold(gain, sc, slot):
                nm[0] += 1
                V.scalar_tensor_tensor(scale1[:, slot, :], mod[:, sc:sc + KD], 1.0,
                                       vcol[:, VROW[gain]:VROW[gain] + KD], ALU.add, ALU.mult).then_inc(s_mod, 1)

            V.tensor_tensor(mod[:, 0:16], bank[7][:, 0:16], vcol[:, 0:16], ALU.add).then_inc(s_mod, 1)
            dve.wait_ge(s_mod, 1)
            fold("g_attn", SC1, 0)
            dve.wait_ge(s_mod, 2)

            norms = [0]

            def rstd_ready():
                norms[0] += 1
                dve.wait_ge(s_sd, norms[0])
                V.reciprocal(rstd[:], rstd[:]).then_inc(s_rstd, 1)
                dve.wait_ge(s_rstd, norms[0])

            splits = [0]

            def normed(slot, shift):
                j = splits[0]
                splits[0] += 1
                for k in range(KD + 1):
                    if k < KD:
                        if k >= 2:
                            dve.wait_ge(s_alo, KD * j + k - 1)
                        V.scalar_tensor_tensor(tmp[k % 2][:], xT[:, k, :], scale1[:, slot, k:k + 1], rstd[:],
                                               ALU.mult, ALU.mult).then_inc(s_u, 1)
                    if k >= 1:
                        dve.wait_ge(s_ahi, KD * j + k)
                        V.scalar_tensor_tensor(act_lo[:, k - 1, :], tmp[(k - 1) % 2][:], modc(shift + k - 1),
                                               act_hi[:, k - 1, :].bitcast(F32), ALU.add, ALU.subtract).then_inc(s_alo, 1)

            rstd_ready()
            normed(0, SH1)

            pairs = list(enumerate(PAIRS))

            def scores_sum(count):
                for _ in range(count):
                    if not pairs:
                        return
                    s, (i, h) = pairs.pop(0)
                    n = P * (i + 1)
                    dve.wait_ge(s_relu, s + 1)
                    w = wi_sb[:, i, h:h + 1]
                    if h == 0:
                        V.tensor_scalar(score[i][:], relu[s % 2][:, 0:n], w, None, ALU.mult).then_inc(s_score, 1)
                    else:
                        dve.wait_ge(s_score, s)
                        V.scalar_tensor_tensor(score[i][:], relu[s % 2][:, 0:n], w, score[i][:], ALU.mult, ALU.add).then_inc(s_score, 1)

            c = ADA_FIRST
            for n in range(6):
                for _ in range(ADA_WINDOW.get(n, 0)):
                    ada(c)
                    c += 1
                if n == 1:
                    dve.wait_ge(s_free, 1)
                    for t in range(TT):
                        V.tensor_tensor_reduce(tmp[2][:, t * P:(t + 1) * P], ckv[:, t, :], ckv[:, t, :], 1.0, 0.0,
                                               ALU.mult, ALU.add, ckv_ss[:, 0, t:t + 1]).then_inc(s_ckv, 1)
                if n == 2:
                    dve.wait_ge(s_ckvsd, 1)
                    V.reciprocal(ckv_ss[:, 2, :], ckv_ss[:, 1, :]).then_inc(s_ckv, 1)
                    dve.wait_ge(s_ckv, TT + 1)
                    dve.wait_ge(s_const, 16 * NCONST)
                    for t in range(TT):
                        V.scalar_tensor_tensor(ckv[:, t, :], ckv[:, t, :], ckv_ss[:, 2, t:t + 1], kvg[:],
                                               ALU.mult, ALU.mult).then_inc(s_ckv, 1)
                if n >= 3:
                    scores_sum(2 * PAIRS_PER_TILE)
            assert not pairs
            dve.wait_ge(s_score, len(PAIRS))
            top = 0
            for i in range(1, TT):
                d = score[i][:, i * P:(i + 1) * P]
                V.tensor_tensor(d, d, causal[:, 1, :], ALU.min).then_inc(s_top, 1)
                top += 1
            for r in range(TOPK // 8):
                for i in range(1, TT):
                    dve.wait_ge(s_top, top - 2)
                    V.max(top8[i][:], (score if r == 0 else work)[i][:]).then_inc(s_top, 1)
                    top += 1
                for i in range(1, TT):
                    dve.wait_ge(s_top, top - 2)
                    V.match_replace(work[i][:], top8[i][:], (score if r == 0 else work)[i][:], -3.0e38).then_inc(s_top, 1)
                    top += 1
            for i in range(1, TT):
                dve.wait_ge(s_top, top - 2)
                V.tensor_tensor(work[i][:], work[i][:], score[i][:], ALU.is_equal).then_inc(s_top, 1)
                top += 1
            for i in range(1, TT):
                dve.wait_ge(s_top, top - 2)
                V.tensor_scalar(work[i][:], work[i][:], BIG, None, ALU.mult).then_inc(s_top, 1)
                top += 1
            assert top == TOP_STEPS
            dve.wait_ge(s_adamm, ADA_DVE)
            V.tensor_tensor(mod[:, 16:2 * ADA_LOOP], bank[7][:, 16:2 * ADA_LOOP], vcol[:, 16:2 * ADA_LOOP], ALU.add).then_inc(s_mod, 1)
            dve.wait_ge(s_mod, 3)
            fold("g_ffn", SC2, 1)

            O_BANK = (7, 1)
            n_items = len(ITEMS)

            def least(s):
                kind, h, i = ITEMS[s]
                n = P * (i + 1)
                dve.wait_ge(s_s, s + 1)
                if kind == "A":
                    dve.wait_ge(s_tab, h + 1)
                    t = table[h % 2][:, T - n:T]
                else:
                    u = s - NH * TT
                    dve.wait_ge(s_comb, u + 1)
                    t = comb[u % 2][:, 0:n]
                if s >= 2:
                    dve.wait_ge(s_exp, s - 1)
                V.tensor_tensor_reduce(tmp[s % 2][:, 0:n], bank[4 + s % 2][:, 0:n], t, 1.0, 3.0e38,
                                       ALU.add, ALU.min, negmax[:, s:s + 1]).then_inc(s_min, 1)

            def normalise(s):
                n = P * (ITEMS[s][2] + 1)
                dve.wait_ge(s_exp, s + 1)
                V.reciprocal(expinv[:, s:s + 1], expsum[:, s:s + 1]).then_inc(s_inv, 1)
                dve.wait_ge(s_inv, s + 1)
                V.tensor_scalar(probs[s % 4][:, 0:n], probs[s % 4][:, 0:n], expinv[:, s:s + 1], None,
                                ALU.mult).then_inc(s_norm, 1)

            def low(g, src, k):
                half = slice(HD * (g % 2), HD * (g % 2) + HD)
                dve.wait_ge(s_mhi, g + 1)
                V.tensor_tensor(act_lo[half, k, :], src[half, :], act_hi[half, k, :].bitcast(F32), ALU.subtract).then_inc(s_mlo, 1)

            for s in range(n_items + 9):
                if s < n_items:
                    least(s)
                if 1 <= s < n_items + 1:
                    normalise(s - 1)
                if 6 <= s < n_items + 6 and ITEMS[s - 6][2] == TT - 1 and ITEMS[s - 6][0] == "A":
                    h = ITEMS[s - 6][1]
                    low(h, bank[O_BANK[h % 2]], h // 2)
                if s >= 8 and s - 8 < n_items and ITEMS[s - 8][0] == "B" and ITEMS[s - 8][2] == TT - 1:
                    h = ITEMS[s - 8][1]
                    low(NH + h, bank[3], 4 + h // 2)
            dve.wait_ge(s_mod, 4)
            added = [0]

            def residual(n0, gain, groups=1):
                r0 = added[0]
                added[0] += KD
                for k in range(KD):
                    dve.wait_ge(*((s_wused, n0 + groups * (k // 2 + 1)) if k % 2 else (s_racc, (r0 + k) // 2 + 1)))
                    V.scalar_tensor_tensor(xT[:, k, :], bank[k % 4][:], gain(k), xT[:, k, :], ALU.mult, ALU.add).then_inc(s_res, 1)

            def residual_2(n0, r0, t):
                dve.wait_ge(*((s_wused, n0 + t // 2 + 1) if t % 2 else (s_racc, (r0 + t) // 2 + 1)))
                V.scalar_tensor_tensor(xT[:, t, :], bank[t % 4][:], scale1[:, 3, t:t + 1], xT[:, t, :],
                                       ALU.mult, ALU.add).then_inc(s_res, 1)

            residual(C_OUT, lambda k: modc(GA1 + k))
            rstd_ready()
            dve.wait_ge(s_res, KD)
            normed(1, SH2)
            ada_steps = steps[0]
            dve.memset(nothing[:, 1:2], 0.0).then_inc(s_up, 2)
            dve.memset(nothing[:, 3:4], 0.0).then_inc(s_fflo, 2)
            with dve.Fori(0, KF // 2) as j:
                dve.wait_ge(s_adaloop, j * 16 + 16)
                dve.wait_ge(s_adamm, j + ADA_DVE)
                for t in range(KD):
                    src, w = ada2_stage[:, t, :], c_act[:, 1, t:t + 1]
                    if t == 0:
                        V.tensor_scalar(ada2_acc[:], src, w, None, ALU.mult).then_inc(s_adastep, 1)
                    else:
                        dve.wait_ge(s_adastep, j * (KD - 1) + (ada_steps + t))
                        V.scalar_tensor_tensor(ada2_acc[:], src, w, ada2_acc[:], ALU.mult, ALU.add).then_inc(
                            s_adaacc if t == KD - 1 else s_adastep, 1)
                for m in range(2):
                    dve.wait_ge(s_silu, j * 2 + (3 + m))
                    dve.wait_ge((s_guacc, s_wused)[m], j * 2 + (2, C_GU + 2)[m])
                    dve.wait_ge(s_fflo, j * 2 + (1 + m))
                    V.tensor_tensor(tmp[2 + m][:], bank[2 + m][:], tmp[m][:], ALU.mult).then_inc(s_up, 1)
                for m in range(2):
                    dve.wait_ge(s_up, j * 2 + (3 + m))
                    V.tensor_copy(ff_hi[:, bass.ds(j * 2 + m, 1), :], tmp[2 + m][:].rearrange("p (o t) -> p o t", o=1)).then_inc(s_ffhi, 1)
                for m in range(2):
                    dve.wait_ge(s_ffhi, j * 2 + (1 + m))
                    V.tensor_tensor(ff_lo[:, bass.ds(j * 2 + m, 1), :], tmp[2 + m][:].rearrange("p (o t) -> p o t", o=1),
                                    ff_hi[:, bass.ds(j * 2 + m, 1), :].bitcast(F32), ALU.subtract).then_inc(s_fflo, 1)
            dve.wait_ge(s_adamm, ADA_DVE + KF // 2)
            V.tensor_tensor(mod[:, 2 * ADA_LOOP:72], bank[5][:, 0:72 - 2 * ADA_LOOP], vcol[:, 2 * ADA_LOOP:72], ALU.add).then_inc(s_mod, 1)
            dve.wait_ge(s_mod, 5)
            fold("norm_g_2", SC3, 2)
            V.tensor_scalar(scale1[:, 3, :], mod[:, GA3:GA3 + KD], 1.0, None, ALU.add).then_inc(s_mod, 1)
            lam = vcol[:, VROW["lam_2"]:VROW["lam_2"] + KD]
            L = lambda r: lam_t[:, r, :]
            ls = [0]

            def link(i):
                ls[0] += 1
                i.then_inc(s_lam, 1)
                dve.wait_ge(s_lam, ls[0])

            dve.wait_ge(s_lama, 2)
            link(V.tensor_scalar(L(2), L(1), 1.0, None, ALU.add))
            link(V.tensor_scalar(L(0), L(2), -1.0, 1e-37, ALU.add, ALU.max))
            dve.wait_ge(s_lama, 3)
            link(V.reciprocal(L(6), L(0)))
            link(V.tensor_tensor(L(6), L(6), L(1), ALU.mult))
            link(V.tensor_tensor(L(6), L(6), L(3), ALU.mult))
            link(V.tensor_scalar(L(5), L(0), 1e-30, None, ALU.is_lt))
            link(V.tensor_tensor(L(5), L(5), L(1), ALU.mult))
            link(V.tensor_tensor(L(6), L(6), L(5), ALU.add))
            link(V.tensor_scalar(L(7), lam, -1.0, 0.0, ALU.mult, ALU.max))
            link(V.tensor_tensor(L(6), L(6), L(7), ALU.add))
            link(V.tensor_scalar(L(5), L(6), 8.0, None, ALU.mult))
            link(V.tensor_scalar(L(4), L(6), -8.0, None, ALU.mult))
            assert ls[0] == LAM_STEPS

            dve.wait_ge(s_mod, 7)
            residual(C_DOWN, lambda k: modc(GA2 + k), 3)
            rstd_ready()
            dve.wait_ge(s_res, 2 * KD)
            for k in range(KD):
                V.scalar_tensor_tensor(xT[:, k, :], xT[:, k, :], col("g_final", k), rstd[:], ALU.mult, ALU.mult).then_inc(s_xf, 1)
            dve.wait_ge(s_xf, KD)
            rstd_ready()
            normed(2, SH3)
            V.memset(v_pad[:, :, 0:PADV], 0.0).then_inc(s_v, 1)
            V.memset(l_pad[:, :, 0:PADL], 0.0).then_inc(s_v, 1)
            taps = [(k, tap) for p in range(KD // 2) for tap in range(CONV) for k in (2 * p, 2 * p + 1)]
            taps_done = [0]

            def convolve(count):
                for _ in range(min(count, len(taps) - taps_done[0])):
                    k, tap = taps[taps_done[0]]
                    src, w = v_pad[:, k, tap:tap + T], col("dw_w_2", 8 * tap + k)
                    if tap == 0:
                        dve.wait_ge(s_v, 2 + k + 1)
                        V.tensor_scalar(conv[:, k, :], src, w, col("dw_b_2", k), ALU.mult, ALU.add).then_inc(s_conv, 1)
                    else:
                        dve.wait_ge(s_conv, taps_done[0] - 1)
                        V.scalar_tensor_tensor(conv[:, k, :], src, w, conv[:, k, :], ALU.mult, ALU.add).then_inc(s_conv, 1)
                    taps_done[0] += 1

            for k in range(KD):
                dve.wait_ge(s_sig, 2 + k + 1)
                dve.wait_ge(*((s_wused, C_IN2 + k + 1) if k % 2 else (s_i2acc, k + 2)))
                V.tensor_tensor(v_pad[:, k, PADV:PADV + T], bank[2 + k % 2][:], tmp[k % 2][:], ALU.mult).then_inc(s_v, 1)
                if k % 2:
                    convolve(TAPS_V if k < KD - 1 else TAPS_LX)

            x_steps = [0]

            def short_conv(p):
                for tap in range(SHORT):
                    for k in (2 * p, 2 * p + 1):
                        src = l_pad[:, k, tap:tap + T]
                        if tap == 0:
                            dve.wait_ge(s_gate, k + 1)
                            if p:
                                dve.wait_ge(s_gmm, 2 * (k - 1))
                                dve.wait_ge(s_gx, k - 1)
                            i = V.tensor_scalar(tmp[k % 2][:], src, col("sc_w_2", k), col("sc_b_2", k), ALU.mult, ALU.add)
                        else:
                            dve.wait_ge(s_xs, x_steps[0] - 1)
                            i = V.scalar_tensor_tensor(tmp[k % 2][:], src, col("sc_w_2", 8 * tap + k), tmp[k % 2][:], ALU.mult, ALU.add)
                        i.then_inc(s_xs, 1)
                        x_steps[0] += 1

            dve.wait_ge(s_v, 2 + KD)
            short_conv(0)
            convolve(TAPS_BEFORE)
            for p in range(KD // 2):
                ks = (2 * p, 2 * p + 1)
                convolve(TAPS_A[p])
                for k in ks:
                    dve.wait_ge(s_i, k + 1)
                    dve.wait_ge(s_xs, 2 * SHORT * (p + 1))
                    V.tensor_tensor(tmp[2 + k % 2][:], tmp[2 + k % 2][:], tmp[k % 2][:], ALU.mult).then_inc(s_gx, 1)
                if p < KD // 2 - 1:
                    short_conv(p + 1)
                for k in ks:
                    dve.wait_ge(s_aa, k + 1)
                    V.scalar_tensor_tensor(l_pad[:, k, 0:T], hidden[k % 2][:], 1.0, l_pad[:, k, 0:T], ALU.add, ALU.mult).then_inc(s_m, 1)
                convolve(TAPS_B[p])
                for k in ks:
                    dve.wait_ge(s_mt, k + 1)
                    dve.wait_ge(s_gx, k + 1)
                    V.tensor_tensor(tmp[2 + k % 2][:], tmp[2 + k % 2][:], l_pad[:, k, 0:T], ALU.mult).then_inc(s_bx, 1)
                for k in ks:
                    dve.wait_ge(s_bx, k + 1)
                    V.tensor_tensor_scan(hidden[k % 2][:], decay[k % 2][:], tmp[2 + k % 2][:], 0.0, ALU.mult, ALU.add).then_inc(s_scan, 1)
            convolve(len(taps))
            for t in range(MEAN_AFTER + 1):
                residual_2(C_LRU, 2 * KD, t)
            dve.wait_ge(s_mu, 1)
            for k in range(KD):
                V.tensor_tensor(conv[:, k, :], conv[:, k, :], tmp[2][:], ALU.subtract).then_inc(s_cen, 1)
            for t in range(MEAN_AFTER + 1, VAR_AFTER + 1):
                residual_2(C_LRU, 2 * KD, t)
            dve.wait_ge(s_cen, KD)
            rstd_ready()
            t = VAR_AFTER + 1
            for k in range(KD + 1):
                if k < KD:
                    if k >= 2:
                        dve.wait_ge(s_lns, k - 1)
                    V.scalar_tensor_tensor(tmp[k % 2][:], conv[:, k, :], col("cln_g_2", k), rstd[:], ALU.mult, ALU.mult).then_inc(s_lnu, 1)
                if k >= 1:
                    dve.wait_ge(s_lns, k)
                    V.tensor_copy(ln_hi[:, k - 1, :], tmp[2 + (k - 1) % 2][:]).then_inc(s_lnhi, 1)
                    dve.wait_ge(s_lnhi, k)
                    V.tensor_tensor(ln_lo[:, k - 1, :], tmp[2 + (k - 1) % 2][:], ln_hi[:, k - 1, :].bitcast(F32), ALU.subtract).then_inc(s_lnlo, 1)
                if k in RES_AT:
                    residual_2(C_LRU, 2 * KD, t)
                    t += 1
            for t in range(t, KD):
                residual_2(C_LRU, 2 * KD, t)
            V.memset(nothing[:, 2:3], 0.0).then_inc(s_yc, 4)
            for k in range(KD):
                dve.wait_ge(*((s_wused, C_PW2 + k // 2 + 1) if k % 2 else (s_pacc, k // 2 + 1)))
                if k >= 2:
                    dve.wait_ge(s_yclo, k - 1)
                V.scalar_tensor_tensor(tmp[k % 2][:], bank[k % 4][:], col("pw2_b_2", k), cgate[:, k, :], ALU.add, ALU.mult).then_inc(s_yc, 1)
                dve.wait_ge(s_yc, 4 + k + 1)
                V.tensor_copy(act_hi[:, k, :], tmp[k % 2][:]).then_inc(s_ychi, 1)
                dve.wait_ge(s_ychi, k + 1)
                V.tensor_tensor(act_lo[:, k, :], tmp[k % 2][:], act_hi[:, k, :].bitcast(F32), ALU.subtract).then_inc(s_yclo, 1)
            for t in range(KD):
                residual_2(C_OUT2, 3 * KD, t)
            rstd_ready()
            dve.wait_ge(s_res, 4 * KD)
            for k in range(KD):
                V.scalar_tensor_tensor(xT[:, k, :], xT[:, k, :], col("final_g_2", k), rstd[:], ALU.mult, ALU.mult).then_inc(s_xf, 1)


VROWS = (128, 80, 128, 120)
NCONST = 4
CKV_STEPS = 2 * TT + 1
TOP_STEPS = 3 + (TOPK // 8) * 6 + 6
LAM_STEPS = 12
N_IN_TILES = 22


_INS = ["x", "c", "w_ada", "b_ada", "g_attn", "w_in", "kv_norm_g", "w_uk", "w_uv", "w_out", "g_ffn", "w_gu",
        "w_down", "g_final", "c_2", "norm_g_2", "mod_w_2", "mod_b_2", "w_in_2", "dw_w_2", "dw_b_2", "cln_g_2",
        "cln_b_2", "pw2_w_2", "pw2_b_2", "sc_w_2", "sc_b_2", "wr_2", "br_2", "wi_2", "bi_2", "lam_2", "w_out_2",
        "final_g_2"]
_OUT = (1, T, D)


def kernel(**inputs):
    import numpy as np
    import concourse.bacc as bacc
    from concourse.bass_utils import run_bass_kernel_spmd

    nc = bacc.Bacc("TRN2", target_bir_lowering=False, num_devices=1)
    p, x = np.arange(P)[:, None], np.arange(T)[None, :]
    d = p + (T - P) - x
    held = ((d >= 0) & (d <= 128)).astype(int) + ((d >= 0) & (d % 4 == 0)) + ((d >= 0) & (d % 16 == 0))
    key = np.arange(P)[None, :]
    tables = {
        "dist": d.astype(np.float32),
        "maskA": np.where(held > 0, -np.log(np.maximum(held, 1)), BIG).astype(np.float32),
        "causal": np.stack([np.where(key > p, BIG, 0.0), np.where(key > p, -3.0e38, 3.0e38)], 1).astype(np.float32),
        "ident": np.eye(P, dtype=np.float32),
    }
    arrays, aps = {}, {}
    for name in _INS:
        v = np.ascontiguousarray(inputs[name])
        if v.ndim >= 3:
            v = v.reshape(v.shape[1:])
        elif name not in ("c", "c_2", "kv_norm_g"):
            v = v.reshape(-1)
        if name == "dw_w_2" or name == "sc_w_2":
            v = v.reshape(-1)
        tables[name] = v
    for name, v in tables.items():
        arrays[f"in_{name}"] = v
        aps[name] = nc.dram_tensor(f"in_{name}", v.shape, F32, kind="ExternalInput").ap()
    out = nc.dram_tensor("out_0", (T, D), F32, kind="ExternalOutput").ap()
    build(nc, aps, out)
    r = run_bass_kernel_spmd(nc, [arrays], core_ids=[0])
    return r.results[0]["out_0"].reshape(_OUT)
```

```python
from contextlib import ExitStack

import concourse.bass as bass
from concourse import mybir

F32 = mybir.dt.float32
F32R = mybir.dt.float32r
ALU = mybir.AluOpType
ACT = mybir.ActivationFunctionType

P = 128
T = 512
TT = T // P
D = 1024
KD = D // P
D_FF = 2816
KF = D_FF // P
HD = 64
NH = 8
TOPK = 128
EPS = 1e-6
BIG = 1.0e30
NCOL = 256
CONV = 31
SHORT = 4
PADV, PADL = CONV - 1, SHORT - 1
QSCALE = -(HD ** -0.5)
IDX_SCALE = (8 * 64) ** -0.5

W_IN_COLS = [2304, 2048, 2560, 1536, 1792, 0, 256, 512, 768, 1024, 1280]
N_IN = len(W_IN_COLS)
C_OUT = N_IN
C_GU = C_OUT + 4
C_DOWN = C_GU + 2 * (D_FF // NCOL)
C_IN2 = C_DOWN + 12
C_LRU = C_IN2 + 20
C_PW2 = C_LRU + 4
C_OUT2 = C_PW2 + 4
C_END = C_OUT2 + 4

ADA1, ADA2 = 24, 12
ADA_FIRST = 8
ADA_WINDOW = {0: 3, 1: 3, 2: 3, 3: 0, 4: 2, 5: 2}
ADA_AFTER = {2: 0, 3: 1, 4: 2, 5: 1, 6: 2, 7: 1, 8: 2, 9: 1, 10: 1, 11: 1, 12: 1}
ADA_ATT = ADA_FIRST + sum(ADA_WINDOW.values())
ADA_LOOP = ADA_ATT + 4
ADA_BUF = [0, 1, 2, 4, 5, 6, 7, 8] + [n % 4 for n in range(ADA_ATT - ADA_FIRST)] + [0, 1, 0, 1]

ITEMS = [(kind, h, i) for kind in "AB" for h in range(NH) for i in range(TT)]
PAIRS = [(i, h) for i in range(1, TT) for h in range(NH)]
PAIRS_PER_TILE = 4

ADA_PE = list(range(0, ADA_FIRST, 2))
ADA_ORD = {c: n for n, c in enumerate(c for c in range(ADA1 + ADA2) if c not in ADA_PE)}
ADA_DVE = ADA_ORD[ADA_LOOP]
ADA_ACC = [o % 4 if o < ADA_ORD[ADA_ATT] else o % 2 for o in range(ADA_DVE)]
ADA_ITEMS = KD + 1

LRU_SLOT = 10
MEAN_AFTER, VAR_AFTER, SPREAD_AFTER = 1, 3, 4
LN_CHUNKS = (3,)
RES_AT = (3, 5, 7)
WARM = 4
TAPS_V, TAPS_LX, TAPS_BEFORE = 31, 16, 26
TAPS_A, TAPS_B = (10, 10, 10, 10), (10, 10, 10, 18)

VECS = [("b_ada", 48), ("mod_b_2", 24), ("g_attn", 8), ("g_ffn", 8), ("g_final", 8), ("norm_g_2", 8),
        ("final_g_2", 8), ("cln_g_2", 8), ("cln_b_2", 8), ("pw2_b_2", 8), ("sc_b_2", 8), ("dw_b_2", 8),
        ("br_2", 8), ("bi_2", 8), ("lam_2", 8), ("sc_w_2", 32), ("pad", 48), ("dw_w_2", 248)]
VROW = {}
_at = 0
for _name, _n in VECS:
    VROW[_name] = _at
    _at += _n
NVEC_DMAS = len(VECS) - 1 + 1


def build(nc, a, out):
    with ExitStack() as ctx:
        offset = [nc.sbuf_base + (-nc.sbuf_base) % 64]

        def fixed(name, shape, dt=F32, at=None):
            n = 4
            for s in shape[1:]:
                n *= s
            if at is None:
                at = offset[0]
                offset[0] += (n + 63) // 64 * 64
                assert offset[0] <= nc.sbuf_usable_end, (name, offset[0])
            return nc.alloc_sbuf_tensor_at(name, shape, dt, offset=at), at

        def sem(name):
            return ctx.enter_context(nc.semaphore(name))

        xT, _ = fixed("xT", [P, KD, T])
        act_hi, at_hi = fixed("act_hi", [P, KD, T], F32R)
        act_lo, at_lo = fixed("act_lo", [P, KD, T], F32R)
        w_stage = [fixed(f"w_stage{b}", [P, KD, NCOL])[0] for b in range(2)]
        w_hi = [fixed(f"w_hi{b}", [P, KD, NCOL], F32R)[0] for b in range(2)]
        w_lo = [fixed(f"w_lo{b}", [P, KD, NCOL], F32R)[0] for b in range(2)]
        tmp = [fixed(f"tmp{b}", [P, T])[0] for b in range(4)]
        rstd, _ = fixed("rstd", [P, T])
        ident, _ = fixed("ident_sb", [P, P])
        ones, _ = fixed("ones", [P, P])
        vcol, _ = fixed("vcol", [P, 512])
        mod, _ = fixed("mod", [P, 72])
        scale1, _ = fixed("scale1", [P, 4, KD])
        c_sb, _ = fixed("c_sb", [P, 2, KD])
        c_act, _ = fixed("c_act", [P, 2, KD])
        eps, _ = fixed("eps", [P, 1])
        lam_t, _ = fixed("lam_t", [P, 8, KD])
        wi_sb, _ = fixed("wi_sb", [P, TT, 8])
        negmax, at_negmax = fixed("negmax", [P, 64])
        cols, _ = fixed("norm_columns", [P, 8, TT], at=at_negmax)
        expsum, _ = fixed("expsum", [P, 64])
        expinv, at_expinv = fixed("expinv", [P, 64])
        nothing, _ = fixed("nothing", [P, 8], at=at_expinv)
        ckv_ss, _ = fixed("ckv_ss", [P, 3, TT])
        region = offset[0]

        dist, _ = fixed("dist_sb", [P, T])
        maskA, _ = fixed("maskA_sb", [P, T])
        causal, _ = fixed("causal_sb", [P, 2, P])
        ada_bufs = [fixed(f"ada_stage{b}", [P, KD, NCOL])[0] for b in range(2)]
        ada_acc = [fixed(f"ada_acc{b}", [P, 2, NCOL])[0] for b in range(2)]
        qaT, at_qa = fixed("qaT", [P, 4, T])
        kaT, at_ka = fixed("kaT", [P, 4, T])
        va, at_va = fixed("va", [P, TT, T])
        qbT, at_qb = fixed("qbT", [P, 4, T])
        x_nat, _ = fixed("x_nat", [P, TT, D], at=at_qa)
        at_score = offset[0]
        score = [None] + [fixed(f"score{i}", [P, P * (i + 1)])[0] for i in range(1, TT)]
        work = [None] + [fixed(f"work{i}", [P, P * (i + 1)])[0] for i in range(1, TT)]
        probs = tmp[2:4] + [fixed(f"probs{b}", [P, T], at=at_score + 2048 * b)[0] for b in range(2)]
        top8 = [None] + [fixed(f"top8_{i}", [P, 8])[0] for i in range(1, TT)]
        qiT, at_qi = fixed("qiT", [P, 4, T])
        for b, at in enumerate((at_va, at_ka, at_qb, at_qi, at_hi, at_hi + 4 * KD * NCOL, at_lo), start=2):
            ada_bufs.append(fixed(f"ada_stage{b}", [P, KD, NCOL], at=at)[0])
        ada_stage = [ada_bufs[b] for b in ADA_BUF]
        qlatT = [fixed(f"qlatT{b}", [P, T], at=at_qi + 2048 * b)[0] for b in range(2)]
        olat = [fixed(f"olat{b}", [P, T], at=at_qi + 2048 * (2 + b))[0] for b in range(2)]
        kiT, at_ki = fixed("kiT", [P, T])
        ckv, at_ckv = fixed("ckv", [P, TT, P])
        ckvT, _ = fixed("ckvT", [P, T])
        wuk, _ = fixed("wuk", [P, 4, P])
        wuv, at_wuv = fixed("wuv", [P, NH, HD])
        probsT, at_probsT = map(list, zip(*[fixed(f"probsT{b}", [P, TT, P]) for b in range(2)]))
        ada_acc += [fixed(f"ada_acc{b + 2}", [P, 2, NCOL], at=at_probsT[b])[0] for b in range(2)]
        probsT.append(fixed("probsT2", [P, TT, P], at=at_ki)[0])
        comb, at_comb = zip(*[fixed(f"comb{b}", [P, T]) for b in range(2)])
        relu = [fixed(f"relu{b}", [P, T], at=at_comb[b])[0] for b in range(2)]
        table = [fixed(f"table{b}", [P, T])[0] for b in range(2)]
        kvg, _ = fixed("kvg", [P, P])
        wiT, _ = fixed("wiT", [P, T], at=at_comb[0])
        vrow, _ = fixed("vrow", [P, 4, P], at=at_wuv)

        offset[0] = region
        ff_hi, _ = fixed("ff_hi", [P, KF, T], F32R)
        ff_lo, _ = fixed("ff_lo", [P, KF, T], F32R)
        ada2_stage, _ = fixed("ada2_stage", [P, KD, NCOL])
        ada2_acc, _ = fixed("ada2_acc", [P, NCOL])

        offset[0] = region
        v_pad, at_v = fixed("v_pad", [P, KD, PADV + T])
        l_pad, at_l = fixed("l_pad", [P, KD, PADL + 1 + T])
        conv, at_conv = fixed("conv", [P, KD, T])
        lgate, at_lgate = fixed("lgate", [P, KD, T])
        cgate, _ = fixed("cgate", [P, KD, T])
        wr, _ = fixed("wr_sb", [P, 8, P])
        wi, _ = fixed("wi2_sb", [P, 8, P])
        decay = [fixed(f"decay{m}", [P, T])[0] for m in range(2)]
        hidden = [fixed("hidden0", [P, T])[0], rstd]
        lru_hi, _ = fixed("lru_hi", [P, KD, T], F32R, at=at_lgate)
        lru_lo, _ = fixed("lru_lo", [P, KD, PADL + 1 + T], F32R, at=at_l)
        ln_hi, _ = fixed("ln_hi", [P, KD, T], F32R, at=at_v)
        ln_lo, _ = fixed("ln_lo", [P, KD, T], F32R, at=at_conv)
        o_nat, _ = fixed("o_nat", [P, TT, D], at=at_v)

        bank = [ctx.enter_context(nc.psum_tensor(f"bank{b}", [P, 512], F32)) for b in range(8)]

        def col(name, j):
            c = VROW[name] + j
            return vcol[:, c:c + 1]

        def modc(j):
            return mod[:, j:j + 1]

        SH1, SC1, GA1, SH2, SC2, GA2, SH3, SC3, GA3 = (KD * j for j in range(9))

        s_c = sem("c_loaded")
        s_ident = sem("ident_loaded")
        s_const = sem("constants_loaded")
        s_vec = sem("vector_rows_loaded")
        s_x = sem("x_loaded")
        s_late = sem("head_weights_loaded")
        s_lruw = sem("lru_weights_loaded")
        s_stage = [sem(f"w_stage_loaded{b}") for b in range(2)]
        s_hi = sem("w_hi_ready")
        s_lo = sem("w_lo_ready")
        s_wused = sem("w_used")
        s_ada = [sem(f"ada_loaded{b}") for b in range(9)]
        s_adadir = sem("ada_chunk_by_pe")
        s_adaloop = sem("ada_loop_loaded")
        s_adastep = sem("ada_step")
        s_adaacc = sem("ada_acc_ready")
        s_adamm = sem("ada_acc_used")
        s_mod = sem("mod_ready")
        s_set = sem("dve_set")
        s_cact = sem("c_act_ready")
        s_vt = sem("vectors_turned")
        s_vcol = sem("vcol_ready")
        s_xt = sem("x_turned")
        s_xTr = sem("xT_ready")
        s_sq = sem("squares_ready")
        s_sqused = sem("squares_used")
        s_gsq = sem("gained_squares_ready")
        s_gsqused = sem("gained_squares_added")
        s_col = sem("column_sums_ready")
        s_mq = sem("second_mean_square_ready")
        s_diag = sem("diagonal_ready")
        s_diag1 = sem("second_diagonal_ready")
        s_spread = sem("rstd_spread")
        s_spread1 = sem("second_rstd_spread")
        s_colstep = sem("column_step")
        s_csum = sem("conv_added_up")
        s_sd = sem("deviation_ready")
        s_u = sem("scaled_ready")
        s_ahi = sem("act_hi_ready")
        s_alo = sem("act_lo_ready")
        s_acc = sem("in_acc_ready")
        s_free = sem("in_acc_free")
        s_ckv = sem("ckv_steps")
        s_ckvsd = sem("ckv_deviation")
        s_ckvt = sem("ckv_turned")
        s_ckvn = sem("ckv_by_token")
        s_ckvT = sem("ckvT_ready")
        s_wiT = sem("indexer_weights_turned")
        s_wi = sem("indexer_weights_ready")
        s_lg = sem("logits_ready")
        s_relu = sem("relu_ready")
        s_score = sem("score_added")
        s_top = sem("topk_step")
        s_tab = sem("table_ready")
        s_tabm = sem("table_made")
        s_comb = sem("comb_ready")
        s_s = sem("scores_ready")
        s_min = sem("min_ready")
        s_exp = sem("exp_ready")
        s_inv = sem("expinv_ready")
        s_norm = sem("probs_ready")
        s_t = sem("probs_turned")
        s_pt = sem("probsT_ready")
        s_pv = sem("pv_done")
        s_ql = sem("qlat_ready")
        s_qlT = sem("qlatT_copied")
        s_oh = sem("olat_copied")
        s_uv = sem("uv_done")
        s_mhi = sem("mixed_hi_ready")
        s_mlo = sem("mixed_lo_ready")
        s_racc = sem("residual_acc_ready")
        s_res = sem("residual_added")
        s_guacc = sem("gu_acc_ready")
        s_silu = sem("silu_ready")
        s_up = sem("up_ready")
        s_ffhi = sem("ff_hi_ready")
        s_fflo = sem("ff_lo_ready")
        s_x1 = sem("first_block_done")
        s_xf = sem("x_normed")
        s_i2acc = sem("in2_acc_ready")
        s_sig = sem("sigmoid_ready")
        s_v = sem("v_ready")
        s_gate = sem("gates_copied")
        s_conv = sem("conv_step")
        s_xs = sem("short_conv_step")
        s_gmm = sem("lru_gate_products")
        s_r = sem("r_ready")
        s_i = sem("i_ready")
        s_gx = sem("gated_ready")
        s_a = sem("decay_ready")
        s_th = sem("tanh_ready")
        s_aa = sem("decay_squared")
        s_m = sem("mult_squared")
        s_bx = sem("scan_input_ready")
        s_y = sem("y_lru_ready")
        s_mt = sem("mult_ready")
        s_scan = sem("scan_done")
        s_lhi = sem("lru_hi_ready")
        s_llo = sem("lru_lo_ready")
        s_mean = sem("mean_sum")
        s_mu = sem("mean_ready")
        s_cen = sem("centred")
        s_lnu = sem("ln_scaled")
        s_lns = sem("ln_silu")
        s_lnhi = sem("ln_hi_ready")
        s_lnlo = sem("ln_lo_ready")
        s_pacc = sem("pw2_acc_ready")
        s_yc = sem("y_conv_ready")
        s_ychi = sem("yc_hi_ready")
        s_yclo = sem("yc_lo_ready")
        s_lam = sem("lam_step")
        s_lama = sem("lam_act")
        s_ot = sem("out_turned")
        s_on = sem("out_copied")
        s_out = sem("out_stored")

        block = ctx.enter_context(nc.Block())

        def ada_use(c):
            return ADA_BUF[:c + 1].count(ADA_BUF[c])

        def ada_wait(engine, c):
            engine.wait_ge(s_ada[ADA_BUF[c]], 16 * ada_use(c))

        def w_cols(w, k0, kn, c0):
            return w.rearrange("(k p) c -> p k c", p=P)[:, k0:k0 + kn, bass.ds(c0, NCOL)]

        @block.sync
        def _(sp):
            def w_dma(n, src, half=None):
                b = n % 2 if half is None else half[0]
                if half is None:
                    if n >= 2:
                        sp.wait_ge(s_lo, n - 1)
                else:
                    sp.wait_ge(s_lo, n - 1)
                kn, cn = src.shape[1], src.shape[2]
                sp.dma_start(w_stage[b][:, 0:kn, 0:cn], src).then_inc(s_stage[b], 16)

            def ada_dma(c):
                if ada_use(c) > 1:
                    last = max(o for o in range(c) if ADA_BUF[o] == ADA_BUF[c])
                    if last in ADA_PE:
                        sp.wait_ge(s_adadir, ADA_PE.index(last) + 1)
                    else:
                        sp.wait_ge(s_adaacc, ADA_ORD[last] + 1)
                elif ADA_BUF[c] == 3:
                    sp.wait_ge(s_xt, KD)
                w, j = (a["w_ada"], c) if c < ADA1 else (a["mod_w_2"], c - ADA1)
                src = w.rearrange("(p t) c -> p t c", t=KD)[:, :, j * NCOL:(j + 1) * NCOL]
                sp.dma_start(ada_stage[c][:], src).then_inc(s_ada[ADA_BUF[c]], 16)

            sp.dma_start(c_sb[:, 0, :], a["c"].rearrange("o (p t) -> (o p) t", t=KD)).then_inc(s_c, 16)
            sp.dma_start(c_sb[:, 1, :], a["c_2"].rearrange("o (p t) -> (o p) t", t=KD)).then_inc(s_c, 16)
            for c in range(3):
                ada_dma(c)
            sp.dma_start(ident[:], a["ident"]).then_inc(s_ident, 16)
            for t in range(TT):
                sp.dma_start(x_nat[:, t, :], a["x"][t * P:(t + 1) * P, :]).then_inc(s_x, 16)
            nvec = 0
            for name, n in VECS:
                if name == "pad":
                    continue
                src = a[name].rearrange("(r c) -> r c", c=P)
                r0, done = VROW[name], 0
                while done < n:
                    tile, row = divmod(r0 + done, P)
                    m = min(n - done, P - row)
                    sp.dma_start(vrow[row:row + m, tile, :], src[done:done + m, :]).then_inc(s_vec, 16)
                    nvec += 1
                    done += m
            assert nvec == NVEC_DMAS, nvec
            for c in range(3, ADA_FIRST - 2):
                ada_dma(c)

            def w_in_dma(n):
                c0 = W_IN_COLS[n]
                cn = min(NCOL, a["w_in"].shape[1] - c0)
                w_dma(n, a["w_in"].rearrange("(k p) c -> p k c", p=P)[:, :, c0:c0 + cn])

            w_in_dma(0)
            ada_dma(ADA_FIRST - 2)
            ada_dma(ADA_FIRST - 1)
            w_in_dma(1)
            ada_dma(ADA_FIRST)
            ada_dma(ADA_FIRST + 1)
            sp.dma_start(dist[:], a["dist"]).then_inc(s_const, 16)
            sp.dma_start(maskA[:], a["maskA"]).then_inc(s_const, 16)
            sp.dma_start(causal[:], a["causal"]).then_inc(s_const, 16)
            sp.dma_start(kvg[:], a["kv_norm_g"].to_broadcast([P, P])).then_inc(s_const, 16)
            ada_dma(ADA_FIRST + 2)
            ada_dma(ADA_FIRST + 3)
            c = ADA_FIRST + 4
            w_in_dma(2)
            w_in_dma(3)
            for n in range(N_IN - 4):
                if n < len(ADA_WINDOW) - 1:
                    end = ADA_FIRST + sum(ADA_WINDOW[m] for m in range(n + 2))
                    for c in range(c, end):
                        ada_dma(c)
                    c = end
                if n == 3:
                    sp.wait_ge(s_vt, 1)
                    sp.dma_start(wuk[:], a["w_uk"].rearrange("(g e) d r -> (e d) g r", e=2)).then_inc(s_late, 16)
                    sp.dma_start(wuv[:], a["w_uv"].rearrange("h r d -> r h d")).then_inc(s_late, 16)
                w_in_dma(n + 4)
            w_dma(C_OUT, w_cols(a["w_out"], 0, KD, 0))
            w_dma(C_OUT + 1, w_cols(a["w_out"], 0, KD, NCOL))
            for c in range(ADA_ATT, ADA_LOOP):
                ada_dma(c)
            w_dma(C_OUT + 2, w_cols(a["w_out"], 0, KD, 2 * NCOL))
            w_dma(C_OUT + 3, w_cols(a["w_out"], 0, KD, 3 * NCOL))

            def stream(n0, steps, srcs, first=0):
                per = len(srcs)
                with sp.Fori(first, first + steps) as j:
                    for q, src in enumerate(srcs):
                        w_dma(j * per + (n0 + q - first * per), src(j), half=((n0 + q) % 2,))

            sp.wait_ge(s_res, 1)
            with sp.Fori(2, KF // 2 + 2) as j:
                w_dma(j * 2 + (C_GU - 4), w_cols(a["w_gu"], 0, KD, j * NCOL - 2 * NCOL), half=(C_GU % 2,))
                w_dma(j * 2 + (C_GU - 3), w_cols(a["w_gu"], 0, KD, j * NCOL + (D_FF - 2 * NCOL)), half=((C_GU + 1) % 2,))
                sp.wait_ge(s_adaacc, j + (ADA_DVE - 2))
                sp.dma_start(ada2_stage[:], a["mod_w_2"].rearrange("(p t) c -> p t c", t=KD)[
                    :, :, bass.ds(j * NCOL + (ADA_LOOP - ADA1 - 2) * NCOL, NCOL)]).then_inc(s_adaloop, 16)
            groups = [(0, 8), (8, 8), (16, 6)]
            stream(C_DOWN, 2, [lambda j, m=m, g=g: w_cols(a["w_down"], g[0], g[1], j * 2 * NCOL + m * NCOL)
                               for m in range(2) for g in groups])
            stream(C_IN2, 4, [lambda j: w_cols(a["w_in_2"], 0, KD, j * NCOL + (D - NCOL)),
                              lambda j: w_cols(a["w_in_2"], 0, KD, j * NCOL - NCOL)], first=1)
            for g in range(2):
                if g == 0:
                    sp.wait_ge(s_res, 2 * KD)
                sp.dma_start((wr, wi)[g][:], a[("wr_2", "wi_2")[g]].rearrange("h d e -> d h e")).then_inc(s_lruw, 16)
            for part in (3, 4, 2):
                n0 = C_IN2 + 8 + 4 * (3, 4, 2).index(part)
                stream(n0, 2, [lambda j, q=q, part=part: w_cols(a["w_in_2"], 0, KD, j * 2 * NCOL + part * D + q * NCOL)
                               for q in range(2)])
            stream(C_LRU, 2, [lambda j, q=q: w_cols(a["w_out_2"], KD, KD, j * 2 * NCOL + q * NCOL) for q in range(2)])
            stream(C_PW2, 2, [lambda j, q=q: w_cols(a["pw2_w_2"], 0, KD, j * 2 * NCOL + q * NCOL) for q in range(2)])
            stream(C_OUT2, 2, [lambda j, q=q: w_cols(a["w_out_2"], 0, KD, j * 2 * NCOL + q * NCOL) for q in range(2)])

            for s in range(2 * TT):
                half, t = divmod(s, TT)
                cols = slice(half * D // 2, (half + 1) * D // 2)
                sp.wait_ge(s_on, s + 1)
                sp.dma_start(out[t * P:(t + 1) * P, cols], o_nat[:, t, cols]).then_inc(s_out, 16)
            sp.wait_ge(s_out, 16 * 2 * TT)

        @block.gpsimd
        def _(pool):
            def lo(n, b):
                pool.wait_ge(s_hi, n + 1)
                nc.gpsimd.tensor_tensor(w_lo[b][:], w_stage[b][:], w_hi[b][:].bitcast(F32),
                                        ALU.subtract).then_inc(s_lo, 1)


            slopes = [2.0 ** (-8.0 * (g + 1.0) / 16) for g in range(16)]

            def make_table(g):
                kind, h = g // NH, g % NH
                if g >= 2:
                    if g - 2 < NH:
                        pool.wait_ge(s_min, TT * (g - 1))
                    else:
                        pool.wait_ge(s_comb, TT * (g - 2 - NH + 1))
                m = nc.gpsimd.tensor_scalar(table[g % 2][:], dist[:], float(slopes[2 * h + kind]), 0.0, ALU.mult, ALU.add)
                if kind == 0:
                    m.then_inc(s_tabm, 1)
                    pool.wait_ge(s_tabm, h + 1)
                    m = nc.gpsimd.tensor_tensor(table[g % 2][:], table[g % 2][:], maskA[:], ALU.add)
                m.then_inc(s_tab, 1)

            for n in range(C_OUT + 2):
                lo(n, n % 2)
                if n == 5:
                    pool.wait_ge(s_const, 16 * NCONST)
                    make_table(0)
                    make_table(1)
            for g in range(2, NH):
                make_table(g)
            for h in range(NH):
                make_table(NH + h)
                pool.wait_ge(s_tab, NH + h + 1)
                for i in range(TT):
                    s, n = TT * h + i, P * (i + 1)
                    if s == 0:
                        pool.wait_ge(s_top, TOP_STEPS)
                    if s >= 2:
                        pool.wait_ge(s_min, TT * NH + s - 1)
                    t = table[h % 2][:, T - n:T]
                    if i == 0:
                        nc.gpsimd.tensor_tensor(comb[s % 2][:, 0:n], t, causal[:, 0, :], ALU.add).then_inc(s_comb, 1)
                    else:
                        nc.gpsimd.tensor_tensor(comb[s % 2][:, 0:n], t, work[i][:], ALU.add).then_inc(s_comb, 1)
            lo(C_OUT + 2, (C_OUT + 2) % 2)
            lo(C_OUT + 3, (C_OUT + 3) % 2)

            def lo_loop(n0, n1):
                with pool.Fori(0, (n1 - n0) // 2) as j:
                    for q in range(2):
                        lo(j * 2 + (n0 + q), (n0 + q) % 2)
                if (n1 - n0) % 2:
                    lo(n1 - 1, (n1 - 1) % 2)

            first_y = C_IN2 + LRU_SLOT + 4
            lo_loop(C_GU, first_y)
            for p in range(KD // 2):
                n = first_y + 2 * p
                for k in (2 * p, 2 * p + 1):
                    pool.wait_ge(s_scan, k + 1)
                    pool.wait_ge(s_gate, KD + k + 1)
                    nc.gpsimd.tensor_tensor(hidden[k % 2][:], hidden[k % 2][:], lgate[:, k, :], ALU.mult).then_inc(s_y, 1)
                lo(n, n % 2)
                for k in (2 * p, 2 * p + 1):
                    pool.wait_ge(s_lhi, k + 1)
                    nc.gpsimd.tensor_tensor(lru_lo[:, k, 0:T], hidden[k % 2][:], lru_hi[:, k, :].bitcast(F32),
                                            ALU.subtract).then_inc(s_llo, 1)
                if p < KD // 2 - 1:
                    lo(n + 1, (n + 1) % 2)
            lo_loop(first_y + KD - 1, C_END)

        @block.tensor
        def _(pe):
            def chunk_ready(n):
                pe.wait_ge(s_lo, n + 1)

            def normed_parts(j, k):
                pe.wait_ge(s_alo, KD * j + k + 1)

            def tile(dst, b, cols, n_k, rhs_hi, rhs_lo, first=True, last=True, wait=None):
                for k in range(n_k):
                    if wait:
                        wait(k)
                    wh, wl = w_hi[b][:, k, cols], w_lo[b][:, k, cols]
                    pe.matmul(dst, wh, rhs_hi(k), start=(first and k == 0), stop=False)
                    pe.matmul(dst, wh, rhs_lo(k), start=False, stop=False)
                    mm = pe.matmul(dst, wl, rhs_hi(k), start=False, stop=(last and k == n_k - 1))
                return mm

            def abreast(tiles, j):
                for k in range(KD):
                    normed_parts(j, k)
                    for dst, b, cols, ready in tiles:
                        wh, wl = w_hi[b][:, k, cols], w_lo[b][:, k, cols]
                        pe.matmul(dst, wh, act_hi[:, k, :], start=(k == 0), stop=False)
                        pe.matmul(dst, wh, act_lo[:, k, :], start=False, stop=False)
                        mm = pe.matmul(dst, wl, act_hi[:, k, :], start=False, stop=(k == KD - 1))
                        if k == KD - 1:
                            mm.then_inc(ready, 1)

            def tile_tokens(dst, b, cols, t, wait=None):
                ts = slice(t * P, (t + 1) * P)
                for k in range(KD):
                    if wait:
                        wait(k)
                    ah, al = act_hi[:, k, ts], act_lo[:, k, ts]
                    pe.matmul(dst, ah, w_hi[b][:, k, cols], start=(k == 0), stop=False)
                    pe.matmul(dst, ah, w_lo[b][:, k, cols], start=False, stop=False)
                    mm = pe.matmul(dst, al, w_hi[b][:, k, cols], start=False, stop=(k == KD - 1))
                return mm

            norms = [0]

            def column_sums(more=None):
                norms[0] += 1
                pe.wait_ge(s_sqused, (KD - 1) * norms[0])
                if more is not None:
                    pe.wait_ge(s_gsqused, KD - 1)
                for g, src in enumerate((rstd, more) if more is not None else (rstd,)):
                    for t in range(TT):
                        mm = pe.matmul(bank[4][:, g * TT + t:g * TT + t + 1], src[:, t * P:(t + 1) * P], ones[:, 0:1],
                                       start=True, stop=True)
                mm.then_inc(s_col, 1)
                if norms[0] > 1:
                    keep_warm(WARM // 2)

            def keep_warm(count):
                for _ in range(count):
                    pe.matmul(bank[6][:, 0:P], ones[:], ones[:], start=True, stop=True)

            def spread(more=None):
                pe.wait_ge(s_diag, TT * norms[0])
                mm = pe.matmul(bank[4][:], ones[:], rstd[:], start=True, stop=True).then_inc(s_spread, 1)
                if more is not None:
                    pe.wait_ge(s_diag1, TT)
                    pe.matmul(bank[5][:], ones[:], more[:], start=True, stop=True).then_inc(s_spread1, 1)
                if norms[0] > 1:
                    keep_warm(WARM)

            def ada_products(c, bank=bank[7]):
                o = ADA_ORD[c]
                pe.wait_ge(s_adaacc, o + 1)
                for m in range(2):
                    mm = pe.matmul(bank[:, 2 * c + m:2 * c + m + 1],
                                   ada_acc[ADA_ACC[o]][:, 0, m * P:(m + 1) * P], ones[:, 0:1], start=True, stop=True)
                mm.then_inc(s_adamm, 1)

            def ada_direct(c):
                ada_wait(pe, c)
                pe.wait_ge(s_cact, 1)
                for m in range(2):
                    for t in range(KD):
                        mm = pe.matmul(bank[7][:, 2 * c + m:2 * c + m + 1], ada_stage[c][:, t, m * P:(m + 1) * P],
                                       c_act[:, 0, t:t + 1], start=(t == 0), stop=(t == KD - 1))
                mm.then_inc(s_adadir, 1)

            ada_direct(0)
            ada_direct(2)
            pe.wait_ge(s_set, 2)
            pe.wait_ge(s_ident, 16)
            pe.wait_ge(s_vec, 16 * NVEC_DMAS)
            for q, rows in enumerate(VROWS):
                mm = pe.transpose(bank[4][:, q * P:q * P + rows], vrow[0:rows, q, :], ident[0:rows, 0:rows])
            mm.then_inc(s_vt, 1)
            pe.wait_ge(s_x, 16 * TT)
            for k in range(KD):
                if k >= 4:
                    pe.wait_ge(s_xTr, k - 3)
                for t in range(TT):
                    mm = pe.transpose(bank[k % 4][:, t * P:(t + 1) * P], x_nat[:, t, k * P:(k + 1) * P], ident[:])
                mm.then_inc(s_xt, 1)

            ada_products(1)
            ada_direct(4)
            ada_products(3)
            ada_direct(6)
            pe.wait_ge(s_vcol, 2)
            column_sums()
            ada_products(5)
            ada_products(7)
            spread()

            hi = lambda k: act_hi[:, k, :]
            lo = lambda k: act_lo[:, k, :]
            t_acc = [0]

            def acc_bank():
                if t_acc[0] >= 4:
                    pe.wait_ge(s_free, t_acc[0] - 3 + (t_acc[0] - 4 >= 5))
                b = bank[t_acc[0] % 4]
                t_acc[0] += 1
                return b

            pairs = list(enumerate(PAIRS))

            def logits():
                for _ in range(PAIRS_PER_TILE):
                    if not pairs:
                        return
                    s, (i, h) = pairs.pop(0)
                    if s == 0:
                        pe.wait_ge(s_free, 7)
                        pe.wait_ge(s_wi, 1)
                    if s >= 2:
                        pe.wait_ge(s_relu, s - 1)
                    half = slice(HD * (h % 2), HD * (h % 2) + HD)
                    n = P * (i + 1)
                    pe.matmul(bank[4 + s % 2][:, 0:n], qiT[half, h // 2, i * P:(i + 1) * P], kiT[half, 0:n],
                              start=True, stop=True).then_inc(s_lg, 1)

            ada_at = [ADA_FIRST]

            def ada_next(count):
                for _ in range(count):
                    ada_products(ada_at[0])
                    ada_at[0] += 1

            for n in range(N_IN):
                chunk_ready(n)
                b = n % 2
                if n == 0:
                    chunk_ready(1)
                    dst = [acc_bank()[:] for _ in range(3)]
                    abreast([(dst[0], 0, slice(0, P), s_acc), (dst[1], 0, slice(P, 2 * P), s_wused),
                             (dst[2], 1, slice(P, 2 * P), s_acc)], 0)
                elif n == 1:
                    tile(acc_bank()[:], b, slice(0, P), KD, hi, lo).then_inc(s_wused, 1)
                    ada_next(ADA_AFTER[3])
                elif n >= 9:
                    for tp in range(2):
                        dst = acc_bank()
                        for t in (2 * tp, 2 * tp + 1):
                            mm = tile_tokens(dst[:, (t % 2) * NCOL:(t % 2 + 1) * NCOL], b, slice(0, NCOL), t)
                        mm.then_inc((s_acc, s_wused)[tp], 1)
                else:
                    for m in range(2):
                        tile(acc_bank()[:], b, slice(m * P, (m + 1) * P), KD, hi, lo).then_inc((s_acc, s_wused)[m], 1)
                        ada_next(ADA_AFTER.get(t_acc[0] - 1, 0))
                        if (n, m) == (2, 0):
                            pe.wait_ge(s_free, 4)
                            for t in range(TT):
                                mm = pe.transpose(bank[6][:, t * P:(t + 1) * P], ckvT[:, t * P:(t + 1) * P], ident[:])
                            mm.then_inc(s_ckvt, 1)
                        if (n, m) == (3, 0):
                            pe.wait_ge(s_free, 7)
                            for t in range(TT):
                                mm = pe.transpose(bank[5][:, t * 8:(t + 1) * 8], wiT[HD:HD + 8, t * P:(t + 1) * P],
                                                  ident[HD:HD + 8, HD:HD + 8])
                            mm.then_inc(s_wiT, 1)
                        if n >= 3:
                            logits()
                        if (n, m) == (5, 1):
                            pe.wait_ge(s_ckv, CKV_STEPS)
                            for t in range(TT):
                                mm = pe.transpose(bank[6][:, t * P:(t + 1) * P], ckv[:, t, :], ident[:])
                            mm.then_inc(s_ckvt, 1)
            assert not pairs and t_acc[0] == N_IN_TILES

            pe.wait_ge(s_free, N_IN_TILES + 1)
            pe.wait_ge(s_ckvT, 1)
            pe.wait_ge(s_late, 32)
            n_items = len(ITEMS)
            O_BANK, T_BANK = (7, 1), (6, 0)

            def q_lat(h):
                half = slice(HD * (h % 2), HD * (h % 2) + HD)
                if h >= 1:
                    pe.wait_ge(s_qlT, h)
                pe.matmul(bank[2][:], wuk[half, h // 2, :], qbT[half, h // 2, :], start=True, stop=True).then_inc(s_ql, 1)

            def scores(s):
                kind, h, i = ITEMS[s]
                n = P * (i + 1)
                if s >= 2:
                    pe.wait_ge(s_min, s - 1)
                qs = slice(i * P, (i + 1) * P)
                if kind == "A":
                    half = slice(HD * (h % 2), HD * (h % 2) + HD)
                    lhs, rhs = qaT[half, h // 2, qs], kaT[half, h // 2, 0:n]
                else:
                    pe.wait_ge(s_qlT, h + 1)
                    lhs, rhs = qlatT[h % 2][:, qs], ckvT[:, 0:n]
                pe.matmul(bank[4 + s % 2][:, 0:n], lhs, rhs, start=True, stop=True).then_inc(s_s, 1)

            def turn(s):
                i = ITEMS[s][2]
                pe.wait_ge(s_norm, s + 1)
                if s >= 2:
                    pe.wait_ge(s_pt, s - 1)
                for kb in range(i + 1):
                    mm = pe.transpose(bank[T_BANK[s % 2]][:, kb * P:(kb + 1) * P], probs[s % 4][:, kb * P:(kb + 1) * P], ident[:])
                mm.then_inc(s_t, 1)

            def weigh(s):
                kind, h, i = ITEMS[s]
                g = s // TT
                pe.wait_ge(s_pt, s + 1)
                if i == 0 and g >= 2:
                    if g - 2 < NH:
                        pe.wait_ge(s_mlo, g - 1)
                    else:
                        pe.wait_ge(s_oh, g - 1 - NH)
                qs = slice(i * P, (i + 1) * P)
                o = bank[O_BANK[g % 2]]
                for kb in range(i + 1):
                    if kind == "A":
                        half = slice(HD * (h % 2), HD * (h % 2) + HD)
                        lhs, dst = va[:, kb, h * HD:(h + 1) * HD], o[half, qs]
                    else:
                        lhs, dst = ckv[:, kb, :], o[:, qs]
                    mm = pe.matmul(dst, lhs, probsT[s % 3][:, kb, :], start=(kb == 0), stop=(kb == i))
                mm.then_inc(s_pv, 1)

            def up_v(h):
                half = slice(HD * (h % 2), HD * (h % 2) + HD)
                pe.wait_ge(s_oh, h + 1)
                if h == 0:
                    pe.wait_ge(s_mod, 5)
                if h >= 1:
                    pe.wait_ge(s_mlo, NH + h)
                pe.matmul(bank[3][half, :], wuv[:, h, :], olat[h % 2][:], start=True, stop=True).then_inc(s_uv, 1)

            def first_out(k):
                if k == 0:
                    pe.wait_ge(s_qlT, NH)
                    pe.wait_ge(s_lo, C_OUT + 1)
                b, cols = C_OUT % 2, slice(0, P)
                pe.wait_ge(s_mlo, 2 * (k + 1))
                pe.matmul(bank[2][:], w_hi[b][:, k, cols], act_hi[:, k, :], start=(k == 0), stop=False)
                pe.matmul(bank[2][:], w_hi[b][:, k, cols], act_lo[:, k, :], start=False, stop=False)
                mm = pe.matmul(bank[2][:], w_lo[b][:, k, cols], act_hi[:, k, :], start=False, stop=(k == KD - 1))
                if k == KD - 1:
                    mm.then_inc(s_racc, 1)

            assert ada_at[0] == ADA_ATT
            pe.wait_ge(s_mod, 3)
            for s in range(n_items + 10):
                if s < n_items:
                    kind, h, i = ITEMS[s]
                    if s + 2 < n_items and ITEMS[s + 2][0] == "B" and ITEMS[s + 2][2] == 0:
                        q_lat(ITEMS[s + 2][1])
                    scores(s)
                if s >= ADA_ITEMS + 2 and (s - 2) % ADA_ITEMS == 0 and ada_at[0] < ADA_LOOP:
                    ada_products(ada_at[0], bank[3])
                    ada_at[0] += 1
                if 3 <= s < n_items + 3:
                    turn(s - 3)
                if 5 <= s < n_items + 5:
                    weigh(s - 5)
                if s >= 8 and s - 8 < n_items and ITEMS[s - 8][0] == "B" and ITEMS[s - 8][2] == TT - 1:
                    up_v(ITEMS[s - 8][1])
                if n_items <= s < n_items + KD - 1:
                    first_out(s - n_items)

            def project(n0, steps, ready, rhs_hi, rhs_lo, waits=None, groups=((0, KD),), pairs=1, t0=0):
                with pe.Fori(0, steps) as j:
                    n = 0
                    for m2 in range(pairs):
                        base = 2 * (m2 % 2) if pairs > 1 else 0
                        for g, (k0, kn) in enumerate(groups):
                            b = (n0 + n) % 2
                            pe.wait_ge(s_lo, j * (pairs * len(groups)) + (n0 + n + 1))
                            for m in range(2):
                                if g == 0 and waits:
                                    waits(j, 2 * m2 + m)
                                mm = tile(bank[base + m][:], b, slice(m * P, (m + 1) * P), kn,
                                          lambda k, k0=k0: rhs_hi(k0 + k), lambda k, k0=k0: rhs_lo(k0 + k),
                                          first=(g == 0), last=(g == len(groups) - 1))
                                if m == 1:
                                    mm.then_inc(s_wused, 1)
                                elif g == len(groups) - 1:
                                    mm.then_inc(ready, 1)
                            n += 1

            pe.wait_ge(s_mlo, 2 * NH)
            RES = [0]

            def residual(n0, rhs_hi, rhs_lo, groups=((0, KD),)):
                r0 = RES[0]
                RES[0] += KD

                def waits(j, t):
                    pe.wait_ge(s_res, j * 4 + (r0 + t - 3))

                if r0:
                    project(n0, 2, s_racc, rhs_hi, rhs_lo, waits, groups, pairs=2)
                else:
                    first_out(KD - 1)
                    for t in range(1, KD):
                        n = n0 + t // 2
                        if t % 2 == 0:
                            pe.wait_ge(s_lo, n + 1)
                        if t >= 4:
                            pe.wait_ge(s_res, t - 3)
                        tile(bank[(t + 2) % 4][:], n % 2, slice((t % 2) * P, (t % 2 + 1) * P), KD, rhs_hi, rhs_lo).then_inc((s_racc, s_wused)[t % 2], 1)

            residual(C_OUT, hi, lo)
            column_sums()
            spread()
            pe.wait_ge(s_res, KD)

            def gu_modulations(j):
                pe.wait_ge(s_adaacc, j + (ADA_DVE + 1))
                for m in range(2):
                    mm = pe.matmul(bank[5][:, bass.ds(j * 2 + m, 1)], ada2_acc[:, m * P:(m + 1) * P], ones[:, 0:1],
                                   start=True, stop=True)
                mm.then_inc(s_adamm, 1)

            b0, b1 = C_GU % 2, (C_GU + 1) % 2
            low, high = slice(0, P), slice(P, 2 * P)
            pe.wait_ge(s_lo, C_GU + 2)
            abreast([(bank[0][:], b0, low, s_guacc), (bank[1][:], b0, high, s_wused), (bank[2][:], b1, low, s_guacc)], 1)
            tile(bank[3][:], b1, high, KD, hi, lo).then_inc(s_wused, 1)
            gu_modulations(0)
            with pe.Fori(1, KF // 2) as j:
                for q in range(2):
                    b = (C_GU + q) % 2
                    pe.wait_ge(s_lo, j * 2 + (C_GU + q + 1))
                    for m in range(2):
                        pe.wait_ge((s_silu, s_up)[q], j * 2 + (1 + m))
                        tile(bank[2 * q + m][:], b, slice(m * P, (m + 1) * P), KD, hi, lo).then_inc((s_guacc, s_wused)[m], 1)
                gu_modulations(j)
            pe.wait_ge(s_silu, 2 + KF)
            pe.wait_ge(s_up, 2 + KF)
            pe.wait_ge(s_fflo, 2 + KF)
            residual(C_DOWN, lambda k: ff_hi[:, k, :], lambda k: ff_lo[:, k, :], ((0, 8), (8, 8), (16, 6)))
            column_sums(tmp[2])
            spread(tmp[2])
            pe.wait_ge(s_res, 2 * KD)
            b0, b1 = C_IN2 % 2, (C_IN2 + 1) % 2
            pe.wait_ge(s_lo, C_IN2 + 2)
            abreast([(bank[0][:], b0, low, s_i2acc), (bank[1][:], b0, high, s_wused), (bank[2][:], b1, low, s_i2acc)], 2)
            tile(bank[3][:], b1, high, KD, hi, lo).then_inc(s_wused, 1)
            with pe.Fori(1, KD // 2) as j:
                for q in range(2):
                    b = (C_IN2 + q) % 2
                    pe.wait_ge(s_lo, j * 2 + (C_IN2 + q + 1))
                    for m in range(2):
                        pe.wait_ge((s_sig, s_v)[q], j * 2 + (1 + m))
                        tile(bank[2 * q + m][:], b, slice(m * P, (m + 1) * P), KD, hi, lo).then_inc((s_i2acc, s_wused)[m], 1)
            pe.wait_ge(s_lruw, 32)
            for slot in range(KD, C_LRU - C_IN2):
                n = C_IN2 + slot
                pe.wait_ge(s_lo, n + 1)
                for m in range(2):
                    t = 2 * (slot - KD) + m
                    if t >= 4:
                        pe.wait_ge(s_gate, t - 3)
                    else:
                        pe.wait_ge((s_sig, s_v)[t // 2], 2 + KD)
                    tile(bank[t % 4][:], n % 2, slice(m * P, (m + 1) * P), KD, hi, lo).then_inc((s_i2acc, s_wused)[m], 1)
                p, odd = divmod(slot - LRU_SLOT, 2)
                if 0 <= p < KD // 2 and not odd:
                    pe.wait_ge(s_xs, 2 * SHORT * (p + 1))
                    for k in (2 * p, 2 * p + 1):
                        for g in range(2):
                            if p:
                                pe.wait_ge((s_r, s_i)[g], k - 1)
                            pe.matmul(bank[4 + 2 * (k % 2) + g][:], (wr, wi)[g][:, k, :], tmp[k % 2][:],
                                      start=True, stop=True).then_inc(s_gmm, 1)

            def residual_tile(n0, t, rhs_hi, rhs_lo, free, ready):
                n = n0 + t // 2
                if t % 2 == 0:
                    pe.wait_ge(s_lo, n + 1)
                free(t)
                tile(bank[t % 4][:], n % 2, slice((t % 2) * P, (t % 2 + 1) * P), KD, rhs_hi, rhs_lo,
                     wait=ready if t == 0 else None).then_inc((s_racc, s_wused)[t % 2], 1)

            def lru_ready(k):
                pe.wait_ge(s_lhi, k + 1)
                pe.wait_ge(s_llo, k + 1)

            for t in range(KD):
                residual_tile(C_LRU, t, lambda k: lru_hi[:, k, :], lambda k: lru_lo[:, k, 0:T],
                              lambda t: pe.wait_ge(*((s_gate, 3 * KD - 3 + t) if t < 4 else (s_res, 2 * KD + t - 3))),
                              lru_ready)
                if t == MEAN_AFTER:
                    pe.wait_ge(s_csum, KD - 1)
                    pe.wait_ge(s_r, KD)
                    pe.wait_ge(s_i, KD)
                    pe.matmul(bank[5][:], ones[:], tmp[3][:], start=True, stop=True).then_inc(s_mean, 1)
                if t == VAR_AFTER:
                    column_sums()
                if t == SPREAD_AFTER:
                    spread()
            pe.wait_ge(s_res, 3 * KD - 4)
            with pe.Fori(0, 2) as j:
                for q in range(2):
                    b = (C_PW2 + q) % 2
                    pe.wait_ge(s_lo, j * 2 + (C_PW2 + q + 1))
                    for m in range(2):
                        pe.wait_ge(s_res, 3 * KD - 3 + 2 * q + m)
                        pe.wait_ge(s_yc, j * 4 + (2 * q + m + 1))
                        tile(bank[2 * q + m][:], b, slice(m * P, (m + 1) * P), KD,
                             lambda k: ln_hi[:, k, :], lambda k: ln_lo[:, k, :],
                             wait=(lambda k: pe.wait_ge(s_lnlo, k + 1)) if (q, m) == (0, 0) else None).then_inc((s_pacc, s_wused)[m], 1)
            for t in range(KD):
                residual_tile(C_OUT2, t, hi, lo,
                              lambda t: pe.wait_ge(*((s_yc, 4 + 4 + t + 1) if t < 4 else (s_res, 3 * KD + t - 3))),
                              lambda k: pe.wait_ge(s_yclo, k + 1))
            column_sums()
            spread()
            pe.wait_ge(s_res, 4 * KD)
            for s in range(2 * TT):
                half, t = divmod(s, TT)
                if t == 0:
                    pe.wait_ge(s_xf, (half + 1) * KD // 2)
                if s >= 4:
                    pe.wait_ge(s_on, s - 3)
                for q in range(4):
                    k = 4 * half + q
                    mm = pe.transpose(bank[s % 4][:, q * P:(q + 1) * P], xT[:, k, t * P:(t + 1) * P], ident[:])
                mm.then_inc(s_ot, 1)

        @block.scalar
        def _(act):
            def hi_part(n, b, half):
                act.wait_ge(s_stage[b], half * 16 + 16)
                if not isinstance(n, int) or n >= 2:
                    act.wait_ge(s_wused, n - 1)
                nc.scalar.activation(w_hi[b][:], w_stage[b][:], ACT.Copy).then_inc(s_hi, 1)

            act.wait_ge(s_c, 32)
            nc.scalar.activation(c_act[:], c_sb[:], ACT.Silu).then_inc(s_cact, 1)
            act.wait_ge(s_vt, 1)
            nc.scalar.activation(vcol[:, 0:208], bank[4][:, 0:208], ACT.Copy).then_inc(s_vcol, 1)
            nc.scalar.activation(vcol[:, 256:504], bank[4][:, 256:504], ACT.Copy).then_inc(s_vcol, 1)
            for k in range(KD):
                act.wait_ge(s_xt, k + 1)
                nc.scalar.activation(xT[:, k, :], bank[k % 4][:], ACT.Copy).then_inc(s_xTr, 1)

            norms = [0]

            def squares(ready, src=None, gains=None, between=None):
                norms[0] += 1
                j = norms[0]
                nc.scalar.activation(nothing[:, 4:5], eps[:, 0:1], ACT.Sqrt)
                for k in range(KD):
                    ready(k)
                    if k >= 3:
                        act.wait_ge(s_sqused, (KD - 1) * (j - 1) + k - 2)
                    nc.scalar.activation((tmp[k % 2] if k else rstd)[:], (src or xT)[:, k, :], ACT.Square).then_inc(s_sq, 1)
                    if gains:
                        if k >= 2:
                            act.wait_ge(s_gsqused, k - 1)
                        nc.scalar.activation(tmp[3 if k else 2][:], xT[:, k, :], ACT.Square, scale=col(gains, k)).then_inc(s_gsq, 1)
                if between:
                    between()
                act.wait_ge(s_col, j)
                nc.scalar.activation(cols[:, 0, :], bank[4][:, 0:TT], ACT.Sqrt, bias=eps[:, 0:1], scale=1.0 / D).then_inc(s_sd, 1)
                if gains:
                    act.wait_ge(s_mq, 1)
                    nc.scalar.activation(cols[:, 4, :], cols[:, 3, :], ACT.Sqrt, bias=eps[:, 0:1], scale=1.0 / D).then_inc(s_sd, 1)

            splits = [0]

            def act_hi_parts(shift):
                j = splits[0]
                splits[0] += 1
                for k in range(KD):
                    act.wait_ge(s_u, KD * j + k + 1)
                    nc.scalar.activation(act_hi[:, k, :], tmp[k % 2][:], ACT.Identity, bias=modc(shift + k)).then_inc(s_ahi, 1)

            act.wait_ge(s_set, 2)
            squares(lambda k: act.wait_ge(s_xTr, k + 1), between=lambda: hi_part(0, 0, 0))
            hi_part(1, 1, 0)
            act.wait_ge(s_mod, 2)
            act_hi_parts(SH1)

            tiles = [0]

            firsts = [0]

            def arrived(n, last):
                if last:
                    act.wait_ge(s_wused, n + 1)
                else:
                    firsts[0] += 1
                    act.wait_ge(s_acc, firsts[0])

            def take(n, last, dst, src, scale=1.0):
                t = tiles[0]
                arrived(n, last)
                i = nc.scalar.activation(dst, src(bank[t % 4]), ACT.Copy, scale=scale)
                tiles[0] += 1
                return i

            whole = lambda b: b[:]
            pairs = list(enumerate(PAIRS))

            def relus():
                for _ in range(PAIRS_PER_TILE):
                    if not pairs:
                        return
                    s, (i, h) = pairs.pop(0)
                    n = P * (i + 1)
                    act.wait_ge(s_lg, s + 1)
                    if s >= 2:
                        act.wait_ge(s_score, s - 1)
                    nc.scalar.activation(relu[s % 2][:, 0:n], bank[4 + s % 2][:, 0:n], ACT.Relu).then_inc(s_relu, 1)

            for n in range(N_IN):
                if n == 0:
                    take(n, False, qiT[:, 1, :], whole).then_inc(s_free, 1)
                    take(n, True, qiT[:, 2, :], whole).then_inc(s_free, 1)
                elif n == 1:
                    take(n, False, qiT[:, 0, :], whole).then_inc(s_free, 1)
                    take(n, True, ckvT[:], whole).then_inc(s_free, 1)
                elif n == 2:
                    take(n, False, qiT[:, 3, :], whole).then_inc(s_free, 1)
                    t = tiles[0]
                    arrived(n, True)
                    nc.scalar.activation(kiT[0:HD, :], bank[t % 4][0:HD, :], ACT.Copy)
                    nc.scalar.activation(kiT[HD:P, :], bank[t % 4][0:HD, :], ACT.Copy).then_inc(s_free, 1)
                    nc.scalar.activation(wiT[HD:HD + 8, :], bank[t % 4][HD:HD + 8, :], ACT.Copy, scale=IDX_SCALE).then_inc(s_free, 1)
                    tiles[0] += 1
                elif n >= 9:
                    if n == 9:
                        act.wait_ge(s_adaacc, ADA_ORD[ADA_ATT - 1] + 1)
                    for tp in range(2):
                        vs = slice((n - 9) * NCOL, (n - 8) * NCOL)
                        take(n, tp == 1, va[:, 2 * tp:2 * tp + 2, vs], lambda b: b[:].rearrange("p (t c) -> p t c", t=2)).then_inc(s_free, 1)
                else:
                    if n == 7:
                        act.wait_ge(s_adaacc, ADA_ORD[ADA_ATT - 1] + 1)
                    for m in range(2):
                        if n <= 4:
                            take(n, m == 1, qbT[:, 2 * (n - 3) + m, :], whole).then_inc(s_free, 1)
                        elif n <= 6:
                            take(n, m == 1, qaT[:, 2 * (n - 5) + m, :], whole, QSCALE).then_inc(s_free, 1)
                        else:
                            take(n, m == 1, kaT[:, 2 * (n - 7) + m, :], whole).then_inc(s_free, 1)
                        if m == 1:
                            hi_part(n + 2, n % 2, (n + 2) // 2)
                        if (n, m) == (3, 0):
                            act.wait_ge(s_wiT, 1)
                            nc.scalar.activation(wi_sb[:].rearrange("p t h -> p (t h)"), bank[5][:, 0:TT * 8], ACT.Copy).then_inc(s_wi, 1)
                        relus()
                if not 3 <= n < 9:
                    hi_part(n + 2, n % 2, (n + 2) // 2)
                if n == 2:
                    act.wait_ge(s_ckvt, 1)
                    nc.scalar.activation(ckv[:].rearrange("p t r -> p (t r)"), bank[6][:], ACT.Copy).then_inc(s_ckvn, 1)
                if n == 4:
                    act.wait_ge(s_ckv, TT)
                    nc.scalar.activation(ckv_ss[:, 1, :], ckv_ss[:, 0, :], ACT.Sqrt, bias=eps[:, 0:1], scale=1.0 / P).then_inc(s_ckvsd, 1)
                if n == 6:
                    act.wait_ge(s_ckvt, 2)
                    nc.scalar.activation(ckvT[:], bank[6][:], ACT.Copy).then_inc(s_ckvT, 1)
            assert tiles[0] == N_IN_TILES

            O_BANK, T_BANK = (7, 1), (6, 0)
            n_items = len(ITEMS)

            def exponentials(s):
                n = P * (ITEMS[s][2] + 1)
                act.wait_ge(s_min, s + 1)
                if s >= 4:
                    act.wait_ge(s_t, s - 3)
                nc.scalar.activation(probs[s % 4][:, 0:n], tmp[s % 2][:, 0:n], ACT.Exp, bias=negmax[:, s:s + 1],
                                     scale=-1.0, accum_out=expsum[:, s:s + 1]).then_inc(s_exp, 1)

            def turned(s):
                i = ITEMS[s][2]
                n = P * (i + 1)
                act.wait_ge(s_t, s + 1)
                if s >= 3:
                    act.wait_ge(s_pv, s - 2)
                nc.scalar.activation(probsT[s % 3][:, 0:i + 1, :].rearrange("p k q -> p (k q)"),
                                     bank[T_BANK[s % 2]][:, 0:n], ACT.Copy).then_inc(s_pt, 1)

            for s in range(n_items + 10):
                if s < n_items:
                    if s + 2 < n_items and ITEMS[s + 2][0] == "B" and ITEMS[s + 2][2] == 0:
                        h = ITEMS[s + 2][1]
                        act.wait_ge(s_ql, h + 1)
                        if h >= 2:
                            act.wait_ge(s_s, TT * (NH + h - 1))
                        nc.scalar.activation(qlatT[h % 2][:], bank[2][:], ACT.Copy, scale=QSCALE).then_inc(s_qlT, 1)
                    exponentials(s)
                if 3 <= s < n_items + 3:
                    turned(s - 3)
                if 6 <= s < n_items + 6 and ITEMS[s - 6][2] == TT - 1:
                    kind, h, i = ITEMS[s - 6]
                    act.wait_ge(s_pv, s - 5)
                    if kind == "A":
                        half = slice(HD * (h % 2), HD * (h % 2) + HD)
                        nc.scalar.activation(act_hi[half, h // 2, :], bank[O_BANK[h % 2]][half, :], ACT.Copy).then_inc(s_mhi, 1)
                    else:
                        if h >= 2:
                            act.wait_ge(s_uv, h - 1)
                        nc.scalar.activation(olat[h % 2][:], bank[O_BANK[h % 2]][:], ACT.Copy).then_inc(s_oh, 1)
                if s >= 9 and s - 9 < n_items and ITEMS[s - 9][0] == "B" and ITEMS[s - 9][2] == TT - 1:
                    h = ITEMS[s - 9][1]
                    half = slice(HD * (h % 2), HD * (h % 2) + HD)
                    act.wait_ge(s_uv, h + 1)
                    nc.scalar.activation(act_hi[half, 4 + h // 2, :], bank[3][half, :], ACT.Copy).then_inc(s_mhi, 1)

            def after(n):
                if n + 2 < C_END:
                    hi_part(n + 2, n % 2, (n + 2) // 2)

            def out_tile(k):
                if k % 2:
                    after(C_OUT + k // 2)
                act.wait_ge(s_res, k + 1)

            squares(out_tile)
            act.wait_ge(s_mod, 4)
            act_hi_parts(SH2)
            act.wait_ge(s_alo, 2 * KD)
            nc.scalar.activation(nothing[:, 4:5], eps[:, 0:1], ACT.Silu).then_inc(s_silu, 2)
            with act.Fori(0, KF // 2) as j:
                for q in range(2):
                    for m in range(2):
                        if q == 0:
                            act.wait_ge((s_guacc, s_wused)[m], j * 2 + (1, C_GU + 1)[m])
                            act.wait_ge(s_up, j * 2 + (1 + m))
                            nc.scalar.activation(tmp[m][:], bank[m][:], ACT.Silu).then_inc(s_silu, 1)
                    hi_part(j * 2 + (C_GU + q + 2), (C_GU + q) % 2, j + (C_GU + q + 2) // 2)
            lam = vcol[:, VROW["lam_2"]:VROW["lam_2"] + KD]
            nc.scalar.activation(lam_t[:, 0, :], lam, ACT.Abs).then_inc(s_lama, 1)
            act.wait_ge(s_lama, 1)
            nc.scalar.activation(lam_t[:, 1, :], lam_t[:, 0, :], ACT.Exp, scale=-1.0).then_inc(s_lama, 1)
            act.wait_ge(s_lama, 2)
            act.wait_ge(s_lam, 2)
            nc.scalar.activation(lam_t[:, 3, :], lam_t[:, 2, :], ACT.Ln).then_inc(s_lama, 1)
            def down_tile(k):
                for g in ((2,) if k % 2 else (0, 1)):
                    after(C_DOWN + 3 * (k // 2) + g)
                act.wait_ge(s_res, KD + k + 1)

            squares(down_tile, gains="g_final")
            act.wait_ge(s_mod, 8)
            act_hi_parts(SH3)
            nc.scalar.activation(nothing[:, 4:5], eps[:, 0:1], ACT.Sigmoid).then_inc(s_sig, 2)
            act.wait_ge(s_alo, 3 * KD)
            with act.Fori(0, KD // 2) as j:
                for q in range(2):
                    if q == 0:
                        for m in range(2):
                            act.wait_ge((s_i2acc, s_wused)[m], j * 2 + (1, C_IN2 + 1)[m])
                            act.wait_ge(s_v, j * 2 + (1 + m))
                            nc.scalar.activation(tmp[m][:], bank[m][:], ACT.Sigmoid).then_inc(s_sig, 1)
                    hi_part(j * 2 + (C_IN2 + q + 2), (C_IN2 + q) % 2, j + (C_IN2 + q + 2) // 2)

            def lru_gates(p):
                for k in (2 * p, 2 * p + 1):
                    m = k % 2
                    act.wait_ge(s_gmm, 2 * k + 1)
                    if p:
                        act.wait_ge(s_scan, k - 1)
                    nc.scalar.activation(decay[m][:], bank[4 + 2 * m][:], ACT.Sigmoid, bias=col("br_2", k)).then_inc(s_r, 1)
                    act.wait_ge(s_gmm, 2 * k + 2)
                    nc.scalar.activation(tmp[2 + m][:], bank[5 + 2 * m][:], ACT.Sigmoid, bias=col("bi_2", k)).then_inc(s_i, 1)
                for k in (2 * p, 2 * p + 1):
                    act.wait_ge(s_r, k + 1)
                    nc.scalar.activation(l_pad[:, k, 0:T], decay[k % 2][:], ACT.Tanh, scale=lam_t[:, 5, k:k + 1]).then_inc(s_th, 1)
                for k in (2 * p, 2 * p + 1):
                    act.wait_ge(s_th, k + 1)
                    nc.scalar.activation(decay[k % 2][:], decay[k % 2][:], ACT.Exp, scale=lam_t[:, 4, k:k + 1]).then_inc(s_a, 1)
                for k in (2 * p, 2 * p + 1):
                    act.wait_ge(s_a, k + 1)
                    if p:
                        act.wait_ge(s_llo, k - 1)
                    nc.scalar.activation(hidden[k % 2][:], decay[k % 2][:], ACT.Square).then_inc(s_aa, 1)

            def lru_mult(p):
                for k in (2 * p, 2 * p + 1):
                    act.wait_ge(s_m, k + 1)
                    nc.scalar.activation(l_pad[:, k, 0:T], l_pad[:, k, 0:T], ACT.Sqrt).then_inc(s_mt, 1)

            def lru_high(p):
                for k in (2 * p, 2 * p + 1):
                    act.wait_ge(s_y, k + 1)
                    nc.scalar.activation(lru_hi[:, k, :], hidden[k % 2][:], ACT.Copy).then_inc(s_lhi, 1)

            act.wait_ge(s_lam, LAM_STEPS)
            for slot in range(KD, C_LRU - C_IN2):
                n = C_IN2 + slot
                dst, func, lead = ((l_pad, ACT.Copy, PADL), (lgate, ACT.Silu, 0), (cgate, ACT.Silu, 0))[(slot - KD) // 4]
                for m in range(2):
                    act.wait_ge(*((s_wused, n + 1) if m else (s_i2acc, slot + 1)))
                    nc.scalar.activation(dst[:, (2 * (slot - KD) + m) % KD, lead:lead + T],
                                         bank[(2 * (slot - KD) + m) % 4][:], func).then_inc(s_gate, 1)
                hi_part(n + 2, n % 2, (n + 2) // 2)
                p, odd = divmod(slot - LRU_SLOT, 2)
                if 1 <= p <= KD // 2 and not odd:
                    lru_high(p - 1)
                if 0 <= p < KD // 2:
                    (lru_gates, lru_mult)[odd](p)

            chunk = [C_LRU]

            def next_chunk():
                n = chunk[0]
                chunk[0] += 1
                hi_part(n + 2, n % 2, (n + 2) // 2)

            for _ in range((MEAN_AFTER + 1) // 2):
                next_chunk()
            act.wait_ge(s_mean, 1)
            nc.scalar.activation(tmp[2][:], bank[5][:], ACT.Copy, scale=1.0 / D).then_inc(s_mu, 1)
            act.wait_ge(s_gx, KD)
            act.wait_ge(s_llo, KD)

            def chunks_to_var():
                while chunk[0] < C_LRU + (VAR_AFTER + 1) // 2:
                    next_chunk()

            squares(lambda k: act.wait_ge(s_cen, k + 1), conv, between=chunks_to_var)
            for k in range(KD):
                if k in LN_CHUNKS:
                    next_chunk()
                act.wait_ge(s_lnu, k + 1)
                if k >= 2:
                    act.wait_ge(s_lnlo, k - 1)
                nc.scalar.activation(tmp[2 + k % 2][:], tmp[k % 2][:], ACT.Silu, bias=col("cln_b_2", k)).then_inc(s_lns, 1)
            while chunk[0] < C_OUT2:
                next_chunk()

            def last_tile(k):
                if k % 2:
                    after(C_OUT2 + k // 2)
                act.wait_ge(s_res, 3 * KD + k + 1)

            squares(last_tile)
            for s in range(2 * TT):
                half, t = divmod(s, TT)
                act.wait_ge(s_ot, s + 1)
                nc.scalar.activation(o_nat[:, t, half * 512:(half + 1) * 512], bank[s % 4][:], ACT.Copy).then_inc(s_on, 1)

        @block.vector
        def _(dve):
            V = nc.vector
            dve.memset(eps[:], EPS).then_inc(s_set, 1)
            dve.memset(ones[:], 1.0).then_inc(s_set, 1)
            dve.wait_ge(s_set, 2)
            steps = [0]

            def ada_step(c, t):
                o = ADA_ORD[c]
                acc = ada_acc[ADA_ACC[o]]
                if t == KD:
                    dve.wait_ge(s_adastep, steps[0])
                    V.tensor_tensor(acc[:, 0, :], acc[:, 0, :], acc[:, 1, :], ALU.add).then_inc(s_adaacc, 1)
                    return
                if t == 0:
                    ada_wait(dve, c)
                    last = [q for q in range(o) if ADA_ACC[q] == ADA_ACC[o]]
                    if last:
                        dve.wait_ge(s_adamm, last[-1] + 1)
                src, w = ada_stage[c][:, t, :], c_act[:, 0 if c < ADA1 else 1, t:t + 1]
                dst = acc[:, t % 2, :]
                if t < 2:
                    i = V.tensor_scalar(dst, src, w, None, ALU.mult)
                else:
                    dve.wait_ge(s_adastep, steps[0] - 1)
                    i = V.scalar_tensor_tensor(dst, src, w, dst, ALU.mult, ALU.add)
                i.then_inc(s_adastep, 1)
                steps[0] += 1

            def ada(c):
                for t in range(KD + 1):
                    ada_step(c, t)

            dve.wait_ge(s_cact, 1)
            norms = [0]

            def add_squares(k, gained=False):
                j = norms[0] + 1
                if k == 0:
                    return
                dve.wait_ge(s_sq, KD * (j - 1) + k + 1)
                if k >= 2:
                    dve.wait_ge(s_sqused, (KD - 1) * (j - 1) + k - 1)
                V.tensor_tensor(rstd[:], rstd[:], tmp[k % 2][:], ALU.add).then_inc(s_sqused, 1)
                if gained:
                    dve.wait_ge(s_gsq, k + 1)
                    if k >= 2:
                        dve.wait_ge(s_gsqused, k - 1)
                    V.tensor_tensor(tmp[2][:], tmp[2][:], tmp[3][:], ALU.add).then_inc(s_gsqused, 1)

            sds, links = [0], [0]

            def link(i):
                links[0] += 1
                i.then_inc(s_colstep, 1)
                dve.wait_ge(s_colstep, links[0])

            def diagonal(dst, c, ready):
                for t in range(TT):
                    V.tensor_scalar(dst[:, t * P:(t + 1) * P], ident[:], cols[:, c, t:t + 1], None, ALU.mult).then_inc(ready, 1)

            def rstd_columns():
                norms[0] += 1
                sds[0] += 1
                dve.wait_ge(s_sd, sds[0])
                link(V.reciprocal(cols[:, 1, :], cols[:, 0, :]))
                diagonal(rstd, 1, s_diag)

            def rstd_columns_2():
                norms[0] += 1
                dve.wait_ge(s_sd, sds[0] + 1)
                link(V.reciprocal(cols[:, 1, :], cols[:, 0, :]))
                link(V.tensor_tensor(cols[:, 2, :], cols[:, 1, :], cols[:, 1, :], ALU.mult))
                V.tensor_tensor(cols[:, 3, :], cols[:, 2, :], bank[4][:, TT:2 * TT], ALU.mult).then_inc(s_mq, 1)
                diagonal(tmp[2], 1, s_diag1)
                sds[0] += 2
                dve.wait_ge(s_sd, sds[0])
                link(V.reciprocal(cols[:, 5, :], cols[:, 4, :]))
                link(V.tensor_tensor(cols[:, 6, :], cols[:, 5, :], cols[:, 1, :], ALU.mult))
                diagonal(rstd, 6, s_diag)

            splits = [0]

            def normed(slot, shift, rstd):
                j = splits[0]
                splits[0] += 1
                for k in range(KD + 1):
                    if k < KD:
                        if k >= 2:
                            dve.wait_ge(s_alo, KD * j + k - 1)
                        V.scalar_tensor_tensor(tmp[k % 2][:], xT[:, k, :], scale1[:, slot, k:k + 1], rstd[:],
                                               ALU.mult, ALU.mult).then_inc(s_u, 1)
                    if k >= 1:
                        dve.wait_ge(s_ahi, KD * j + k)
                        V.scalar_tensor_tensor(act_lo[:, k - 1, :], tmp[(k - 1) % 2][:], modc(shift + k - 1),
                                               act_hi[:, k - 1, :].bitcast(F32), ALU.add, ALU.subtract).then_inc(s_alo, 1)

            ada(1)
            ada(3)
            for k in range(KD):
                add_squares(k)
            ada(5)
            ada(7)
            rstd_columns()
            dve.wait_ge(s_vcol, 2)
            dve.wait_ge(s_adadir, len(ADA_PE))
            dve.wait_ge(s_adamm, ADA_FIRST - len(ADA_PE))
            nm = [0]

            def fold(gain, sc, slot):
                nm[0] += 1
                V.scalar_tensor_tensor(scale1[:, slot, :], mod[:, sc:sc + KD], 1.0,
                                       vcol[:, VROW[gain]:VROW[gain] + KD], ALU.add, ALU.mult).then_inc(s_mod, 1)

            V.tensor_tensor(mod[:, 0:16], bank[7][:, 0:16], vcol[:, 0:16], ALU.add).then_inc(s_mod, 1)
            dve.wait_ge(s_mod, 1)
            fold("g_attn", SC1, 0)
            dve.wait_ge(s_mod, 2)

            dve.wait_ge(s_spread, 1)
            normed(0, SH1, bank[4])

            pairs = list(enumerate(PAIRS))

            def scores_sum(count):
                for _ in range(count):
                    if not pairs:
                        return
                    s, (i, h) = pairs.pop(0)
                    n = P * (i + 1)
                    dve.wait_ge(s_relu, s + 1)
                    w = wi_sb[:, i, h:h + 1]
                    if h == 0:
                        V.tensor_scalar(score[i][:], relu[s % 2][:, 0:n], w, None, ALU.mult).then_inc(s_score, 1)
                    else:
                        dve.wait_ge(s_score, s)
                        V.scalar_tensor_tensor(score[i][:], relu[s % 2][:, 0:n], w, score[i][:], ALU.mult, ALU.add).then_inc(s_score, 1)

            c = ADA_FIRST
            for n in range(6):
                for _ in range(ADA_WINDOW.get(n, 0)):
                    ada(c)
                    c += 1
                if n == 3:
                    dve.wait_ge(s_ckvn, 1)
                    for t in range(TT):
                        V.tensor_tensor_reduce(tmp[2][:, t * P:(t + 1) * P], ckv[:, t, :], ckv[:, t, :], 1.0, 0.0,
                                               ALU.mult, ALU.add, ckv_ss[:, 0, t:t + 1]).then_inc(s_ckv, 1)
                if n == 5:
                    dve.wait_ge(s_ckvsd, 1)
                    V.reciprocal(ckv_ss[:, 2, :], ckv_ss[:, 1, :]).then_inc(s_ckv, 1)
                    dve.wait_ge(s_ckv, TT + 1)
                    dve.wait_ge(s_const, 16 * NCONST)
                    for t in range(TT):
                        V.scalar_tensor_tensor(ckv[:, t, :], ckv[:, t, :], ckv_ss[:, 2, t:t + 1], kvg[:],
                                               ALU.mult, ALU.mult).then_inc(s_ckv, 1)
                if n >= 3:
                    scores_sum(2 * PAIRS_PER_TILE)
            assert not pairs
            dve.wait_ge(s_score, len(PAIRS))
            top = 0
            for i in range(1, TT):
                d = score[i][:, i * P:(i + 1) * P]
                V.tensor_tensor(d, d, causal[:, 1, :], ALU.min).then_inc(s_top, 1)
                top += 1
            for r in range(TOPK // 8):
                for i in range(1, TT):
                    dve.wait_ge(s_top, top - 2)
                    V.max(top8[i][:], (score if r == 0 else work)[i][:]).then_inc(s_top, 1)
                    top += 1
                for i in range(1, TT):
                    dve.wait_ge(s_top, top - 2)
                    V.match_replace(work[i][:], top8[i][:], (score if r == 0 else work)[i][:], -3.0e38).then_inc(s_top, 1)
                    top += 1
            for i in range(1, TT):
                dve.wait_ge(s_top, top - 2)
                V.tensor_tensor(work[i][:], work[i][:], score[i][:], ALU.is_equal).then_inc(s_top, 1)
                top += 1
            for i in range(1, TT):
                dve.wait_ge(s_top, top - 2)
                V.tensor_scalar(work[i][:], work[i][:], BIG, None, ALU.mult).then_inc(s_top, 1)
                top += 1
            assert top == TOP_STEPS
            dve.wait_ge(s_adamm, ADA_ORD[ADA_ATT])
            V.tensor_tensor(mod[:, 16:2 * ADA_ATT], bank[7][:, 16:2 * ADA_ATT], vcol[:, 16:2 * ADA_ATT], ALU.add).then_inc(s_mod, 1)
            dve.wait_ge(s_mod, 3)
            fold("g_ffn", SC2, 1)

            O_BANK, T_BANK = (7, 1), (6, 0)
            n_items = len(ITEMS)

            def least(s):
                kind, h, i = ITEMS[s]
                n = P * (i + 1)
                dve.wait_ge(s_s, s + 1)
                if kind == "A":
                    dve.wait_ge(s_tab, h + 1)
                    t = table[h % 2][:, T - n:T]
                else:
                    u = s - NH * TT
                    dve.wait_ge(s_comb, u + 1)
                    t = comb[u % 2][:, 0:n]
                if s >= 2:
                    dve.wait_ge(s_exp, s - 1)
                V.tensor_tensor_reduce(tmp[s % 2][:, 0:n], bank[4 + s % 2][:, 0:n], t, 1.0, 3.0e38,
                                       ALU.add, ALU.min, negmax[:, s:s + 1]).then_inc(s_min, 1)

            def normalise(s):
                n = P * (ITEMS[s][2] + 1)
                dve.wait_ge(s_exp, s + 1)
                V.reciprocal(expinv[:, s:s + 1], expsum[:, s:s + 1]).then_inc(s_inv, 1)
                dve.wait_ge(s_inv, s + 1)
                V.tensor_scalar(probs[s % 4][:, 0:n], probs[s % 4][:, 0:n], expinv[:, s:s + 1], None,
                                ALU.mult).then_inc(s_norm, 1)

            def low(g, src, k):
                half = slice(HD * (g % 2), HD * (g % 2) + HD)
                dve.wait_ge(s_mhi, g + 1)
                V.tensor_tensor(act_lo[half, k, :], src[half, :], act_hi[half, k, :].bitcast(F32), ALU.subtract).then_inc(s_mlo, 1)

            for s in range(n_items + 10):
                if s < n_items:
                    least(s)
                if 1 <= s < n_items + 1:
                    normalise(s - 1)
                c, t = divmod(s, ADA_ITEMS)
                if ADA_ATT + c < ADA_LOOP:
                    ada_step(ADA_ATT + c, t)
                if s == ADA_ITEMS * (ADA_LOOP - ADA_ATT) + 4:
                    dve.wait_ge(s_adamm, ADA_DVE)
                    ms = slice(2 * ADA_ATT, 2 * ADA_LOOP)
                    V.tensor_tensor(mod[:, ms], bank[3][:, ms], vcol[:, ms], ALU.add).then_inc(s_mod, 1)
                if 7 <= s < n_items + 7 and ITEMS[s - 7][2] == TT - 1 and ITEMS[s - 7][0] == "A":
                    h = ITEMS[s - 7][1]
                    low(h, bank[O_BANK[h % 2]], h // 2)
                if s >= 9 and s - 9 < n_items and ITEMS[s - 9][0] == "B" and ITEMS[s - 9][2] == TT - 1:
                    h = ITEMS[s - 9][1]
                    low(NH + h, bank[3], 4 + h // 2)
            dve.wait_ge(s_mod, 4)
            added = [0]

            def residual(n0, gain, groups=1, gained=False, turn=0):
                r0 = added[0]
                added[0] += KD
                for k in range(KD + 1):
                    if k < KD:
                        dve.wait_ge(*((s_wused, n0 + groups * (k // 2 + 1)) if k % 2 else (s_racc, (r0 + k) // 2 + 1)))
                        V.scalar_tensor_tensor(xT[:, k, :], bank[(k + turn) % 4][:], gain(k), xT[:, k, :], ALU.mult, ALU.add).then_inc(s_res, 1)
                    if k >= 1:
                        add_squares(k - 1, gained)

            def residual_2(n0, r0, t):
                dve.wait_ge(*((s_wused, n0 + t // 2 + 1) if t % 2 else (s_racc, (r0 + t) // 2 + 1)))
                V.scalar_tensor_tensor(xT[:, t, :], bank[t % 4][:], scale1[:, 3, t:t + 1], xT[:, t, :],
                                       ALU.mult, ALU.add).then_inc(s_res, 1)

            residual(C_OUT, lambda k: modc(GA1 + k), turn=2)
            rstd_columns()
            dve.wait_ge(s_res, KD)
            dve.wait_ge(s_spread, 2)
            normed(1, SH2, bank[4])
            ada_steps = steps[0]
            dve.memset(nothing[:, 1:2], 0.0).then_inc(s_up, 2)
            dve.memset(nothing[:, 3:4], 0.0).then_inc(s_fflo, 2)
            with dve.Fori(0, KF // 2) as j:
                dve.wait_ge(s_adaloop, j * 16 + 16)
                dve.wait_ge(s_adamm, j + ADA_DVE)
                for t in range(KD):
                    src, w = ada2_stage[:, t, :], c_act[:, 1, t:t + 1]
                    if t == 0:
                        V.tensor_scalar(ada2_acc[:], src, w, None, ALU.mult).then_inc(s_adastep, 1)
                    else:
                        dve.wait_ge(s_adastep, j * (KD - 1) + (ada_steps + t))
                        V.scalar_tensor_tensor(ada2_acc[:], src, w, ada2_acc[:], ALU.mult, ALU.add).then_inc(
                            s_adaacc if t == KD - 1 else s_adastep, 1)
                for m in range(2):
                    dve.wait_ge(s_silu, j * 2 + (3 + m))
                    dve.wait_ge((s_guacc, s_wused)[m], j * 2 + (2, C_GU + 2)[m])
                    dve.wait_ge(s_fflo, j * 2 + (1 + m))
                    V.tensor_tensor(tmp[2 + m][:], bank[2 + m][:], tmp[m][:], ALU.mult).then_inc(s_up, 1)
                for m in range(2):
                    dve.wait_ge(s_up, j * 2 + (3 + m))
                    V.tensor_copy(ff_hi[:, bass.ds(j * 2 + m, 1), :], tmp[2 + m][:].rearrange("p (o t) -> p o t", o=1)).then_inc(s_ffhi, 1)
                for m in range(2):
                    dve.wait_ge(s_ffhi, j * 2 + (1 + m))
                    V.tensor_tensor(ff_lo[:, bass.ds(j * 2 + m, 1), :], tmp[2 + m][:].rearrange("p (o t) -> p o t", o=1),
                                    ff_hi[:, bass.ds(j * 2 + m, 1), :].bitcast(F32), ALU.subtract).then_inc(s_fflo, 1)
            dve.wait_ge(s_adamm, ADA_DVE + KF // 2)
            V.tensor_tensor(mod[:, 2 * ADA_LOOP:72], bank[5][:, 0:72 - 2 * ADA_LOOP], vcol[:, 2 * ADA_LOOP:72], ALU.add).then_inc(s_mod, 1)
            dve.wait_ge(s_mod, 6)
            fold("norm_g_2", SC3, 2)
            V.tensor_scalar(scale1[:, 3, :], mod[:, GA3:GA3 + KD], 1.0, None, ALU.add).then_inc(s_mod, 1)
            lam = vcol[:, VROW["lam_2"]:VROW["lam_2"] + KD]
            L = lambda r: lam_t[:, r, :]
            ls = [0]

            def lam_link(i):
                ls[0] += 1
                i.then_inc(s_lam, 1)
                dve.wait_ge(s_lam, ls[0])

            dve.wait_ge(s_lama, 2)
            lam_link(V.tensor_scalar(L(2), L(1), 1.0, None, ALU.add))
            lam_link(V.tensor_scalar(L(0), L(2), -1.0, 1e-37, ALU.add, ALU.max))
            dve.wait_ge(s_lama, 3)
            lam_link(V.reciprocal(L(6), L(0)))
            lam_link(V.tensor_tensor(L(6), L(6), L(1), ALU.mult))
            lam_link(V.tensor_tensor(L(6), L(6), L(3), ALU.mult))
            lam_link(V.tensor_scalar(L(5), L(0), 1e-30, None, ALU.is_lt))
            lam_link(V.tensor_tensor(L(5), L(5), L(1), ALU.mult))
            lam_link(V.tensor_tensor(L(6), L(6), L(5), ALU.add))
            lam_link(V.tensor_scalar(L(7), lam, -1.0, 0.0, ALU.mult, ALU.max))
            lam_link(V.tensor_tensor(L(6), L(6), L(7), ALU.add))
            lam_link(V.tensor_scalar(L(5), L(6), 8.0, None, ALU.mult))
            lam_link(V.tensor_scalar(L(4), L(6), -8.0, None, ALU.mult))
            assert ls[0] == LAM_STEPS

            dve.wait_ge(s_mod, 8)
            V.tensor_tensor(scale1[:, 0, :], scale1[:, 2, :], vcol[:, VROW["g_final"]:VROW["g_final"] + KD], ALU.mult).then_inc(s_mod, 1)
            residual(C_DOWN, lambda k: modc(GA2 + k), 3, gained=True)
            rstd_columns_2()
            dve.wait_ge(s_res, 2 * KD)
            dve.wait_ge(s_mod, 9)
            dve.wait_ge(s_spread, 3)
            normed(0, SH3, bank[4])
            dve.wait_ge(s_spread1, 1)
            dve.wait_ge(s_u, 3 * KD)
            for k in range(KD):
                V.scalar_tensor_tensor(xT[:, k, :], xT[:, k, :], col("g_final", k), bank[5][:], ALU.mult, ALU.mult).then_inc(s_x1, 1)
            V.memset(v_pad[:, :, 0:PADV], 0.0).then_inc(s_v, 1)
            V.memset(l_pad[:, :, 0:PADL], 0.0).then_inc(s_v, 1)
            taps = [(k, tap) for p in range(KD // 2) for tap in range(CONV) for k in (2 * p, 2 * p + 1)]
            taps_done = [0]

            def convolve(count):
                for _ in range(min(count, len(taps) - taps_done[0])):
                    k, tap = taps[taps_done[0]]
                    src, w = v_pad[:, k, tap:tap + T], col("dw_w_2", 8 * tap + k)
                    if tap == 0:
                        dve.wait_ge(s_v, 2 + k + 1)
                        V.tensor_scalar(conv[:, k, :], src, w, col("dw_b_2", k), ALU.mult, ALU.add).then_inc(s_conv, 1)
                    else:
                        dve.wait_ge(s_conv, taps_done[0] - 1)
                        V.scalar_tensor_tensor(conv[:, k, :], src, w, conv[:, k, :], ALU.mult, ALU.add).then_inc(s_conv, 1)
                    taps_done[0] += 1

            for k in range(KD):
                dve.wait_ge(s_sig, 2 + k + 1)
                dve.wait_ge(*((s_wused, C_IN2 + k + 1) if k % 2 else (s_i2acc, k + 2)))
                V.tensor_tensor(v_pad[:, k, PADV:PADV + T], bank[2 + k % 2][:], tmp[k % 2][:], ALU.mult).then_inc(s_v, 1)
                if k % 2:
                    convolve(TAPS_V if k < KD - 1 else TAPS_LX)

            x_steps = [0]

            def short_conv(p):
                for tap in range(SHORT):
                    for k in (2 * p, 2 * p + 1):
                        src = l_pad[:, k, tap:tap + T]
                        if tap == 0:
                            dve.wait_ge(s_gate, k + 1)
                            if p:
                                dve.wait_ge(s_gmm, 2 * (k - 1))
                                dve.wait_ge(s_gx, k - 1)
                            i = V.tensor_scalar(tmp[k % 2][:], src, col("sc_w_2", k), col("sc_b_2", k), ALU.mult, ALU.add)
                        else:
                            dve.wait_ge(s_xs, x_steps[0] - 1)
                            i = V.scalar_tensor_tensor(tmp[k % 2][:], src, col("sc_w_2", 8 * tap + k), tmp[k % 2][:], ALU.mult, ALU.add)
                        i.then_inc(s_xs, 1)
                        x_steps[0] += 1

            dve.wait_ge(s_v, 2 + KD)
            short_conv(0)
            convolve(TAPS_BEFORE)
            for p in range(KD // 2):
                ks = (2 * p, 2 * p + 1)
                convolve(TAPS_A[p])
                for k in ks:
                    dve.wait_ge(s_i, k + 1)
                    dve.wait_ge(s_xs, 2 * SHORT * (p + 1))
                    V.tensor_tensor(tmp[2 + k % 2][:], tmp[2 + k % 2][:], tmp[k % 2][:], ALU.mult).then_inc(s_gx, 1)
                if p < KD // 2 - 1:
                    short_conv(p + 1)
                for k in ks:
                    dve.wait_ge(s_aa, k + 1)
                    V.scalar_tensor_tensor(l_pad[:, k, 0:T], hidden[k % 2][:], 1.0, l_pad[:, k, 0:T], ALU.add, ALU.mult).then_inc(s_m, 1)
                convolve(TAPS_B[p])
                for k in ks:
                    dve.wait_ge(s_mt, k + 1)
                    dve.wait_ge(s_gx, k + 1)
                    V.tensor_tensor(tmp[2 + k % 2][:], tmp[2 + k % 2][:], l_pad[:, k, 0:T], ALU.mult).then_inc(s_bx, 1)
                for k in ks:
                    dve.wait_ge(s_bx, k + 1)
                    V.tensor_tensor_scan(hidden[k % 2][:], decay[k % 2][:], tmp[2 + k % 2][:], 0.0, ALU.mult, ALU.add).then_inc(s_scan, 1)
            convolve(len(taps))
            dve.wait_ge(s_scan, KD)
            dve.wait_ge(s_conv, CONV * KD)
            for k in range(1, KD):
                if k >= 2:
                    dve.wait_ge(s_csum, k - 1)
                V.tensor_tensor(tmp[3][:], (conv[:, 0, :] if k == 1 else tmp[3][:]), conv[:, k, :], ALU.add).then_inc(s_csum, 1)
            dve.wait_ge(s_x1, KD)
            for t in range(MEAN_AFTER + 1):
                residual_2(C_LRU, 2 * KD, t)
            dve.wait_ge(s_mu, 1)
            for k in range(KD):
                V.tensor_tensor(conv[:, k, :], conv[:, k, :], tmp[2][:], ALU.subtract).then_inc(s_cen, 1)
                if k >= 1:
                    add_squares(k - 1)
            add_squares(KD - 1)
            for t in range(MEAN_AFTER + 1, VAR_AFTER + 1):
                residual_2(C_LRU, 2 * KD, t)
            dve.wait_ge(s_cen, KD)
            rstd_columns()
            dve.wait_ge(s_spread, 4)
            t = VAR_AFTER + 1
            for k in range(KD + 1):
                if k < KD:
                    if k >= 2:
                        dve.wait_ge(s_lns, k - 1)
                    V.scalar_tensor_tensor(tmp[k % 2][:], conv[:, k, :], col("cln_g_2", k), bank[4][:], ALU.mult, ALU.mult).then_inc(s_lnu, 1)
                if k >= 1:
                    dve.wait_ge(s_lns, k)
                    V.tensor_copy(ln_hi[:, k - 1, :], tmp[2 + (k - 1) % 2][:]).then_inc(s_lnhi, 1)
                    dve.wait_ge(s_lnhi, k)
                    V.tensor_tensor(ln_lo[:, k - 1, :], tmp[2 + (k - 1) % 2][:], ln_hi[:, k - 1, :].bitcast(F32), ALU.subtract).then_inc(s_lnlo, 1)
                if k in RES_AT:
                    residual_2(C_LRU, 2 * KD, t)
                    t += 1
            for t in range(t, KD):
                residual_2(C_LRU, 2 * KD, t)
            V.memset(nothing[:, 2:3], 0.0).then_inc(s_yc, 4)
            for k in range(KD):
                dve.wait_ge(*((s_wused, C_PW2 + k // 2 + 1) if k % 2 else (s_pacc, k // 2 + 1)))
                if k >= 2:
                    dve.wait_ge(s_yclo, k - 1)
                V.scalar_tensor_tensor(tmp[k % 2][:], bank[k % 4][:], col("pw2_b_2", k), cgate[:, k, :], ALU.add, ALU.mult).then_inc(s_yc, 1)
                dve.wait_ge(s_yc, 4 + k + 1)
                V.tensor_copy(act_hi[:, k, :], tmp[k % 2][:]).then_inc(s_ychi, 1)
                dve.wait_ge(s_ychi, k + 1)
                V.tensor_tensor(act_lo[:, k, :], tmp[k % 2][:], act_hi[:, k, :].bitcast(F32), ALU.subtract).then_inc(s_yclo, 1)
            for t in range(KD + 1):
                if t < KD:
                    residual_2(C_OUT2, 3 * KD, t)
                if t >= 1:
                    add_squares(t - 1)
            rstd_columns()
            dve.wait_ge(s_res, 4 * KD)
            dve.wait_ge(s_spread, 5)
            for k in range(KD):
                V.scalar_tensor_tensor(xT[:, k, :], xT[:, k, :], col("final_g_2", k), bank[4][:], ALU.mult, ALU.mult).then_inc(s_xf, 1)


VROWS = (128, 80, 128, 120)
NCONST = 4
CKV_STEPS = 2 * TT + 1
TOP_STEPS = 3 + (TOPK // 8) * 6 + 6
LAM_STEPS = 12
N_IN_TILES = 22


_INS = ["x", "c", "w_ada", "b_ada", "g_attn", "w_in", "kv_norm_g", "w_uk", "w_uv", "w_out", "g_ffn", "w_gu",
        "w_down", "g_final", "c_2", "norm_g_2", "mod_w_2", "mod_b_2", "w_in_2", "dw_w_2", "dw_b_2", "cln_g_2",
        "cln_b_2", "pw2_w_2", "pw2_b_2", "sc_w_2", "sc_b_2", "wr_2", "br_2", "wi_2", "bi_2", "lam_2", "w_out_2",
        "final_g_2"]
_OUT = (1, T, D)


def kernel(**inputs):
    import numpy as np
    import concourse.bacc as bacc
    from concourse.bass_utils import run_bass_kernel_spmd

    nc = bacc.Bacc("TRN2", target_bir_lowering=False, num_devices=1)
    p, x = np.arange(P)[:, None], np.arange(T)[None, :]
    d = p + (T - P) - x
    held = ((d >= 0) & (d <= 128)).astype(int) + ((d >= 0) & (d % 4 == 0)) + ((d >= 0) & (d % 16 == 0))
    key = np.arange(P)[None, :]
    tables = {
        "dist": d.astype(np.float32),
        "maskA": np.where(held > 0, -np.log(np.maximum(held, 1)), BIG).astype(np.float32),
        "causal": np.stack([np.where(key > p, BIG, 0.0), np.where(key > p, -3.0e38, 3.0e38)], 1).astype(np.float32),
        "ident": np.eye(P, dtype=np.float32),
    }
    arrays, aps = {}, {}
    for name in _INS:
        v = np.ascontiguousarray(inputs[name])
        if v.ndim >= 3:
            v = v.reshape(v.shape[1:])
        elif name not in ("c", "c_2", "kv_norm_g"):
            v = v.reshape(-1)
        if name == "dw_w_2" or name == "sc_w_2":
            v = v.reshape(-1)
        tables[name] = v
    for name, v in tables.items():
        arrays[f"in_{name}"] = v
        aps[name] = nc.dram_tensor(f"in_{name}", v.shape, F32, kind="ExternalInput").ap()
    out = nc.dram_tensor("out_0", (T, D), F32, kind="ExternalOutput").ap()
    build(nc, aps, out)
    r = run_bass_kernel_spmd(nc, [arrays], core_ids=[0])
    return r.results[0]["out_0"].reshape(_OUT)
```
